# Optimizing a Trainium2 kernel written in Bass

```python
import math
import jax, jax.numpy as jnp
from jax import lax
import numpy as np

D_MODEL = 1024
BATCH = 1
SEQ = 512
DEPTH = 1

CHUNK = 64
Q_BLOCK = 128
PLE_DIM = 256
D_FF = 4 * D_MODEL
EPS = 1e-6

GLA_HEADS = 4
GLA_DK = D_MODEL // 16
GLA_DV = D_MODEL // 8
GLA_GATE_RANK = 16
GLA_TAU = 16.0
GLA_WIDTH = GLA_HEADS * GLA_DV

MLA_HEADS = 8
MLA_NOPE = 64
MLA_ROPE = 32
MLA_V = 64
MLA_QK = MLA_NOPE + MLA_ROPE
MLA_Q_RANK = 256
MLA_KV_RANK = 128
MLA_WIDTH = MLA_HEADS * MLA_V
ROPE_THETA = 10000.0

D_MIX = GLA_WIDTH + MLA_WIDTH
IN_SPLITS = (GLA_HEADS * GLA_DK, GLA_HEADS * GLA_DK, GLA_WIDTH, GLA_GATE_RANK,
             GLA_WIDTH, MLA_Q_RANK, MLA_KV_RANK, MLA_ROPE)
D_IN = (GLA_HEADS * GLA_DK * 2 + GLA_WIDTH * 2 + GLA_GATE_RANK
        + MLA_Q_RANK + MLA_KV_RANK + MLA_ROPE)


def rms_norm(x, g):
    xf = x.astype(jnp.float32)
    y = xf * lax.rsqrt(jnp.mean(xf * xf, axis=-1, keepdims=True) + EPS)
    return (y * g.astype(jnp.float32)).astype(x.dtype)

def split_cols(t, sizes):
    out, start = [], 0
    for s in sizes:
        out.append(t[..., start:start + s])
        start += s
    return out

def rope_cos_sin(positions):
    inv_freq = ROPE_THETA ** (-jnp.arange(0, MLA_ROPE, 2, dtype=jnp.float32) / MLA_ROPE)
    ang = positions.astype(jnp.float32)[..., None] * inv_freq
    return jnp.cos(ang)[:, :, None, :], jnp.sin(ang)[:, :, None, :]

def apply_rope(x, cos, sin):
    half = x.shape[-1] // 2
    x1, x2 = x[..., :half], x[..., half:]
    c, s = cos.astype(x.dtype), sin.astype(x.dtype)
    return jnp.concatenate([x1 * c - x2 * s, x2 * c + x1 * s], axis=-1)

def gla_chunked(q, k, v, log_a):
    out_dtype = v.dtype
    B, S, H, DK = q.shape
    DV = v.shape[-1]
    NC = S // CHUNK

    def to_chunks(t):
        return t.astype(jnp.float32).reshape(B, NC, CHUNK, H, -1).transpose(1, 0, 3, 2, 4)

    qc, kc, vc, gc = to_chunks(q), to_chunks(k), to_chunks(v), to_chunks(log_a)
    causal = jnp.tril(jnp.ones((CHUNK, CHUNK), dtype=bool))[:, :, None]

    def step(state, inp):
        qi, ki, vi, gi = inp
        b = jnp.cumsum(gi, axis=2)
        b_last = b[:, :, -1:, :]
        o_inter = jnp.einsum('bhtk,bhkv->bhtv', qi * jnp.exp(b), state)
        diff = b[:, :, :, None, :] - b[:, :, None, :, :]
        decay = jnp.exp(jnp.where(causal, diff, -jnp.inf))
        scores = jnp.einsum('bhtk,bhsk,bhtsk->bhts', qi, ki, decay)
        o_intra = jnp.einsum('bhts,bhsv->bhtv', scores, vi)
        k_dec = ki * jnp.exp(b_last - b)
        state = state * jnp.exp(b_last[:, :, 0, :, None]) + jnp.einsum('bhsk,bhsv->bhkv', k_dec, vi)
        return state, o_inter + o_intra

    state0 = jnp.zeros((B, H, DK, DV), dtype=jnp.float32)
    _, oc = lax.scan(step, state0, (qc, kc, vc, gc))
    return oc.transpose(1, 0, 3, 2, 4).reshape(B, S, H, DV).astype(out_dtype)

def mla_attention(q, k, v):
    S = q.shape[1]
    scale = 1.0 / math.sqrt(MLA_QK)
    outs = []
    for blk in range(S // Q_BLOCK):
        qs, qe = blk * Q_BLOCK, (blk + 1) * Q_BLOCK
        qb, kb, vb = q[:, qs:qe], k[:, :qe], v[:, :qe]
        logits = jnp.einsum('bqhd,bkhd->bhqk', qb, kb).astype(jnp.float32) * scale
        q_chunk = (jnp.arange(qs, qe) // CHUNK)[:, None]
        k_chunk = (jnp.arange(qe) // CHUNK)[None, :]
        logits = jnp.where(k_chunk <= q_chunk, logits, -jnp.inf)
        probs = jax.nn.softmax(logits, axis=-1).astype(vb.dtype)
        outs.append(jnp.einsum('bhqk,bkhd->bqhd', probs, vb))
    return jnp.concatenate(outs, axis=1)

def first_inputs(seed: int = 0) -> dict:
    key = jax.random.key(seed)
    ks = jax.random.split(key, 24)
    f32 = jnp.float32

    def w(k, shape, fan_in):
        return jax.random.normal(k, shape, f32) * (fan_in ** -0.5)

    def gain(k, shape):
        return 1.0 + 0.1 * jax.random.normal(k, shape, f32)

    x = jax.random.normal(ks[0], (BATCH, SEQ, D_MODEL), f32)
    p = jax.random.normal(ks[1], (DEPTH, BATCH, SEQ, PLE_DIM), f32)
    offset = jax.random.randint(ks[2], (BATCH,), 0, 64, dtype=jnp.int32) * CHUNK
    positions = (offset[:, None] + jnp.arange(SEQ, dtype=jnp.int32)[None, :]).astype(jnp.int32)
    return {
        "x": x,
        "p": p,
        "positions": positions,
        "attn_norm": gain(ks[3], (DEPTH, D_MODEL)),
        "w_in": w(ks[4], (DEPTH, D_MODEL, D_IN), D_MODEL),
        "gla_gate_w2": w(ks[5], (DEPTH, GLA_GATE_RANK, GLA_HEADS * GLA_DK), GLA_GATE_RANK),
        "gla_gate_b": 0.1 * jax.random.normal(ks[6], (DEPTH, GLA_HEADS * GLA_DK), f32),
        "gla_out_norm": gain(ks[7], (DEPTH, GLA_DV)),
        "mla_q_norm": gain(ks[8], (DEPTH, MLA_Q_RANK)),
        "mla_w_uq": w(ks[9], (DEPTH, MLA_Q_RANK, MLA_HEADS * MLA_QK), MLA_Q_RANK),
        "mla_kv_norm": gain(ks[10], (DEPTH, MLA_KV_RANK)),
        "mla_w_ukv": w(ks[11], (DEPTH, MLA_KV_RANK, MLA_HEADS * (MLA_NOPE + MLA_V)), MLA_KV_RANK),
        "qk_norm_q": gain(ks[12], (DEPTH, MLA_QK)),
        "qk_norm_k": gain(ks[13], (DEPTH, MLA_QK)),
        "w_out": w(ks[14], (DEPTH, D_MIX, D_MODEL), D_MIX),
        "mlp_norm": gain(ks[15], (DEPTH, D_MODEL)),
        "w_mlp_up": w(ks[16], (DEPTH, D_MODEL, D_FF), D_MODEL),
        "w_mlp_down": w(ks[17], (DEPTH, D_FF, D_MODEL), D_FF),
        "ple_norm": gain(ks[18], (DEPTH, D_MODEL)),
        "w_ple_gate": w(ks[19], (DEPTH, D_MODEL, D_MODEL), D_MODEL),
        "b_ple_gate": 0.1 * jax.random.normal(ks[20], (DEPTH, D_MODEL), f32),
        "w_ple_proj": w(ks[21], (DEPTH, PLE_DIM, D_MODEL), PLE_DIM),
    }

def first_block(x, p, positions, attn_norm, w_in, gla_gate_w2, gla_gate_b, gla_out_norm,
              mla_q_norm, mla_w_uq, mla_kv_norm, mla_w_ukv, qk_norm_q, qk_norm_k,
              w_out, mlp_norm, w_mlp_up, w_mlp_down, ple_norm, w_ple_gate, b_ple_gate,
              w_ple_proj):
    B, S, _ = x.shape
    cos, sin = rope_cos_sin(positions)
    h = x
    for i in range(DEPTH):
        n = rms_norm(h, attn_norm[i])
        z = n @ w_in[i]
        gq, gk, gv, g_low, g_r, c_q, c_kv, k_r = split_cols(z, IN_SPLITS)

        q_g = gq.reshape(B, S, GLA_HEADS, GLA_DK) * (GLA_DK ** -0.5)
        k_g = gk.reshape(B, S, GLA_HEADS, GLA_DK)
        v_g = gv.reshape(B, S, GLA_HEADS, GLA_DV)
        log_a = jax.nn.log_sigmoid((g_low @ gla_gate_w2[i] + gla_gate_b[i]).astype(jnp.float32)) / GLA_TAU
        log_a = log_a.reshape(B, S, GLA_HEADS, GLA_DK)
        o_g = gla_chunked(q_g, k_g, v_g, log_a)
        o_g = rms_norm(o_g, gla_out_norm[i]).reshape(B, S, GLA_WIDTH) * jax.nn.silu(g_r)

        q_m = (rms_norm(c_q, mla_q_norm[i]) @ mla_w_uq[i]).reshape(B, S, MLA_HEADS, MLA_QK)
        kv = (rms_norm(c_kv, mla_kv_norm[i]) @ mla_w_ukv[i]).reshape(B, S, MLA_HEADS, MLA_NOPE + MLA_V)
        k_nope, v_m = kv[..., :MLA_NOPE], kv[..., MLA_NOPE:]
        k_rope = jnp.broadcast_to(k_r[:, :, None, :], (B, S, MLA_HEADS, MLA_ROPE))
        k_m = jnp.concatenate([k_nope, k_rope], axis=-1)
        q_m = rms_norm(q_m, qk_norm_q[i])
        k_m = rms_norm(k_m, qk_norm_k[i])
        q_m = jnp.concatenate([q_m[..., :MLA_NOPE], apply_rope(q_m[..., MLA_NOPE:], cos, sin)], axis=-1)
        k_m = jnp.concatenate([k_m[..., :MLA_NOPE], apply_rope(k_m[..., MLA_NOPE:], cos, sin)], axis=-1)
        o_m = mla_attention(q_m, k_m, v_m).reshape(B, S, MLA_WIDTH)

        h = h + jnp.concatenate([o_g, o_m], axis=-1) @ w_out[i]

        m = rms_norm(h, mlp_norm[i])
        h = h + jnp.square(jax.nn.relu(m @ w_mlp_up[i])) @ w_mlp_down[i]

        gate = jax.nn.sigmoid(rms_norm(h, ple_norm[i]) @ w_ple_gate[i] + b_ple_gate[i])
        h = h + (p[i] @ w_ple_proj[i]) * gate
    return h


DEPTH_2 = 2

N_MIXERS = 2
POOL_WINDOWS = (2, 4, 8, 16)
POOL_GROUPS = len(POOL_WINDOWS)
POOL_GW = D_MODEL // POOL_GROUPS
N_HEADS = 16
HEAD_DIM = D_MODEL // N_HEADS
LEFT_CHUNKS = 8
BAND_CHUNKS = LEFT_CHUNKS + 1
BAND = BAND_CHUNKS * CHUNK
REL_CLIP = 256
D_FF_2 = 2816
CONV_W = 3
N_A = (DEPTH_2 + 1) // 2
N_B = DEPTH_2 // 2


def rmsnorm(x, g):
    xf = x.astype(jnp.float32)
    y = xf * lax.rsqrt(jnp.mean(xf * xf, axis=-1, keepdims=True) + EPS)
    return (y * g.astype(jnp.float32)).astype(x.dtype)

def pool_mixer(h, w_pool, b_pool, scale):
    B, S, D = h.shape
    hf = h.astype(jnp.float32)
    csp = jnp.concatenate([jnp.zeros((B, 1, D), jnp.float32), jnp.cumsum(hf, axis=1)], axis=1)
    t = jnp.arange(S)
    outs = []
    for g, w in enumerate(POOL_WINDOWS):
        c = csp[:, :, g * POOL_GW:(g + 1) * POOL_GW]
        upper = c[:, 1:]
        lower = jnp.concatenate([jnp.zeros((B, w - 1, POOL_GW), jnp.float32), c[:, :S - w + 1]], axis=1)
        cnt = jnp.minimum(t + 1, w).astype(jnp.float32)[None, :, None]
        outs.append((upper - lower) / cnt)
    pooled = jnp.concatenate(outs, axis=-1)
    y = (pooled - hf).astype(h.dtype).reshape(B, S, POOL_GROUPS, POOL_GW)
    y = jnp.einsum('bsgc,gcd->bsgd', y, w_pool).reshape(B, S, D) + b_pool
    return y * scale

def head_rmsnorm(x, g):
    xf = x.astype(jnp.float32)
    y = xf * lax.rsqrt(jnp.mean(xf * xf, axis=-1, keepdims=True) + EPS)
    return (y * g.astype(jnp.float32)).astype(x.dtype)

def chunk_attention(h, w_qkv, q_norm, k_norm, rel_table, w_o):
    B, S, D = h.shape
    nc = S // CHUNK
    qkv = h @ w_qkv
    q, k, v = jnp.split(qkv, 3, axis=-1)
    q = head_rmsnorm(q.reshape(B, S, N_HEADS, HEAD_DIM), q_norm)
    k = head_rmsnorm(k.reshape(B, S, N_HEADS, HEAD_DIM), k_norm)
    v = v.reshape(B, S, N_HEADS, HEAD_DIM)
    q = q.reshape(B, nc, CHUNK, N_HEADS, HEAD_DIM)
    pad = jnp.zeros((B, LEFT_CHUNKS, CHUNK, N_HEADS, HEAD_DIM), k.dtype)
    kp = jnp.concatenate([pad, k.reshape(B, nc, CHUNK, N_HEADS, HEAD_DIM)], axis=1)
    vp = jnp.concatenate([pad, v.reshape(B, nc, CHUNK, N_HEADS, HEAD_DIM)], axis=1)
    rel = jnp.arange(CHUNK)[:, None] - jnp.arange(BAND)[None, :] + LEFT_CHUNKS * CHUNK
    idx = jnp.clip(rel, -REL_CLIP, REL_CLIP) + REL_CLIP
    bias = rel_table.astype(jnp.float32)[:, idx]
    band_chunk = jnp.repeat(jnp.arange(BAND_CHUNKS), CHUNK)
    scale = HEAD_DIM ** -0.5

    def one_chunk(c):
        qc = lax.dynamic_index_in_dim(q, c, axis=1, keepdims=False)
        kb = lax.dynamic_slice_in_dim(kp, c, BAND_CHUNKS, axis=1).reshape(B, BAND, N_HEADS, HEAD_DIM)
        vb = lax.dynamic_slice_in_dim(vp, c, BAND_CHUNKS, axis=1).reshape(B, BAND, N_HEADS, HEAD_DIM)
        s = jnp.einsum('bqhd,bkhd->bhqk', qc, kb).astype(jnp.float32) * scale + bias[None]
        valid = (band_chunk + c - LEFT_CHUNKS) >= 0
        s = jnp.where(valid[None, None, None, :], s, -1e30)
        p = jax.nn.softmax(s, axis=-1).astype(vb.dtype)
        return jnp.einsum('bhqk,bkhd->bqhd', p, vb)

    o = lax.map(one_chunk, jnp.arange(nc))
    o = jnp.transpose(o, (1, 0, 2, 3, 4)).reshape(B, S, D)
    return o @ w_o

def conv_ffn(h, w_gate, w_val, conv_w, conv_b, w_out):
    S = h.shape[1]
    a = h @ w_gate
    ap = jnp.pad(a, ((0, 0), (CONV_W - 1, 0), (0, 0)))
    a = ap[:, 0:S] * conv_w[0] + ap[:, 1:S + 1] * conv_w[1] + ap[:, 2:S + 2] * conv_w[2] + conv_b
    return (jax.nn.silu(a) * (h @ w_val)) @ w_out

def second_inputs(seed: int = 0) -> dict:
    key = jax.random.key(seed)
    ks = jax.random.split(key, 16)
    f32 = jnp.float32
    D, F = D_MODEL, D_FF_2
    nrm = lambda k, shape, s: jax.random.normal(k, shape, f32) * s
    return {
        "x": nrm(ks[0], (BATCH, SEQ, D), 1.0),
        "mix_norm": 1.0 + nrm(ks[1], (DEPTH_2, D), 0.02),
        "ffn_norm": 1.0 + nrm(ks[2], (DEPTH_2, D), 0.02),
        "pool_w": nrm(ks[3], (N_A, POOL_GROUPS, POOL_GW, POOL_GW), POOL_GW ** -0.5),
        "pool_b": nrm(ks[4], (N_A, D), 0.02),
        "pool_scale": 1.0 + nrm(ks[5], (N_A, D), 0.1),
        "attn_wqkv": nrm(ks[6], (N_B, D, 3 * D), D ** -0.5),
        "attn_q_norm": 1.0 + nrm(ks[7], (N_B, HEAD_DIM), 0.02),
        "attn_k_norm": 1.0 + nrm(ks[8], (N_B, HEAD_DIM), 0.02),
        "attn_rel_bias": nrm(ks[9], (N_B, N_HEADS, 2 * REL_CLIP + 1), 0.1),
        "attn_wo": nrm(ks[10], (N_B, D, D), D ** -0.5),
        "ffn_w_gate": nrm(ks[11], (DEPTH_2, D, F), D ** -0.5),
        "ffn_w_val": nrm(ks[12], (DEPTH_2, D, F), D ** -0.5),
        "ffn_conv_w": nrm(ks[13], (DEPTH_2, CONV_W, F), CONV_W ** -0.5),
        "ffn_conv_b": nrm(ks[14], (DEPTH_2, F), 0.02),
        "ffn_w_out": nrm(ks[15], (DEPTH_2, F, D), F ** -0.5),
    }

def second_block(x, mix_norm, ffn_norm, pool_w, pool_b, pool_scale, attn_wqkv, attn_q_norm,
              attn_k_norm, attn_rel_bias, attn_wo, ffn_w_gate, ffn_w_val, ffn_conv_w,
              ffn_conv_b, ffn_w_out):
    for i in range(DEPTH_2):
        h = rmsnorm(x, mix_norm[i])
        j = i // N_MIXERS
        if i % N_MIXERS == 0:
            x = x + pool_mixer(h, pool_w[j], pool_b[j], pool_scale[j])
        else:
            x = x + chunk_attention(h, attn_wqkv[j], attn_q_norm[j], attn_k_norm[j],
                                    attn_rel_bias[j], attn_wo[j])
        h = rmsnorm(x, ffn_norm[i])
        x = x + conv_ffn(h, ffn_w_gate[i], ffn_w_val[i], ffn_conv_w[i], ffn_conv_b[i], ffn_w_out[i])
    return x


def setup_inputs(seed=0):
    out = dict(first_inputs(seed))
    for name, value in second_inputs(seed + 1).items():
        if name != "x":
            out[name + "_2"] = value
    return out


def reference(
    x, p, positions, attn_norm, w_in, gla_gate_w2, gla_gate_b, gla_out_norm, mla_q_norm,
    mla_w_uq, mla_kv_norm, mla_w_ukv, qk_norm_q, qk_norm_k, w_out, mlp_norm, w_mlp_up,
    w_mlp_down, ple_norm, w_ple_gate, b_ple_gate, w_ple_proj, mix_norm_2, ffn_norm_2, pool_w_2,
    pool_b_2, pool_scale_2, attn_wqkv_2, attn_q_norm_2, attn_k_norm_2, attn_rel_bias_2,
    attn_wo_2, ffn_w_gate_2, ffn_w_val_2, ffn_conv_w_2, ffn_conv_b_2, ffn_w_out_2,
):
    x = first_block(
        x, p, positions, attn_norm, w_in, gla_gate_w2, gla_gate_b, gla_out_norm, mla_q_norm,
        mla_w_uq, mla_kv_norm, mla_w_ukv, qk_norm_q, qk_norm_k, w_out, mlp_norm, w_mlp_up,
        w_mlp_down, ple_norm, w_ple_gate, b_ple_gate, w_ple_proj,
    )
    return second_block(
        x, mix_norm_2, ffn_norm_2, pool_w_2, pool_b_2, pool_scale_2, attn_wqkv_2, attn_q_norm_2,
        attn_k_norm_2, attn_rel_bias_2, attn_wo_2, ffn_w_gate_2, ffn_w_val_2, ffn_conv_w_2,
        ffn_conv_b_2, ffn_w_out_2,
    )


_drawn_inputs = setup_inputs


def setup_inputs(seed=0):
    import zlib

    import numpy as np

    out = dict(_drawn_inputs(seed))
    spreads = {}
    factors = {'gla_gate_b': 2.862,
     'mla_q_norm': 5.756,
     'mla_kv_norm': 3.155,
     'qk_norm_q': 5.426,
     'qk_norm_k': 5.377,
     'ple_norm': 4.417,
     'b_ple_gate': 4.48,
     'mix_norm_2': 5.76,
     'ffn_norm_2': 4.712,
     'pool_b_2': 4.63,
     'attn_q_norm_2': 8.0,
     'attn_k_norm_2': 8.0,
     'attn_rel_bias_2': 8.0,
     'ffn_conv_b_2': 6.759}
    for name, (base, spread) in spreads.items():
        noise = np.random.default_rng([zlib.crc32(name.encode()), seed]).standard_normal(out[name].shape)
        drawn = base * np.exp(spread * noise) if base else spread * noise
        out[name] = __import__('jax').numpy.asarray(drawn.astype(out[name].dtype))
    for name, factor in factors.items():
        out[name] = (out[name] * factor).astype(out[name].dtype)
    return out
```

```python
import math
from contextlib import ExitStack

import numpy as np
import concourse.bass as bass
from concourse import mybir

F = mybir.dt.float32
R = mybir.dt.float32r
I32 = mybir.dt.int32
ALU = mybir.AluOpType
ACT = mybir.ActivationFunctionType
AX = mybir.AxisListType

P = 128
S = 512
D = 1024
NT = 4
EPS = 1e-6
UE = 2048

GH, GK, GV = 4, 64, 128
MH, MN, MR, MV, MQ = 8, 64, 32, 64, 96
H2, HD2 = 16, 64
FF2 = 2816
NJ = FF2 // P
GROUPS2 = [(0, 8), (8, 16), (16, 22)]
LEVELS = [32, 16, 8, 4, 2, 1]
WINDOWS = (2, 4, 8, 16)

PC_ATT, PC_MLP, PC_PLE, PC_BPLE, PC_MIX, PC_FFN = 0, 8, 16, 24, 32, 48
PC_PB, PC_PS, PC_CW, PC_CB, PC_GB, PC_GN, PC_QN, PC_KVN = 64, 72, 80, 212, 256, 258, 259, 261
NPC = 262
C_ID, C_ONE, C_HALF, C_SCAN, C_MA, C_MB, C_IF, C_CNT = 0, 128, 256, 384, 896, 1024, 1152, 1168
NCC = 1168 + 64
ROWS = 2 * MQ + 2 * HD2

TWO_PI = 2.0 * math.pi


def cody_waite():
    parts, rest = [], TWO_PI
    for bits in (8, 8, 8):
        e = math.floor(math.log2(abs(rest)))
        q = 2.0 ** (e - bits + 1)
        parts.append(math.floor(rest / q) * q)
        rest -= parts[-1]
    return parts + [float(np.float32(rest))]


def unit_plan():
    plan = [("small", 0, 8 * 48), ("cq", 0, 2048), ("ckv", 0, 1024), ("gq", 0, 2048), ("gk", 0, 2048),
            ("gv", 0, 2048), ("gv", 1, 2048), ("gr", 0, 2048), ("gr", 1, 2048), ("uq", 0, 1536), ("ukv", 0, 1024)]
    plan += [("wout", i, 2048) for i in range(4)]
    for g in range(4):
        plan += [("up", 4 * g + i, 2048) for i in range(4)]
    order = plan[:-16]
    ups, k = plan[-16:], 0
    for g in range(5):
        if g < 4:
            order += ups[4 * g:4 * g + 1]
        if g > 0:
            order += [("down", 4 * (g - 1) + i, 2048) for i in range(4)]
        if g < 4:
            order += ups[4 * g + 1:4 * g + 4]
    order += [("proj", 0, 2048)] + [("pg", i, 2048) for i in range(4)] + [("pool", 0, 2048)]

    def ffn(l):
        out = []
        pairs = [[4 * g + i for i in range((b - a) // 2)] for g, (a, b) in enumerate(GROUPS2)]
        for g in range(4):
            if g < 3:
                out += [(f"gate{l}", pairs[g][0], 2048), (f"val{l}", pairs[g][0], 2048)]
            if g > 0:
                kc = GROUPS2[g - 1][1] - GROUPS2[g - 1][0]
                out += [(f"fo{l}", 4 * (g - 1) + i, kc * 256) for i in range(4)]
            if g < 3:
                for j in pairs[g][1:]:
                    out += [(f"gate{l}", j, 2048), (f"val{l}", j, 2048)]
        return out

    order += ffn(0)
    order += [("qkv", i, 2048) for i in range(12)]
    order += [("wo", i, 2048) for i in range(4)]
    order += ffn(1)
    return order


class Prog:

    def __init__(self, sems):
        self.q = {k: [] for k in ("tensor", "vector", "scalar", "gpsimd", "sync")}
        self.n = {k: 0 for k in self.q}
        self.sems = sems

    def __call__(self, eng, fn, waits=(), count=True):
        if count:
            self.n[eng] += 1
        self.q[eng].append((fn, [w for w in waits if w is not None], self.sems[eng] if count else None, 1))
        return (eng, self.n[eng]) if count else None

    def dma(self, eng, out, in_, sem, total, waits=()):
        self.q[eng].append((lambda e: e.dma_start(out, in_), [w for w in waits if w is not None], sem, 16))
        return (sem, total)

    def play(self, eng, e):
        seen = {}
        for fn, waits, sem, by in self.q[eng]:
            for w, n in waits:
                s = self.sems[w] if isinstance(w, str) else w
                if seen.get(id(s), 0) < n:
                    e.wait_ge(s, n)
                    seen[id(s)] = n
            ins = fn(e)
            if sem is not None:
                ins.then_inc(sem, by)


def build(nc, W, XT, PT, PV, ROW, GW2, POS, REL, CST, MSK, OUT):
    plan = unit_plan()
    ctx = ExitStack()
    with ctx:
        sems = {k: ctx.enter_context(nc.semaphore(f"s_{k}")) for k in ("tensor", "vector", "scalar", "gpsimd", "sync")}
        pr = Prog(sems)
        nsem = [0]

        def newsem():
            nsem[0] += 1
            return ctx.enter_context(nc.semaphore(f"s_x{nsem[0]}"))

        def sb(name, shape, dt=F, at=None):
            return (at or ctx).enter_context(nc.sbuf_tensor(name, shape, dt))

        bank = [ctx.enter_context(nc.psum_tensor(f"bank{i}", [P, 512], F)) for i in range(8)]
        bfree = [[] for _ in range(8)]

        cst = sb("cst", [P, NCC])
        par = sb("par", [P, NPC])
        X = sb("X", [P, 8, S])
        AH = sb("AH", [P, 8, S], R)
        AL = sb("AL", [P, 8, S], R)
        NR, NW = 2, 3
        RAW = [sb(f"RAW{i}", [P, UE]) for i in range(NR)]
        WH = [sb(f"WH{i}", [P, UE], R) for i in range(NW)]
        WL = [sb(f"WL{i}", [P, UE], R) for i in range(NW)]
        rb = sb("rb", [P, S])
        sq = [sb(f"sq{i}", [P, S]) for i in range(2)]
        dg = sb("dg", [P, 4, P])
        t2s = [sb(f"t2s{i}", [P, S]) for i in range(2)]
        row = sb("row", [P, ROWS])
        r4 = sb("r4", [P, 4])
        m4 = sb("m4", [P, 4])
        ident = cst[:, C_ID:C_ID + P]
        ones = cst[:, C_ONE:C_ONE + P]

        def V(fn, *w):
            return pr("vector", fn, w)

        def A(fn, *w):
            return pr("scalar", fn, w)

        def G(fn, *w):
            return pr("gpsimd", fn, w)

        def T(fn, *w, count=False):
            return pr("tensor", fn, w, count)

        def tt(out, a, b, op, *w):
            return V(lambda e: e.tensor_tensor(out, a, b, op), *w)

        def ts(out, a, s1, op0, *w, s2=None, op1=None):
            if op1 is None:
                return V(lambda e: e.tensor_scalar(out, a, s1, None, op0), *w)
            return V(lambda e: e.tensor_scalar(out, a, s1, s2, op0, op1), *w)

        def stt(out, a, s, b, op0, op1, *w):
            return V(lambda e: e.scalar_tensor_tensor(out, a, s, b, op0, op1), *w)

        def act(out, a, f, *w, **k):
            return A(lambda e: e.activation(out, a, f, **k), *w)

        def mm(out, l, r, start, stop, *w, count=False, share=False):
            return T(lambda e: e.matmul(out, l, r, start=start, stop=stop, skip_group_check=share), *w, count=count)

        def tr(out, a, *w, count=False):
            k = a.shape[0]
            return T(lambda e: e.transpose(out, a, ident[0:k, 0:k]), *w, count=count)

        s_c, s_p, s_xl = newsem(), newsem(), newsem()
        t_x = pr.dma("sync", X[:, :, :], XT, s_xl, 16)
        t_p = pr.dma("sync", par[:, :], PV, s_p, 16)
        t_c = pr.dma("sync", cst[:, :], CST, s_c, 16)

        s_w = [newsem() for _ in range(NR)]
        raw_free = {}
        pe_done = {}
        hi_tok, lo_tok = {}, {}
        w_tok = {}

        def load(u):
            w = raw_free.get(u - NR, [])
            n = plan[u][2]
            w_tok[u] = pr.dma("sync", RAW[u % NR][:, 0:n], W[u, :, 0:n], s_w[u % NR], 16 * (u // NR + 1), w)

        def split(u):
            if u >= len(plan):
                return
            n, i, j = plan[u][2], u % NR, u % NW
            free = pe_done.get(u - NW)
            hi_tok[u] = act(WH[j][:, 0:n], RAW[i][:, 0:n], ACT.Copy, w_tok[u], free)
            lo_tok[u] = tt(WL[j][:, 0:n], RAW[i][:, 0:n], WH[j][:, 0:n].bitcast(F), ALU.subtract, hi_tok[u], free)
            raw_free[u] = [hi_tok[u], lo_tok[u]]
            if u + NR < len(plan):
                load(u + NR)

        for u in range(NR):
            load(u)
        cur = [0]

        def take(name, idx):
            u = cur[0]
            assert plan[u][:2] == (name, idx), (u, plan[u], name, idx)
            cur[0] += 1
            split(u + 2)
            j, n = u % NW, plan[u][2]
            return u, WH[j][:, 0:n], WL[j][:, 0:n], [hi_tok[u], lo_tok[u]]

        main = [0]

        def mbank():
            b = main[0] % 4
            main[0] += 1
            return b

        def prod_t(b, wh, wl, cols, kcs, ah, al, rows, waits, last=None, first=True, m=P):
            tok = None
            n = len(kcs)
            for i, (k, r) in enumerate(zip(kcs, rows)):
                w = list(waits[i]) if waits else []
                if i == 0 and first:
                    w += bfree[b]
                a, c = wh[:, k, cols], wl[:, k, cols]
                st = first and i == 0
                en = i == n - 1
                mm(bank[b][0:m, :], a, ah[:, r, :], st, False, *w)
                mm(bank[b][0:m, :], a, al[:, r, :], False, False)
                tok = mm(bank[b][0:m, :], c, ah[:, r, :], False, en, count=en)
            return tok

        split(0)
        split(1)

        sqr = [[], []]

        def square_small(src, c, n, b, col, start, *w):
            k = c % 2
            t = act(sq[k][:, :], src, ACT.Square, *w, *sqr[k])
            tok = None
            for q in range(NT):
                tok = mm(bank[b][:, col + q:col + q + 1], sq[k][:, q * P:(q + 1) * P], ones[:, 0:1],
                         start and q == 0, c == n - 1, t, t_c, *(bfree[b] if start and q == 0 else []),
                         count=q == NT - 1, share=True)
            sqr[k] = [tok]
            return tok

        def rpow(out, src, tmp, scale, *w):
            t1 = ts(tmp, src, scale, ALU.mult, *w, s2=EPS, op1=ALU.add)
            n = out.shape[1]
            return t1, G(lambda e: e.tensor_tensor(out, tmp, cst[:, C_HALF:C_HALF + n], ALU.pow), t1, t_c)

        spread_free = [[], []]

        def spread(r, b, w, dst=None):
            t = tt(dg[:, :, :], ident[:, None, :].to_broadcast([P, 4, P]), r[:, :, None].to_broadcast([P, 4, P]),
                   ALU.mult, *w, *spread_free[0], t_c)
            t2 = mm(bank[b][:, :], ones, dg[:, :, :].rearrange("p q n -> p (q n)"), True, True, t, *bfree[b], count=True)
            spread_free[0] = [t2]
            if dst is None:
                return t2
            t3 = act(dst, bank[b][:, :], ACT.Copy, t2, *spread_free[1])
            bfree[b] = [t3]
            return t3

        a_free = [[] for _ in range(8)]

        def prep(c, gcol, w):
            g = par[:, gcol + c:gcol + c + 1]
            t1 = ts(AH[:, c, :], X[:, c, :], g, ALU.mult, *w, *a_free[c], t_p)
            t2 = stt(AL[:, c, :], X[:, c, :], g, AH[:, c, :].bitcast(F), ALU.mult, ALU.subtract, t1)
            return [t1, t2]

        SB_ = 7

        def norm_in(gcol, c, w):
            tk = square_small(X[:, c, :], c, 8, SB_, 0, c == 0, *w)
            return tk, prep(c, gcol, w)

        rb_free = [[]]

        def norm_r(tk):
            t1, t2 = rpow(r4[:, :], bank[SB_][:, 0:4], m4[:, :], 1.0 / D, tk)
            bfree[SB_] = [t1]
            return t2

        def norm_spread(t2):
            spread_free[1] = rb_free[0]
            return spread(r4, SB_, [t2], rb[:, :])

        ph1 = ExitStack()
        ctx.enter_context(ph1)
        cqH = sb("cqH", [P, 3, S], R, ph1)
        cqL = sb("cqL", [P, 3, S], R, ph1)
        rq3 = sb("rq3", [P, 8], F, ph1)
        mq3 = sb("mq3", [P, 8], F, ph1)
        kr = sb("kr", [P, 4, 32], F, ph1)
        gla = ExitStack()
        ctx.enter_context(gla)
        msk = sb("msk", [P, 7, P], I32, gla)
        gw2 = sb("gw2", [16, 256], F, gla)
        s_m, s_g = newsem(), newsem()
        t_m = pr.dma("sync", msk[:, :, :], MSK, s_m, 16)
        t_g = pr.dma("sync", gw2[:, :], GW2, s_g, 16)
        gq = sb("gq", [P, 2, S], F, gla)
        gk = sb("gk", [P, 2, S], F, gla)
        gb = sb("gb", [P, 2, S], F, gla)
        gsil = sb("gsil", [P, 4, S], F, gla)
        gv = sb("gv", [P, 4, 512], F, gla)
        dd = sb("dd", [P, 2, S], F, gla)
        glow = dd[0:16, 0, :]

        xk = [None] * 8
        tk = None
        for c in range(8):
            tk, xk[c] = norm_in(PC_ATT, c, [t_x])
        t_r4 = norm_r(tk)

        u, wh, wl, wt = take("small", 0)
        whv, wlv = wh.rearrange("p (k n) -> p k n", k=8), wl.rearrange("p (k n) -> p k n", k=8)
        b0 = mbank()
        tg0 = prod_t(b0, whv, wlv, slice(0, 16), range(8), AH, AL, range(8), [wt + xk[i] for i in range(8)], m=16)
        b1 = mbank()
        for q in range(NT):
            for k in range(8):
                o = bank[b1][:, 32 * q:32 * q + 32]
                l = AH[:, k, q * P:(q + 1) * P]
                mm(o, l, whv[:, k, 16:48], q == 0 and k == 0, False, *bfree[b1], share=True)
                mm(o, l, wlv[:, k, 16:48], False, False, share=True)
                tkr = mm(o, AL[:, k, q * P:(q + 1) * P], whv[:, k, 16:48], False, k == 7, count=k == 7, share=True)
        pe_done[u] = tkr
        t_rb = norm_spread(t_r4)
        tgl = tt(glow, bank[b0][0:16, :], rb[0:16, :], ALU.mult, tg0, t_rb)
        bfree[b0] = [tgl]
        for q in range(NT):
            tkr = ts(kr[:, q, :], bank[b1][:, 32 * q:32 * q + 32], r4[:, q:q + 1], ALU.mult, tkr, t_r4)
        bfree[b1] = [tkr]
        t_kr = tkr

        ctmp = t2s
        cfree = [[], []]
        t_cq = [None] * 3
        tsq = [None] * 3
        for i in range(3):
            if i != 1:
                u, wh, wl, wt = take("cq" if i == 0 else "ckv", 0)
                nn = 256 if i == 0 else 128
                whv, wlv = wh.rearrange("p (k n) -> p k n", k=8), wl.rearrange("p (k n) -> p k n", k=8)
            b = mbank()
            col = (i % 2) * P
            t = prod_t(b, whv, wlv, slice(col, col + P), range(8), AH, AL, range(8), [wt] * 8)
            if i != 0:
                pe_done[u] = t
            k = i % 2
            t1 = tt(ctmp[k][:, :], bank[b][:, :], rb[:, :], ALU.mult, t, t_rb, *cfree[k])
            bfree[b] = [t1]
            tsq[i] = square_small(ctmp[k][:, :], i if i < 2 else 0, 2 if i < 2 else 1, SB_ - 1, 0 if i < 2 else 4, i == 0, t1)
            g = par[:, PC_QN + i:PC_QN + i + 1]
            t2 = ts(cqH[:, i, :], ctmp[k][:, :], g, ALU.mult, t1, t_p)
            t3 = stt(cqL[:, i, :], ctmp[k][:, :], g, cqH[:, i, :].bitcast(F), ALU.mult, ALU.subtract, t2)
            cfree[k] = [t3, tsq[i]]
            t_cq[i] = [t2, t3]
        t1 = ts(mq3[:, 0:4], bank[SB_ - 1][:, 0:4], 1.0 / 256, ALU.mult, tsq[2], s2=EPS, op1=ALU.add)
        t2 = ts(mq3[:, 4:8], bank[SB_ - 1][:, 4:8], 1.0 / 128, ALU.mult, tsq[2], s2=EPS, op1=ALU.add)
        bfree[SB_ - 1] = [t1, t2]
        t_rq3 = G(lambda e: e.tensor_tensor(rq3[:, :], mq3[:, :], cst[:, C_HALF:C_HALF + 8], ALU.pow), t1, t2, t_c)

        t_gq, t_gk = [None, None], [None, None]
        for name, dst, scale, toks in (("gq", gq, GK ** -0.5, t_gq), ("gk", gk, 1.0, t_gk)):
            u, wh, wl, wt = take(name, 0)
            whv, wlv = wh.rearrange("p (k n) -> p k n", k=8), wl.rearrange("p (k n) -> p k n", k=8)
            for i in range(2):
                b = mbank()
                t = prod_t(b, whv, wlv, slice(i * P, i * P + P), range(8), AH, AL, range(8), [wt] * 8)
                toks[i] = stt(dst[:, i, :], bank[b][:, :], scale, rb[:, :], ALU.mult, ALU.mult, t, t_rb)
                bfree[b] = [toks[i]]
            pe_done[u] = t
        t_b = [None, None]
        for j in range(2):
            b = 5
            t = mm(bank[b][:, :], gw2[:, j * P:(j + 1) * P], glow, True, True, tgl, t_g, *bfree[b], count=True)
            t1 = ts(ctmp[0][:, :], bank[b][:, :], par[:, PC_GB + j:PC_GB + j + 1], ALU.add, t, t_p, *cfree[0])
            bfree[b] = [t1]
            t2 = act(ctmp[1][:, :], ctmp[0][:, :], ACT.Abs, t1, *cfree[1])
            t3 = act(ctmp[1][:, :], ctmp[1][:, :], ACT.Exp, t2, scale=-1.0)
            t4 = act(ctmp[1][:, :], ctmp[1][:, :], ACT.Ln, t3, bias=1.0)
            t5 = stt(ctmp[0][:, :], ctmp[0][:, :], 0.0, ctmp[1][:, :], ALU.min, ALU.subtract, t4, t1)
            cfree[1] = [t5]
            oj = gb[:, j, :]
            t_b[j] = V(lambda e, oj=oj: e.tensor_tensor_scan(oj, cst[:, C_SCAN:C_SCAN + S], ctmp[0][:, :], 0.0,
                                                           ALU.mult, ALU.add), t5, t_c)
            cfree[0] = [t_b[j]]

        bs = [mbank() for _ in range(NT)]
        for hlf in range(2):
            u, wh, wl, wt = take("gv", hlf)
            whv, wlv = wh.rearrange("p (k n) -> p k n", k=4), wl.rearrange("p (k n) -> p k n", k=4)
            for q in range(NT):
                for k in range(4):
                    kk = 4 * hlf + k
                    o = bank[bs[q]][:, :]
                    st = hlf == 0 and k == 0
                    en = k == 3
                    ah, al = AH[:, kk, q * P:(q + 1) * P], AL[:, kk, q * P:(q + 1) * P]
                    mm(o, ah, whv[:, k, :], st, False, *wt, *(bfree[bs[q]] if st else []))
                    mm(o, ah, wlv[:, k, :], False, False)
                    t = mm(o, al, whv[:, k, :], False, en and hlf == 1, count=en)
                if hlf == 1:
                    t_gv = ts(gv[:, q, :], bank[bs[q]][:, :], r4[:, q:q + 1], ALU.mult, t, t_r4)
                    bfree[bs[q]] = [t_gv]
            pe_done[u] = t

        t_sil = [None] * 4
        for i in range(2):
            u, wh, wl, wt = take("gr", i)
            whv, wlv = wh.rearrange("p (k n) -> p k n", k=8), wl.rearrange("p (k n) -> p k n", k=8)
            for c in range(2):
                b = mbank()
                h = 2 * i + c
                t = prod_t(b, whv, wlv, slice(c * P, c * P + P), range(8), AH, AL, range(8), [wt] * 8)
                t1 = tt(gsil[:, h, :], bank[b][:, :], rb[:, :], ALU.mult, t, t_rb)
                bfree[b] = [t1]
                t_sil[h] = act(gsil[:, h, :], gsil[:, h, :], ACT.Silu, t1)
            pe_done[u] = t
        rb_free[0] = [t1]
        a_free = [[t]] * 8

        qt_ = sb("qt_", [P, 2, S], F, gla)
        kt_ = sb("kt_", [P, 2, S], F, gla)
        AT = sb("AT", [P, GH, S], F, gla)
        kd = sb("kd", [P, 4, 256], F, gla)
        ST = sb("ST", [P, 2, 7, P], F, gla)
        el = sb("el", [P, 2, 8], F, gla)
        t_at0 = G(lambda e: e.memset(AT[:, :, :], 0.0))
        f_qk = [[t_x], [t_x]]
        t_at = [t_at0] * GH
        sb4 = [0]
        for lv in range(7):
            for j in range(2):
                if lv == 0:
                    qs, ks, tq = gq, gk, [t_gq[j], t_gk[j]]
                else:
                    B = LEVELS[lv - 1]
                    bv = gb[:, j, :].rearrange("p (n w) -> p n w", w=2 * B)
                    dv = dd[:, j, :].rearrange("p (n w) -> p n w", w=2 * B)
                    n = S // (2 * B)
                    ref = bv[:, :, B - 1:B].to_broadcast([P, n, B])
                    t1 = tt(dv[:, :, B:2 * B], bv[:, :, B:2 * B], ref, ALU.subtract, t_b[j], *f_qk[j])
                    t2 = tt(dv[:, :, 0:B], ref, bv[:, :, 0:B], ALU.subtract, t_b[j])
                    t3 = act(dd[:, j, :], dd[:, j, :], ACT.Exp, t1, t2, scale=1.0 / 16)
                    t4 = tt(qt_[:, j, :], gq[:, j, :], dd[:, j, :], ALU.mult, t3, *f_qk[j])
                    t5 = tt(kt_[:, j, :], gk[:, j, :], dd[:, j, :], ALU.mult, t3, *f_qk[j])
                    qs, ks, tq = qt_, kt_, [t4, t5]
                for hh in range(2):
                    h = 2 * j + hh
                    b = 4 + sb4[0] % 3
                    sb4[0] += 1
                    rows = slice(64 * hh, 64 * hh + 64)
                    for q in range(NT):
                        cs = slice(q * P, (q + 1) * P)
                        t = mm(bank[b][:, cs], ks[rows, j, cs], qs[rows, j, cs], True, True, *tq,
                               *(bfree[b] if q == 0 else []), count=q == NT - 1, share=True)
                    m = msk[:, lv, None, :].to_broadcast([P, 4, P])
                    o = AT[:, h, :].rearrange("p (q n) -> p q n", q=4)
                    d = bank[b][:, :].rearrange("p (q n) -> p q n", q=4)
                    t_at[h] = V(lambda e, o=o, m=m, d=d: e.copy_predicated(o, m, d), t, t_at[h], t_m)
                    bfree[b] = [t_at[h]]
                if lv > 0:
                    f_qk[j] = [t, t5]
        t_kd, t_qe, t_el = [None] * 2, [None] * 2, [None] * 2
        for j in range(2):
            bv = gb[:, j, :].rearrange("p (n w) -> p n w", w=64)
            dv = dd[:, j, :].rearrange("p (n w) -> p n w", w=64)
            last = bv[:, :, 63:64]
            t_el[j] = act(el[:, j, :], last.rearrange("p n o -> p (n o)"), ACT.Exp, t_b[j], scale=1.0 / 16)
            t1 = tt(dv, last.to_broadcast([P, 8, 64]), bv, ALU.subtract, t_b[j], *f_qk[j])
            t2 = act(dd[:, j, :], dd[:, j, :], ACT.Exp, t1, scale=1.0 / 16)
            t3 = tt(kt_[:, j, :], gk[:, j, :], dd[:, j, :], ALU.mult, t2, *f_qk[j])
            t4 = act(dd[:, j, :], gb[:, j, :], ACT.Exp, t3, scale=1.0 / 16)
            t_qe[j] = tt(qt_[:, j, :], gq[:, j, :], dd[:, j, :], ALU.mult, t4, *f_qk[j])
            b = 4 + j
            for q in range(NT):
                t = tr(bank[b][:, q * P:(q + 1) * P], kt_[:, j, q * P:(q + 1) * P], t3, t_c,
                       *(bfree[b] if q == 0 else []), count=q == NT - 1)
            t_kd[j] = act(kd[:, :, j * P:(j + 1) * P], bank[b][:, :].rearrange("p (q n) -> p q n", q=4), ACT.Copy, t)
            bfree[b] = [t_kd[j]]
        t_st = [None, None]
        for j in range(2):
            tu = {}
            for c in [0, 2, 4, 6, 1, 3, 5]:
                b = 4 + 2 * j + c % 2
                r0 = 64 * (c % 2)
                for hh in range(2):
                    o = bank[b][64 * hh:64 * hh + 64, (c // 2) * P:(c // 2 + 1) * P]
                    h = 2 * j + hh
                    tu[c] = mm(o, kd[r0:r0 + 64, c // 2, j * P + 64 * hh:j * P + 64 * hh + 64],
                               gv[r0:r0 + 64, c // 2, h * GV:(h + 1) * GV], True, True, t_kd[j], t_gv,
                               *(bfree[b] if c < 2 else []), count=True, share=True)
            for c in range(7):
                b = 4 + 2 * j + c % 2
                o = bank[b][:, (c // 2) * P:(c // 2 + 1) * P]
                w = tu[6] if c % 2 == 0 else tu[5]
                if c == 0:
                    t_st[j] = V(lambda e, j=j, o=o: e.tensor_copy(ST[:, j, 0, :], o), w)
                else:
                    t_st[j] = stt(ST[:, j, c, :], ST[:, j, c - 1, :], el[:, j, c:c + 1], o, ALU.mult, ALU.add,
                                  w, t_st[j], t_el[j])
                bfree[b] = [t_st[j]]
        ogs = AT
        t_og, tgs = [None] * 4, None
        SG = 7
        rg = sb("rg", [P, 16], F, gla)
        mg = sb("mg", [P, 16], F, gla)
        for h in range(GH):
            j, hh = h // 2, h % 2
            b = mbank()
            for q in range(NT):
                cs = slice(q * P, (q + 1) * P)
                mm(bank[b][:, cs], gv[:, q, h * GV:(h + 1) * GV], AT[:, h, cs], q == 0, True, t_at[h], t_gv,
                   *(bfree[b] if q == 0 else []), share=True)
            for c in range(1, 8):
                rows = slice(64 * hh, 64 * hh + 64)
                cs = slice(c * 64, c * 64 + 64)
                t = mm(bank[b][:, cs], ST[rows, j, c - 1, :], qt_[rows, j, cs], False, True, t_st[j], t_qe[j],
                       count=c == 7, share=True)
            t_og[h] = act(ogs[:, h, :], bank[b][:, :], ACT.Copy, t)
            bfree[b] = [t_og[h]]
            k = h % 2
            t2 = act(sq[k][:, :], ogs[:, h, :], ACT.Square, t_og[h], *sqr[k])
            for q in range(NT):
                tgs = mm(bank[SG][:, 4 * h + q:4 * h + q + 1], sq[k][:, q * P:(q + 1) * P], ones[:, 0:1], True, True,
                         t2, *(bfree[SG] if h == 0 else []), count=q == NT - 1, share=True)
            sqr[k] = [tgs]
        t1 = ts(mg[:, :], bank[SG][:, 0:16], 1.0 / GV, ALU.mult, tgs, s2=EPS, op1=ALU.add)
        bfree[SG] = [t1]
        t_rg = G(lambda e: e.tensor_tensor(rg[:, :], mg[:, :], cst[:, C_HALF:C_HALF + 16], ALU.pow), t1, t_c)
        o_tok = [None] * 8
        for h in range(GH):
            b = 4 + h % 2
            t = spread(rg[:, 4 * h:4 * h + 4], b, [t_rg])
            t1 = stt(ogs[:, h, :], ogs[:, h, :], par[:, PC_GN:PC_GN + 1], bank[b][:, :], ALU.mult, ALU.mult, t, t_og[h])
            bfree[b] = [t1]
            t2 = tt(ogs[:, h, :], ogs[:, h, :], gsil[:, h, :], ALU.mult, t1, t_sil[h])
            t3 = act(AH[:, h, :], ogs[:, h, :], ACT.Copy, t2, *a_free[h])
            t4 = tt(AL[:, h, :], ogs[:, h, :], AH[:, h, :].bitcast(F), ALU.subtract, t3)
            o_tok[h] = [t3, t4]
        fence = [o_tok[h][i] for h in range(4) for i in range(2)] + [tgs, t_kd[1], t, t_rg]
        gla.close()

        mla = ExitStack()
        ctx.enter_context(mla)
        qm = sb("qm", [P, 4, MH, MQ], F, mla)
        km = sb("km", [P, 4, MH, MQ], F, mla)
        vm = sb("vm", [P, 4, 512], F, mla)
        tmp = sb("tmp", [P, 3072], F, mla)
        trig = sb("trig", [P, 8, 4, 16], F, mla)
        posi = sb("posi", [P, 4], I32, mla)
        posf = sb("posf", [P, 4], F, mla)
        s_r, s_pos = newsem(), newsem()
        t_row = pr.dma("gpsimd", row[:, :], ROW.to_broadcast([P, ROWS]), s_r, 16, fence)
        t_pos = pr.dma("gpsimd", posi[:, :], POS, s_pos, 16, fence)

        u, wh, wl, wt = take("uq", 0)
        whv, wlv = wh.rearrange("p (k n) -> p k n", k=2), wl.rearrange("p (k n) -> p k n", k=2)
        t_qm = [None] * 4
        for q in range(NT):
            for n in range(2):
                b = mbank()
                for k in range(2):
                    ah, al = cqH[:, k, q * P:(q + 1) * P], cqL[:, k, q * P:(q + 1) * P]
                    cs = slice(384 * n, 384 * n + 384)
                    o = bank[b][:, 0:384]
                    mm(o, ah, whv[:, k, cs], k == 0, False, *wt, *t_cq[0], *t_cq[1], *(bfree[b] if k == 0 else []))
                    mm(o, ah, wlv[:, k, cs], False, False)
                    t = mm(o, al, whv[:, k, cs], False, k == 1, count=k == 1)
                t_qm[q] = ts(qm[:, q, 4 * n:4 * n + 4, :], bank[b][:, 0:384].rearrange("p (h d) -> p h d", h=4),
                             rq3[:, q:q + 1], ALU.mult, t, t_rq3, *fence)
                bfree[b] = [t_qm[q]]
        pe_done[u] = t
        u, wh, wl, wt = take("ukv", 0)
        t_km, t_vm = [None] * 4, [None] * 4
        for q in range(NT):
            for n in range(2):
                b = mbank()
                ah, al = cqH[:, 2, q * P:(q + 1) * P], cqL[:, 2, q * P:(q + 1) * P]
                cs = slice(512 * n, 512 * n + 512)
                mm(bank[b][:, :], ah, wh[:, cs], True, False, *wt, *t_cq[2], *bfree[b])
                mm(bank[b][:, :], ah, wl[:, cs], False, False)
                t = mm(bank[b][:, :], al, wh[:, cs], False, True, count=True)
                if n == 0:
                    t_km[q] = ts(km[:, q, :, 0:MN], bank[b][:, :].rearrange("p (h d) -> p h d", h=8),
                                 rq3[:, 4 + q:5 + q], ALU.mult, t, t_rq3)
                    bfree[b] = [t_km[q]]
                else:
                    t_vm[q] = act(vm[:, q, :], bank[b][:, :], ACT.Copy, t, t_rq3, *fence, scale=rq3[:, 4 + q:5 + q])
                    bfree[b] = [t_vm[q]]
        pe_done[u] = t
        for q in range(NT):
            t_krb = V(lambda e, q=q: e.tensor_copy(km[:, q, :, MN:MQ], kr[:, q, None, :].to_broadcast([P, 8, 32])),
                      t_kr, *fence)
        cw = cody_waite()
        t1 = V(lambda e: e.tensor_copy(posf[:, :], posi[:, :]), t_pos)
        ang, nn_, r0_, r1_, co, si, sc = (trig[:, i, :, :].rearrange("p q f -> p (q f)") for i in range(7))
        t2 = tt(trig[:, 0, :, :], posf[:, :, None].to_broadcast([P, 4, 16]),
                cst[:, None, C_IF:C_IF + 16].to_broadcast([P, 4, 16]), ALU.mult, t1, t_c)
        M = 12582912.0
        t3 = ts(nn_, ang, 1.0 / TWO_PI, ALU.mult, t2, s2=M, op1=ALU.add)
        t3 = ts(nn_, nn_, M, ALU.subtract, t3)
        t = t3
        src = ang
        for i, c in enumerate(cw):
            dst = (r0_, r1_)[i % 2]
            t = stt(dst, nn_, -c, src, ALU.mult, ALU.add, t)
            src = dst
        PI_ = 3.1415925
        t = ts(r0_, src, PI_, ALU.min, t, s2=-PI_, op1=ALU.max)
        t_sin = act(si, r0_, ACT.Sin, t)
        t = ts(r1_, r0_, math.pi / 2, ALU.add, t)
        t = ts(sc, r1_, math.pi, ALU.is_gt, t, s2=TWO_PI, op1=ALU.mult)
        t = tt(r1_, r1_, sc, ALU.subtract, t)
        t = ts(r1_, r1_, PI_, ALU.min, t, s2=-PI_, op1=ALU.max)
        t_cos = act(co, r1_, ACT.Sin, t)
        rn = sb("rn", [P, 2, 32], F, mla)
        mn = sb("mn", [P, 2, 32], F, mla)
        t_m = [None, None]
        tf = []
        for i, (z, tz) in enumerate(((qm, t_qm), (km, t_km + [t_krb]))):
            zf = z[:, :, :, :].rearrange("p q h d -> p (q h d)")
            t = act(tmp[:, :], zf, ACT.Square, *tz, *tf, *fence)
            t = V(lambda e, i=i: e.tensor_reduce(mn[:, i, :], tmp[:, :].rearrange("p (a d) -> p a d", d=MQ), AX.X, ALU.add), t)
            t1 = ts(mn[:, i, :], mn[:, i, :], 1.0 / MQ, ALU.mult, t, s2=EPS, op1=ALU.add)
            t = G(lambda e, i=i: e.tensor_tensor(rn[:, i, :], mn[:, i, :], cst[:, C_HALF:C_HALF + 32], ALU.pow), t1, t_c)
            z3 = z[:, :, :, :].rearrange("p q h d -> p (q h) d")
            t = tt(z3, z3, rn[:, i, :, None].to_broadcast([P, 32, MQ]), ALU.mult, t)
            t = tt(z3, z3, row[:, None, MQ * i:MQ * i + MQ].to_broadcast([P, 32, MQ]), ALU.mult, t, t_row)
            x1, x2 = z[:, :, :, MN:MN + 16], z[:, :, :, MN + 16:MQ]
            tv = tmp[:, 0:2048].rearrange("p (i q h f) -> p i q h f", i=4, q=4, h=8)
            cb = trig[:, 4, :, None, :].to_broadcast([P, 4, 8, 16])
            sb_ = trig[:, 5, :, None, :].to_broadcast([P, 4, 8, 16])
            ta = tt(tv[:, 0], x1, cb, ALU.mult, t, t_cos, t1)
            tb = tt(tv[:, 1], x2, sb_, ALU.mult, t, t_sin)
            tc = tt(tv[:, 2], x2, cb, ALU.mult, t)
            td = tt(tv[:, 3], x1, sb_, ALU.mult, t)
            te = tt(x1, tv[:, 0], tv[:, 1], ALU.subtract, ta, tb, td)
            t_m[i] = tt(x2, tv[:, 2], tv[:, 3], ALU.add, tc, td, te)
            tf = [t_m[i]]


        def attention(nh, kdim, qT, kT, head_rows, fetch, v, t_v, scale, bias, hq, od, at):
            pb = [sb(f"pb{nh}_{i}", [P, 512], F, at) for i in range(3)]
            ptb = t2s
            st = sb(f"st{nh}", [P, 3, 4], F, at)
            steps = [(h, q) for h in range(nh) for q in range(NT)]
            s_t, p_t, pt_t = {}, {}, {}
            pfree, ptfree, stf = [[], [], []], [[], []], [[], [], []]
            out_t = []

            def scores(i):
                h, q = steps[i]
                tqk = fetch(h, q)
                b = i % 3
                n = (q + 1) * P
                rows = head_rows(h)
                t = mm(bank[b][:, 0:n], qT(h)[rows, q * P:(q + 1) * P], kT(h)[rows, 0:n], True, True,
                       *tqk, *bfree[b], count=bias is not None)
                if bias is None:
                    t = mm(bank[b][:, n - P:n], cst[0:1, C_MA:C_MA + P], cst[0:1, C_MB:C_MB + P], False, True,
                           count=True, share=True)
                hq(h, q, t)
                k = i % 3
                if bias is None:
                    t1 = V(lambda e: e.reduce_max(st[:, k, 0:1], bank[b][:, 0:n], AX.X), t, *stf[k])
                    t2 = ts(st[:, k, 1:2], st[:, k, 0:1], -scale, ALU.mult, t1)
                    t3 = act(pb[k][:, 0:n], bank[b][:, 0:n], ACT.Exp, t2, *pfree[k], bias=st[:, k, 1:2], scale=scale,
                             accum_out=st[:, k, 2:3])
                    bfree[b] = [t3]
                else:
                    gbuf, tg, gdone = bias(h)
                    t1 = V(lambda e: e.tensor_tensor_reduce(out=pb[k][:, 0:n], in0=bank[b][:, 0:n], in1=gbuf[:, 512 - n:512],
                                                            scale=scale, scalar=-3.0e38, op0=ALU.add, op1=ALU.max,
                                                            accum_out=st[:, k, 0:1]), t, *tg, *pfree[k], *stf[k])
                    bfree[b] = [t1]
                    gdone(t1)
                    t2 = ts(st[:, k, 1:2], st[:, k, 0:1], -1.0, ALU.mult, t1)
                    t3 = act(pb[k][:, 0:n], pb[k][:, 0:n], ACT.Exp, t2, bias=st[:, k, 1:2], accum_out=st[:, k, 2:3])
                p_t[i] = t3

            def turn(i):
                h, q = steps[i]
                k = i % 3
                b = 3 + i % 2
                for c in range(q + 1):
                    t = tr(bank[b][:, c * P:(c + 1) * P], pb[k][:, c * P:(c + 1) * P], p_t[i],
                           *(bfree[b] if c == 0 else []), count=c == q)
                pfree[k] = [t]
                n = (q + 1) * P
                t1 = V(lambda e: e.tensor_copy(ptb[i % 2][:, 0:n], bank[b][:, 0:n]), t, *ptfree[i % 2])
                bfree[b] = [t1]
                pt_t[i] = t1

            def values(i):
                h, q = steps[i]
                b = 5 + i % 2
                for c in range(q + 1):
                    t = mm(bank[b][:, 0:64], ptb[i % 2][:, c * P:(c + 1) * P], v[:, c, h * 64:(h + 1) * 64], c == 0, c == q,
                           pt_t[i], *t_v, *(bfree[b] if c == 0 else []), count=c == q)
                ptfree[i % 2] = [t]
                k = i % 3
                t1 = V(lambda e: e.reciprocal(st[:, k, 3:4], st[:, k, 2:3]), p_t[i])
                t2 = ts(od[h // 2][:, q, (h % 2) * 64:(h % 2) * 64 + 64], bank[b][:, 0:64], st[:, k, 3:4], ALU.mult, t, t1)
                bfree[b] = [t2]
                stf[k] = [t2]
                out_t.append(t2)

            n = len(steps)
            for i in range(n + 2):
                if i < n:
                    if i >= 3:
                        pass
                    scores(i)
                if 0 <= i - 1 < n:
                    turn(i - 1)
                if 0 <= i - 2 < n:
                    values(i - 2)
            return out_t[-1]

        qT = [sb(f"qT{i}", [P, S], F, mla) for i in range(2)]
        kT = [sb(f"kT{i}", [P, S], F, mla) for i in range(2)]
        qk_t = {}
        qk_free = [[], []]

        def fetch1(h, q):
            if h not in qk_t:
                k = h % 2
                toks = []
                for z, dst, tz in ((qm, qT, t_m[0]), (km, kT, t_m[1])):
                    for c in range(NT):
                        t = tr(bank[7][0:MQ, c * P:(c + 1) * P], z[:, c, h, :], tz, t_c,
                               *(bfree[7] if c == 0 else []), count=c == 3)
                    dd_ = dst[k]
                    t1 = act(dd_[0:MQ, :], bank[7][0:MQ, :], ACT.Copy, t, *qk_free[k])
                    bfree[7] = [t1]
                    toks.append(t1)
                qk_t[h] = toks
            return qk_t[h]

        def hq1(h, q, t):
            qk_free[h % 2] = [t]

        od1 = [tmp[:, i * 512:(i + 1) * 512].rearrange("p (q d) -> p q d", q=4) for i in range(4)]
        t_o = attention(MH, MQ, lambda h: qT[h % 2], lambda h: kT[h % 2], lambda h: slice(0, MQ), fetch1, vm, t_vm,
                        MQ ** -0.5, None, hq1, od1, mla)
        for i in range(4):
            b = mbank()
            for q in range(NT):
                t = tr(bank[b][:, q * P:(q + 1) * P], od1[i][:, q, :], t_o,
                       *(bfree[b] if q == 0 else []), count=q == 3)
            t1 = act(AH[:, 4 + i, :], bank[b][:, :], ACT.Copy, t, *a_free[4 + i])
            t2 = tt(AL[:, 4 + i, :], bank[b][:, :], AH[:, 4 + i, :].bitcast(F), ALU.subtract, t1)
            bfree[b] = [t2]
            o_tok[4 + i] = [t1, t2]
        fence = [t_o, t2, t]
        mla.close()
        ph1.close()

        def project_residual(name, act_tok, gcol, evac=None, finish=True):
            nxt, tk = [None] * 8, None
            for i in range(4):
                u, wh, wl, wt = take(name, i)
                whv, wlv = wh.rearrange("p (k n) -> p k n", k=8), wl.rearrange("p (k n) -> p k n", k=8)
                for c in range(2):
                    m = 2 * i + c
                    b = mbank()
                    t = prod_t(b, whv, wlv, slice(c * P, c * P + P), range(8), AH, AL, range(8),
                               [wt + act_tok[k] for k in range(8)])
                    x_t[m] = tt(X[:, m, :], X[:, m, :], bank[b][:, :], ALU.add, t, *x_t_w(m))
                    bfree[b] = [x_t[m]]
                pe_done[u] = t
            return t

        x_t = [None] * 8
        x_read = [[] for _ in range(8)]

        def x_t_w(m):
            return [x_t[m], *x_read[m]]

        def next_norm(gcol, a_done):
            toks, tk = [None] * 8, None
            for c in range(8):
                a_free[c] = [a_done]
                tk, toks[c] = norm_in(gcol, c, [x_t[c], t_x])
                x_read[c] = [tk, toks[c][1]]
            return norm_r(tk), toks

        a_free = [[] for _ in range(8)]
        tp = project_residual("wout", o_tok, None)
        t_r4, xk = next_norm(PC_MLP, tp)

        hid = ExitStack()
        ctx.enter_context(hid)
        NH = 10
        HH = [sb(f"HH{i}", [P, S], R, hid) for i in range(NH)]
        HL = [sb(f"HL{i}", [P, S], R, hid) for i in range(NH)]
        hfree = [list(fence) for _ in range(NH)]
        t1s = [sb(f"t1s{i}", [P, S + 2], F, hid) for i in range(2)]
        t1f, t2f = [list(fence), list(fence)], [list(fence), list(fence)]
        h_t = {}

        def up(i):
            nonlocal t_rb
            u, wh, wl, wt = take("up", i)
            whv, wlv = wh.rearrange("p (k n) -> p k n", k=8), wl.rearrange("p (k n) -> p k n", k=8)
            for c in range(2):
                m = 2 * i + c
                b = mbank()
                t = prod_t(b, whv, wlv, slice(c * P, c * P + P), range(8), AH, AL, range(8),
                           [wt + xk[k] for k in range(8)])
                if m == 0:
                    t_rb = norm_spread(t_r4)
                k, s = m % 2, m % NH
                t1 = stt(t1s[k][:, 0:S], bank[b][:, :], 0.0, rb[:, :], ALU.max, ALU.mult, t, t_rb, *t1f[k])
                bfree[b] = [t1]
                t2 = act(t2s[k][:, :], t1s[k][:, 0:S], ACT.Square, t1, *t2f[k])
                t1f[k] = [t2]
                t3 = act(HH[s][:, :], t2s[k][:, :], ACT.Copy, t2, *hfree[s])
                t4 = tt(HL[s][:, :], t2s[k][:, :], HH[s][:, :].bitcast(F), ALU.subtract, t3)
                t2f[k] = [t4]
                h_t[m] = [t3, t4]
            pe_done[u] = t
            return t, t1

        def down(name, g, base, kc):
            for i in range(4):
                u, wh, wl, wt = take(name, 4 * g + i)
                whv, wlv = wh.rearrange("p (k n) -> p k n", k=kc), wl.rearrange("p (k n) -> p k n", k=kc)
                for c in range(2):
                    m = 2 * i + c
                    b = mbank()
                    for k in range(kc):
                        s = (base + k) % NH
                        a = whv[:, k, c * P:(c + 1) * P]
                        mm(bank[b][:, :], a, HH[s][:, :], k == 0, False, *wt, *h_t[base + k],
                           *(bfree[b] if k == 0 else []))
                        mm(bank[b][:, :], a, HL[s][:, :], False, False)
                        t = mm(bank[b][:, :], wlv[:, k, c * P:(c + 1) * P], HH[s][:, :], False, k == kc - 1,
                               count=k == kc - 1)
                    x_t[m] = tt(X[:, m, :], X[:, m, :], bank[b][:, :], ALU.add, t, *x_t_w(m))
                    bfree[b] = [x_t[m]]
                pe_done[u] = t
            for k in range(kc):
                hfree[(base + k) % NH] = [t]
            return t

        up_last = None
        for g in range(5):
            if g < 4:
                up_last = up(4 * g)
            if g > 0:
                down("down", g - 1, 8 * (g - 1), 8)
            if g < 4:
                for i in range(1, 4):
                    up_last = up(4 * g + i)
        rb_free[0] = [up_last[1]]
        t_r4, xk = next_norm(PC_PLE, up_last[0])

        ple = ExitStack()
        ctx.enter_context(ple)
        pe_x = sb("pe_x", [P, 2, S], F, ple)
        pH = sb("pH", [P, 2, S], R, ple)
        pL = sb("pL", [P, 2, S], R, ple)
        pj = sb("pj", [P, 8, S], F, ple)
        s_pe = newsem()
        t_pe = pr.dma("gpsimd", pe_x[:, :, :], PT, s_pe, 16, fence)
        t1 = act(pH[:, :, :], pe_x[:, :, :], ACT.Copy, t_pe, *fence)
        t2 = tt(pL[:, :, :], pe_x[:, :, :], pH[:, :, :].bitcast(F), ALU.subtract, t1, *fence)
        u, wh, wl, wt = take("proj", 0)
        whv, wlv = wh.rearrange("p (k n) -> p k n", k=2), wl.rearrange("p (k n) -> p k n", k=2)
        t_pj = [None] * 8
        for m in range(8):
            b = mbank()
            t = prod_t(b, whv, wlv, slice(m * P, m * P + P), range(2), pH, pL, range(2), [wt + [t1, t2]] * 2)
            if m == 0:
                t_rb = norm_spread(t_r4)
            t_pj[m] = act(pj[:, m, :], bank[b][:, :], ACT.Copy, t, *fence)
            bfree[b] = [t_pj[m]]
        pe_done[u] = t
        for i in range(4):
            u, wh, wl, wt = take("pg", i)
            whv, wlv = wh.rearrange("p (k n) -> p k n", k=8), wl.rearrange("p (k n) -> p k n", k=8)
            for c in range(2):
                m = 2 * i + c
                k = m % 2
                b = mbank()
                t = prod_t(b, whv, wlv, slice(c * P, c * P + P), range(8), AH, AL, range(8),
                           [wt + xk[j] for j in range(8)])
                t1 = tt(t2s[k][:, :], bank[b][:, :], rb[:, :], ALU.mult, t, t_rb, *t2f[k])
                bfree[b] = [t1]
                t2 = act(t2s[k][:, :], t2s[k][:, :], ACT.Sigmoid, t1, t_p, bias=par[:, PC_BPLE + m:PC_BPLE + m + 1])
                t3 = tt(t2s[k][:, :], t2s[k][:, :], pj[:, m, :], ALU.mult, t2, t_pj[m])
                x_t[m] = tt(X[:, m, :], X[:, m, :], t2s[k][:, :], ALU.add, t3, *x_t_w(m))
                t2f[k] = [x_t[m]]
            pe_done[u] = t
        rb_free[0] = [t1]
        a_done = t
        fence = [t, x_t[7]]
        ple.close()

        tk = None
        for c in range(8):
            tk = square_small(X[:, c, :], c, 8, SB_, 0, c == 0, x_t[c])
        t_r4 = norm_r(tk)
        t_rb = norm_spread(t_r4)
        pool = ExitStack()
        ctx.enter_context(pool)
        hp = [sb(f"hp{i}", [P, S + 16], F, pool) for i in range(2)]
        sa = [sb(f"sa{i}", [P, S + 16], F, pool) for i in range(2)]
        sb2 = [sb(f"sb2{i}", [P, S + 16], F, pool) for i in range(2)]
        tz = None
        for z in (*hp, *sa, *sb2):
            tz = G(lambda e, z=z: e.memset(z[:, 0:16], 0.0), *fence)
        hpf = [[tz], [tz]]
        xk = [None] * 8
        for c in range(8):
            k, w = c % 2, WINDOWS[c // 2]
            t0 = stt(hp[k][:, 16:], X[:, c, :], par[:, PC_MIX + c:PC_MIX + c + 1], rb[:, :], ALU.mult, ALU.mult,
                     x_t[c], t_rb, *hpf[k])
            src, t, step = hp[k], t0, 1
            for dst in (sa[k], sb2[k], sa[k], sb2[k]):
                if step >= w:
                    break
                t = tt(dst[:, 16:], src[:, 16:], src[:, 16 - step:16 - step + S], ALU.add, t)
                src = dst
                step *= 2
            cnt = cst[:, C_CNT + 16 * (c // 2):C_CNT + 16 * (c // 2) + 16]
            ta = tt(src[:, 16:32], src[:, 16:32], cnt, ALU.mult, t)
            tb = ts(src[:, 32:], src[:, 32:], 1.0 / w, ALU.mult, t)
            t = tt(src[:, 16:], src[:, 16:], hp[k][:, 16:], ALU.subtract, ta, tb)
            t3 = act(AH[:, c, :], src[:, 16:], ACT.Copy, t, a_done)
            t4 = tt(AL[:, c, :], src[:, 16:], AH[:, c, :].bitcast(F), ALU.subtract, t3, a_done)
            hpf[k] = [t4]
            xk[c] = [t3, t4]
            x_read[c] = [tk, t0]
        rb_free[0] = [t0]
        u, wh, wl, wt = take("pool", 0)
        whv, wlv = wh.rearrange("p (k n) -> p k n", k=8), wl.rearrange("p (k n) -> p k n", k=8)
        for m in range(8):
            g = m // 2
            b = mbank()
            t = prod_t(b, whv, wlv, slice((m % 2) * P, (m % 2) * P + P), [2 * g, 2 * g + 1], AH, AL,
                       [2 * g, 2 * g + 1], [wt + xk[2 * g], xk[2 * g + 1]])
            k = m % 2
            t1 = ts(t2s[k][:, :], bank[b][:, :], par[:, PC_PB + m:PC_PB + m + 1], ALU.add, t, *t2f[k],
                    s2=par[:, PC_PS + m:PC_PS + m + 1], op1=ALU.mult)
            bfree[b] = [t1]
            x_t[m] = tt(X[:, m, :], X[:, m, :], t2s[k][:, :], ALU.add, t1, *x_t_w(m))
            t2f[k] = [x_t[m]]
        pe_done[u] = t
        fence = [t, x_t[7], t4]
        pool.close()
        t_r4, xk = next_norm(PC_FFN, t)

        cvs = [sb(f"cvs{i}", [P, S], F, hid) for i in range(2)]
        cvf = [[], []]
        tz1 = None
        for z in t1s:
            tz1 = G(lambda e, z=z: e.memset(z[:, 0:2], 0.0), *t1f[0], *t1f[1])
        t1f = [[tz1], [tz1]]

        def ffn(l, fence):
            nonlocal t_rb
            for s in range(NH):
                hfree[s] = hfree[s] + list(fence)
            gp = {}
            pairs = [[4 * g + i for i in range((b - a) // 2)] for g, (a, b) in enumerate(GROUPS2)]

            def pair(j):
                nonlocal t_rb
                us = []
                banks = {}
                for name in ("gate", "val"):
                    u, wh, wl, wt = take(f"{name}{l}", j)
                    whv, wlv = wh.rearrange("p (k n) -> p k n", k=8), wl.rearrange("p (k n) -> p k n", k=8)
                    for c in range(2):
                        b = mbank()
                        t = prod_t(b, whv, wlv, slice(c * P, c * P + P), range(8), AH, AL, range(8),
                                   [wt + xk[k] for k in range(8)])
                        if j == 0 and name == "gate" and c == 0:
                            t_rb = norm_spread(t_r4)
                        m = 2 * j + c
                        k, s = c, m % NH
                        if name == "gate":
                            a = t1s[k]
                            cw_ = [par[:, PC_CW + 66 * l + 22 * i + m:PC_CW + 66 * l + 22 * i + m + 1] for i in range(3)]
                            cb_ = par[:, PC_CB + 22 * l + m:PC_CB + 22 * l + m + 1]
                            t1 = tt(a[:, 2:], bank[b][:, :], rb[:, :], ALU.mult, t, t_rb, *t1f[k])
                            bfree[b] = [t1]
                            t2 = ts(t2s[k][:, :], a[:, 0:S], cw_[0], ALU.mult, t1, *t2f[k])
                            t3 = stt(t2s[k][:, :], a[:, 1:S + 1], cw_[1], t2s[k][:, :], ALU.mult, ALU.add, t2)
                            t4 = stt(t2s[k][:, :], a[:, 2:S + 2], cw_[2], t2s[k][:, :], ALU.mult, ALU.add, t3)
                            t1f[k] = [t4]
                            gp[m] = act(t2s[k][:, :], t2s[k][:, :], ACT.Silu, t4, bias=cb_)
                        else:
                            t1 = tt(cvs[k][:, :], bank[b][:, :], rb[:, :], ALU.mult, t, *cvf[k])
                            bfree[b] = [t1]
                            t2 = tt(cvs[k][:, :], cvs[k][:, :], t2s[k][:, :], ALU.mult, t1, gp[m])
                            t2f[k] = [t2]
                            t3 = act(HH[s][:, :], cvs[k][:, :], ACT.Copy, t2, *hfree[s])
                            t4 = tt(HL[s][:, :], cvs[k][:, :], HH[s][:, :].bitcast(F), ALU.subtract, t3)
                            cvf[k] = [t4]
                            h_t[m] = [t3, t4]
                    pe_done[u] = t
                return t, t1

            for g in range(4):
                if g < 3:
                    last = pair(pairs[g][0])
                if g > 0:
                    a, b = GROUPS2[g - 1]
                    t = down(f"fo{l}", g - 1, a, b - a)
                if g < 3:
                    for j in pairs[g][1:]:
                        last = pair(j)
            rb_free[0] = [last[1]]
            return last[0], t

        a_done, t_dn = ffn(0, fence)
        t_r4, xk = next_norm(PC_MIX + 8, a_done)
        fence = [t_dn, x_t[7]]
        hid.close()

        at2 = ExitStack()
        ctx.enter_context(at2)
        v2 = sb("v2", [P, 4, D], F, at2)
        qT2 = [sb(f"qT2{i}", [P, S], F, at2) for i in range(8)]
        kT2 = [sb(f"kT2{i}", [P, S], F, at2) for i in range(8)]
        qn = [sb(f"qn{i}", [P, 512], F, at2) for i in range(2)]
        qs_ = sb("qs_", [P, 512], F, at2)
        rn2 = sb("rn2", [P, 2, 8], F, at2)
        mn2 = sb("mn2", [P, 2, 8], F, at2)
        NG = 2
        Gb = [sb(f"Gb{i}", [P, 512], F, at2) for i in range(NG)]
        rel = sb("rel", [16, 513], F, at2)
        ev = sb("ev", [16, 640], F, at2)
        EV = nc.dram_tensor("ev_scratch", (16, P, 640), F, kind="Internal")
        s_rel, s_ev, s_gb = newsem(), newsem(), [newsem() for _ in range(NG)]
        t_rel = pr.dma("gpsimd", rel[:, :], REL, s_rel, 16, fence)
        t1 = ts(ev[:, 0:255], rel[:, 0:1].to_broadcast([16, 255]), 8.0, ALU.mult, t_rel, *fence)
        t2 = ts(ev[:, 255:640], rel[:, 0:385], 8.0, ALU.mult, t_rel)
        t_ev = pr.dma("gpsimd", EV.ap(), ev[:, None, :].to_broadcast([16, P, 640]), s_ev, 16, [t1, t2])
        tms = None
        for i in range(NG):
            tms = G(lambda e, i=i: e.memset(Gb[i][0:64, 448:512], -1e30), *fence)
        qnf = [list(fence), list(fence)]
        rnf = [[], []]
        qk2 = {}
        tqs = list(fence)
        t_v2 = []
        cnt_b = 0
        for blk in range(6):
            bs = [mbank() for _ in range(NT)]
            for hlf in range(2):
                u, wh, wl, wt = take("qkv", 2 * blk + hlf)
                whv, wlv = wh.rearrange("p (k n) -> p k n", k=4), wl.rearrange("p (k n) -> p k n", k=4)
                for q in range(NT):
                    for k in range(4):
                        kk = 4 * hlf + k
                        o = bank[bs[q]][:, :]
                        st = hlf == 0 and k == 0
                        ah, al = AH[:, kk, q * P:(q + 1) * P], AL[:, kk, q * P:(q + 1) * P]
                        mm(o, ah, whv[:, k, :], st, False, *wt, *xk[kk], *(bfree[bs[q]] if st else []))
                        mm(o, ah, wlv[:, k, :], False, False)
                        t = mm(o, al, whv[:, k, :], False, k == 3 and hlf == 1, count=k == 3)
                    if hlf == 0:
                        continue
                    if blk >= 4:
                        tv = act(v2[:, q, (blk - 4) * 512:(blk - 3) * 512], bank[bs[q]][:, :], ACT.Copy, t, t_r4, *fence,
                                 scale=r4[:, q:q + 1])
                        bfree[bs[q]] = [tv]
                        t_v2.append(tv)
                        continue
                    z = qn[cnt_b % 2]
                    kx = cnt_b % 2
                    cnt_b += 1
                    t1 = ts(z[:, :], bank[bs[q]][:, :], r4[:, q:q + 1], ALU.mult, t, t_r4, *qnf[kx])
                    bfree[bs[q]] = [t1]
                    t2 = act(qs_[:, :], z[:, :], ACT.Square, t1, *tqs)
                    t3 = V(lambda e, kx=kx: e.tensor_reduce(mn2[:, kx, :], qs_[:, :].rearrange("p (h d) -> p h d", d=64),
                                                            AX.X, ALU.add), t2, *rnf[kx])
                    tqs = [t3]
                    t4 = ts(mn2[:, kx, :], mn2[:, kx, :], 1.0 / 64, ALU.mult, t3, s2=EPS, op1=ALU.add)
                    t5 = G(lambda e, kx=kx: e.tensor_tensor(rn2[:, kx, :], mn2[:, kx, :], cst[:, C_HALF:C_HALF + 8], ALU.pow),
                           t4, t_c)
                    z3 = z[:, :].rearrange("p (h d) -> p h d", d=64)
                    t6 = tt(z3, z3, rn2[:, kx, :, None].to_broadcast([P, 8, 64]), ALU.mult, t5)
                    rnf[kx] = [t6]
                    g0 = 2 * MQ + (0 if blk < 2 else HD2)
                    t7 = tt(z3, z3, row[:, None, g0:g0 + HD2].to_broadcast([P, 8, 64]), ALU.mult, t6, t_row)
                    dstT = qT2 if blk < 2 else kT2
                    bb = 4 + kx
                    for i in range(4):
                        tt_ = tr(bank[bb][:, i * P:(i + 1) * P], z[:, i * P:(i + 1) * P], t7, *(bfree[bb] if i == 0 else []),
                                 count=i == 3)
                    qnf[kx] = [tt_]
                    for i in range(4):
                        d = dstT[4 * (blk % 2) + i]
                        tc = act(d[:, q * P:(q + 1) * P], bank[bb][:, i * P:(i + 1) * P], ACT.Copy, tt_, *fence)
                    bfree[bb] = [tc]
                    qk2[(blk, q)] = tc
                pe_done[u] = t
        a_done = t
        fence2 = [t]
        tqk_all = [qk2[k] for k in qk2]
        gb_t, gb_free = {}, [[tms], [tms]]

        def loadG(h):
            i = h % NG
            w = [t_ev, *gb_free[i]]
            src = EV.ap()

            def toe(r0, rows, cols):
                return bass.AP(EV, (h * P + r0) * 640 + 127 - r0, [[639, rows], [1, cols]])
            pr.dma("gpsimd", Gb[i][0:64, 0:448], toe(0, 64, 448), s_gb[i], 0, w)
            gb_t[h] = [pr.dma("gpsimd", Gb[i][64:128, :], toe(64, 64, 512), s_gb[i], 32 * (h // NG + 1), w)]

        def bias2(h):
            def done(t):
                gb_free[h % NG] = [t]
            return Gb[h % NG], gb_t[h], done

        loaded = set()

        def fetch2(h, q):
            if q == 0:
                for x in (h, h + 1):
                    if x < H2 and x not in loaded and (x < NG or x - NG < h):
                        loaded.add(x)
                        loadG(x)
            return tqk_all

        oex = sb("oex", [P, 512], F, at2)
        od2 = [z[:, :].rearrange("p (q d) -> p q d", q=4) for z in [oex] + qT2[0:7]]
        t_o = attention(H2, HD2, lambda h: qT2[h // 2], lambda h: kT2[h // 2], lambda h: slice(64 * (h % 2), 64 * (h % 2) + 64),
                        fetch2, v2, t_v2, 0.125, bias2, lambda h, q, t: None, od2, at2)
        for i in range(8):
            b = mbank()
            for q in range(NT):
                t = tr(bank[b][:, q * P:(q + 1) * P], od2[i][:, q, :], t_o,
                       *(bfree[b] if q == 0 else []), count=q == 3)
            t1 = act(AH[:, i, :], bank[b][:, :], ACT.Copy, t, a_done)
            t2 = tt(AL[:, i, :], bank[b][:, :], AH[:, i, :].bitcast(F), ALU.subtract, t1, a_done)
            bfree[b] = [t2]
            o_tok[i] = [t1, t2]
        fence = [t, t1, t2, t_o, gb_t[15][0], gb_t[14][0]]
        at2.close()
        tp = project_residual("wo", o_tok, None)
        t_r4, xk = next_norm(PC_FFN + 8, tp)

        hid = ExitStack()
        ctx.enter_context(hid)
        HH = [sb(f"HI{i}", [P, S], R, hid) for i in range(NH)]
        HL = [sb(f"HM{i}", [P, S], R, hid) for i in range(NH)]
        cvs = [sb(f"cvt{i}", [P, S], F, hid) for i in range(2)]
        t1s = [sb(f"t1t{i}", [P, S + 2], F, hid) for i in range(2)]
        for z in t1s:
            tz1 = G(lambda e, z=z: e.memset(z[:, 0:2], 0.0), *fence)
        t1f = [[tz1], [tz1]]
        cvf = [list(fence), list(fence)]
        hfree = [[] for _ in range(NH)]
        t2f = [list(fence), list(fence)]
        ffn(1, fence)

        s_o = newsem()
        for m in range(8):
            t_out = pr.dma("sync", OUT[:, m, :], X[:, m, :], s_o, 16 * 8, [x_t[m]])
        assert cur[0] == len(plan)

        block = ctx.enter_context(nc.Block())

        @block.sync
        def _(e):
            pr.play("sync", e)
            e.wait_ge(s_o, 16 * 8)

        @block.tensor
        def _(e):
            pr.play("tensor", e)

        @block.vector
        def _(e):
            pr.play("vector", e)

        @block.scalar
        def _(e):
            pr.play("scalar", e)

        @block.gpsimd
        def _(e):
            pr.play("gpsimd", e)


def constants():
    c = np.zeros((P, NCC), np.float32)
    c[:, C_ID:C_ID + P] = np.eye(P)
    c[:, C_ONE:C_ONE + P] = 1.0
    c[:, C_HALF:C_HALF + P] = -0.5
    c[:, C_SCAN:C_SCAN + S] = (np.arange(S) % 64 != 0)
    c[0, C_MA:C_MA + 64] = -1e30
    c[0, C_MB + 64:C_MB + P] = 1.0
    c[:, C_IF:C_IF + 16] = np.float32(10000.0) ** (-np.arange(0, 32, 2, dtype=np.float32) / np.float32(32))
    for g, w in enumerate(WINDOWS):
        c[:, C_CNT + 16 * g:C_CNT + 16 * g + 16] = 1.0 / np.minimum(np.arange(16) + 1, w)
    s, t = np.meshgrid(np.arange(P), np.arange(P), indexing="ij")
    m = np.zeros((P, 7, P), np.int32)
    m[:, 0, :] = s == t
    for i, b in enumerate(LEVELS):
        m[:, i + 1, :] = (s // (2 * b) == t // (2 * b)) & (s % (2 * b) < b) & (t % (2 * b) >= b)
    return c, m


def kernel(**x):
    import concourse.bacc as bacc
    from concourse.bass_utils import run_bass_kernel_spmd as run

    x = {k: np.asarray(v) for k, v in x.items()}
    f4 = np.float32

    def cols(w, a, b):
        k = w.shape[0] // P
        return w[:, a:b].reshape(k, P, b - a).transpose(1, 0, 2).reshape(P, -1)

    w_in = x["w_in"][0]
    ukv = x["mla_w_ukv"][0].reshape(128, MH, 128)
    units = {
        "small": lambda i: cols(np.concatenate([w_in[:, 1024:1040], w_in[:, 1936:1968]], 1), 0, 48),
        "cq": lambda i: cols(w_in, 1552, 1808),
        "ckv": lambda i: cols(w_in, 1808, 1936),
        "gq": lambda i: cols(w_in, 0, 256),
        "gk": lambda i: cols(w_in, 256, 512),
        "gv": lambda i: cols(w_in[512 * i:512 * i + 512], 512, 1024),
        "gr": lambda i: cols(w_in, 1040 + 256 * i, 1296 + 256 * i),
        "uq": lambda i: cols(x["mla_w_uq"][0], 0, 768),
        "ukv": lambda i: np.concatenate([ukv[:, :, 0:64].reshape(128, 512), ukv[:, :, 64:].reshape(128, 512)], 1),
        "wout": lambda i: cols(x["w_out"][0], 256 * i, 256 * i + 256),
        "up": lambda i: cols(x["w_mlp_up"][0], 256 * i, 256 * i + 256),
        "down": lambda i: cols(x["w_mlp_down"][0][1024 * (i // 4):1024 * (i // 4) + 1024], 256 * (i % 4), 256 * (i % 4) + 256),
        "proj": lambda i: cols(x["w_ple_proj"][0], 0, 1024),
        "pg": lambda i: cols(x["w_ple_gate"][0], 256 * i, 256 * i + 256),
        "pool": lambda i: cols(x["pool_w_2"][0].reshape(1024, 256), 0, 256),
        "qkv": lambda i: cols(x["attn_wqkv_2"][0][512 * (i % 2):512 * (i % 2) + 512], 512 * (i // 2), 512 * (i // 2) + 512),
        "wo": lambda i: cols(x["attn_wo_2"][0], 256 * i, 256 * i + 256),
    }
    for l in range(2):
        units[f"gate{l}"] = lambda i, l=l: cols(x["ffn_w_gate_2"][l], 256 * i, 256 * i + 256)
        units[f"val{l}"] = lambda i, l=l: cols(x["ffn_w_val_2"][l], 256 * i, 256 * i + 256)
        units[f"fo{l}"] = lambda i, l=l: cols(x["ffn_w_out_2"][l][P * GROUPS2[i // 4][0]:P * GROUPS2[i // 4][1]],
                                              256 * (i % 4), 256 * (i % 4) + 256)
    plan = unit_plan()
    W = np.zeros((len(plan), P, UE), f4)
    for u, (name, i, n) in enumerate(plan):
        W[u, :, 0:n] = units[name](i)
    vecs = [x["attn_norm"], x["mlp_norm"], x["ple_norm"], x["b_ple_gate"], x["mix_norm_2"], x["ffn_norm_2"],
            x["pool_b_2"], x["pool_scale_2"], x["ffn_conv_w_2"], x["ffn_conv_b_2"], x["gla_gate_b"],
            x["gla_out_norm"], x["mla_q_norm"], x["mla_kv_norm"]]
    PV = np.ascontiguousarray(np.concatenate([v.reshape(-1, P) for v in vecs], 0).T)
    ROW = np.concatenate([x["qk_norm_q"][0], x["qk_norm_k"][0], x["attn_q_norm_2"][0], x["attn_k_norm_2"][0]])[None]
    CST, MSK = constants()
    arrays = {
        "W": W,
        "XT": np.ascontiguousarray(x["x"][0].T.reshape(8, P, S).transpose(1, 0, 2)),
        "PT": np.ascontiguousarray(x["p"][0, 0].T.reshape(2, P, S).transpose(1, 0, 2)),
        "PV": PV,
        "ROW": np.ascontiguousarray(ROW),
        "GW2": np.ascontiguousarray(x["gla_gate_w2"][0]),
        "POS": np.ascontiguousarray(x["positions"][0].reshape(4, P).T),
        "REL": np.ascontiguousarray(x["attn_rel_bias_2"][0][:, ::-1]),
        "CST": CST,
        "MSK": MSK,
    }
    nc = bacc.Bacc("TRN2", target_bir_lowering=False, num_devices=1)
    aps = [nc.dram_tensor(f"in_{k}", a.shape, mybir.dt.from_np(a.dtype), kind="ExternalInput").ap() for k, a in arrays.items()]
    out = nc.dram_tensor("out_0", (P, 8, S), F, kind="ExternalOutput").ap()
    build(nc, *aps, out)
    r = run(nc, [{f"in_{k}": a for k, a in arrays.items()}], core_ids=[0])
    o = r.results[0]["out_0"]
    return np.ascontiguousarray(o.transpose(1, 0, 2).reshape(D, S).T)[None]
```

```python
import math
from contextlib import ExitStack

import numpy as np
import concourse.bass as bass
from concourse import mybir

F = mybir.dt.float32
R = mybir.dt.float32r
I32 = mybir.dt.int32
ALU = mybir.AluOpType
ACT = mybir.ActivationFunctionType
AX = mybir.AxisListType

P = 128
S = 512
D = 1024
NT = 4
EPS = 1e-6
UE = 2048

GH, GK, GV = 4, 64, 128
MH, MN, MR, MV, MQ = 8, 64, 32, 64, 96
H2, HD2 = 16, 64
FF2 = 2816
NJ = FF2 // P
GROUPS2 = [(0, 8), (8, 16), (16, 22)]
LEVELS = [32, 16, 8, 4, 2, 1]
WINDOWS = (2, 4, 8, 16)

PC_ATT, PC_MLP, PC_PLE, PC_BPLE, PC_MIX, PC_FFN = 0, 8, 16, 24, 32, 48
PC_PB, PC_PS, PC_CW, PC_CB, PC_GB, PC_GN, PC_QN, PC_KVN = 64, 72, 80, 212, 256, 258, 259, 261
NPC = 262
C_ID, C_ONE, C_HALF, C_SCAN, C_MA, C_MB, C_IF, C_CNT = 0, 128, 256, 384, 896, 1024, 1152, 1168
NCC = 1168 + 64
ROWS = 2 * MQ + 2 * HD2

TWO_PI = 2.0 * math.pi


def cody_waite():
    parts, rest = [], TWO_PI
    for bits in (8, 8, 8):
        e = math.floor(math.log2(abs(rest)))
        q = 2.0 ** (e - bits + 1)
        parts.append(math.floor(rest / q) * q)
        rest -= parts[-1]
    return parts + [float(np.float32(rest))]


def unit_plan():
    plan = [("small", 0, 8 * 48), ("cq", 0, 2048), ("ckv", 0, 1024), ("gq", 0, 2048), ("gk", 0, 2048),
            ("gv", 0, 2048), ("gv", 1, 2048), ("gr", 0, 2048), ("gr", 1, 2048), ("uq", 0, 1536), ("ukv", 0, 1024)]
    plan += [("wout", i, 2048) for i in range(4)]
    for g in range(4):
        plan += [("up", 4 * g + i, 2048) for i in range(4)]
    order = plan[:-16]
    ups, k = plan[-16:], 0
    for g in range(5):
        if g < 4:
            order += ups[4 * g:4 * g + 1]
        if g > 0:
            order += [("down", 4 * (g - 1) + i, 2048) for i in range(4)]
        if g < 4:
            order += ups[4 * g + 1:4 * g + 4]
    order += [("proj", 0, 2048)] + [("pg", i, 2048) for i in range(4)] + [("pool", 0, 2048)]

    def ffn(l):
        out = []
        pairs = [[4 * g + i for i in range((b - a) // 2)] for g, (a, b) in enumerate(GROUPS2)]
        for g in range(4):
            if g < 3:
                out += [(f"gate{l}", pairs[g][0], 2048), (f"val{l}", pairs[g][0], 2048)]
            if g > 0:
                kc = GROUPS2[g - 1][1] - GROUPS2[g - 1][0]
                out += [(f"fo{l}", 4 * (g - 1) + i, kc * 256) for i in range(4)]
            if g < 3:
                for j in pairs[g][1:]:
                    out += [(f"gate{l}", j, 2048), (f"val{l}", j, 2048)]
        return out

    order += ffn(0)
    order += [("qkv", i, 2048) for i in range(12)]
    order += [("wo", i, 2048) for i in range(4)]
    order += ffn(1)
    return order


class Prog:

    def __init__(self, sems):
        self.q = {k: [] for k in ("tensor", "vector", "scalar", "gpsimd", "sync")}
        self.n = {k: 0 for k in self.q}
        self.sems = sems

    def __call__(self, eng, fn, waits=(), count=True):
        if count:
            self.n[eng] += 1
        self.q[eng].append((fn, [w for w in waits if w is not None], self.sems[eng] if count else None, 1))
        return (eng, self.n[eng]) if count else None

    def dma(self, eng, out, in_, sem, total, waits=()):
        self.q[eng].append((lambda e: e.dma_start(out, in_), [w for w in waits if w is not None], sem, 16))
        return (sem, total)

    def play(self, eng, e):
        seen = {}
        for fn, waits, sem, by in self.q[eng]:
            for w, n in waits:
                s = self.sems[w] if isinstance(w, str) else w
                if seen.get(id(s), 0) < n:
                    e.wait_ge(s, n)
                    seen[id(s)] = n
            ins = fn(e)
            if sem is not None:
                ins.then_inc(sem, by)


def build(nc, W, XT, PT, PV, ROW, GW2, POS, REL, CST, MSK, OUT):
    plan = unit_plan()
    ctx = ExitStack()
    with ctx:
        sems = {k: ctx.enter_context(nc.semaphore(f"s_{k}")) for k in ("tensor", "vector", "scalar", "gpsimd", "sync")}
        pr = Prog(sems)
        nsem = [0]

        def newsem():
            nsem[0] += 1
            return ctx.enter_context(nc.semaphore(f"s_x{nsem[0]}"))

        def sb(name, shape, dt=F, at=None):
            return (at or ctx).enter_context(nc.sbuf_tensor(name, shape, dt))

        bank = [ctx.enter_context(nc.psum_tensor(f"bank{i}", [P, 512], F)) for i in range(8)]
        bfree = [[] for _ in range(8)]

        cst = sb("cst", [P, NCC])
        par = sb("par", [P, NPC])
        X = sb("X", [P, 8, S])
        AH = sb("AH", [P, 8, S], R)
        AL = sb("AL", [P, 8, S], R)
        NR, NW = 2, 3
        RAW = [sb(f"RAW{i}", [P, UE]) for i in range(NR)]
        WH = [sb(f"WH{i}", [P, UE], R) for i in range(NW)]
        WL = [sb(f"WL{i}", [P, UE], R) for i in range(NW)]
        rb = sb("rb", [P, S])
        sq = [sb(f"sq{i}", [P, S]) for i in range(2)]
        dg = sb("dg", [P, 4, P])
        t2s = [sb(f"t2s{i}", [P, S]) for i in range(2)]
        row = sb("row", [P, ROWS])
        r4 = sb("r4", [P, 4])
        m4 = sb("m4", [P, 4])
        ident = cst[:, C_ID:C_ID + P]
        ones = cst[:, C_ONE:C_ONE + P]

        def V(fn, *w):
            return pr("vector", fn, w)

        def A(fn, *w):
            return pr("scalar", fn, w)

        def G(fn, *w):
            return pr("gpsimd", fn, w)

        def T(fn, *w, count=False):
            return pr("tensor", fn, w, count)

        def tt(out, a, b, op, *w):
            return V(lambda e: e.tensor_tensor(out, a, b, op), *w)

        def ts(out, a, s1, op0, *w, s2=None, op1=None):
            if op1 is None:
                return V(lambda e: e.tensor_scalar(out, a, s1, None, op0), *w)
            return V(lambda e: e.tensor_scalar(out, a, s1, s2, op0, op1), *w)

        def stt(out, a, s, b, op0, op1, *w):
            return V(lambda e: e.scalar_tensor_tensor(out, a, s, b, op0, op1), *w)

        def act(out, a, f, *w, **k):
            return A(lambda e: e.activation(out, a, f, **k), *w)

        def mm(out, l, r, start, stop, *w, count=False, share=False):
            return T(lambda e: e.matmul(out, l, r, start=start, stop=stop, skip_group_check=share), *w, count=count)

        def tr(out, a, *w, count=False):
            k = a.shape[0]
            return T(lambda e: e.transpose(out, a, ident[0:k, 0:k]), *w, count=count)

        s_c, s_p, s_xl = newsem(), newsem(), newsem()
        t_x = pr.dma("sync", X[:, :, :], XT, s_xl, 16)
        t_p = pr.dma("sync", par[:, :], PV, s_p, 16)
        t_c = pr.dma("sync", cst[:, :], CST, s_c, 16)

        s_w = [newsem() for _ in range(NR)]
        raw_free = {}
        pe_done = {}
        hi_tok, lo_tok = {}, {}
        w_tok = {}

        def load(u):
            w = raw_free.get(u - NR, [])
            n = plan[u][2]
            w_tok[u] = pr.dma("sync", RAW[u % NR][:, 0:n], W[u, :, 0:n], s_w[u % NR], 16 * (u // NR + 1), w)

        def split(u):
            if u >= len(plan):
                return
            n, i, j = plan[u][2], u % NR, u % NW
            free = pe_done.get(u - NW)
            hi_tok[u] = act(WH[j][:, 0:n], RAW[i][:, 0:n], ACT.Copy, w_tok[u], free)
            lo_tok[u] = tt(WL[j][:, 0:n], RAW[i][:, 0:n], WH[j][:, 0:n].bitcast(F), ALU.subtract, hi_tok[u], free)
            raw_free[u] = [hi_tok[u], lo_tok[u]]
            if u + NR < len(plan):
                load(u + NR)

        for u in range(NR):
            load(u)
        cur = [0]

        def take(name, idx):
            u = cur[0]
            assert plan[u][:2] == (name, idx), (u, plan[u], name, idx)
            cur[0] += 1
            split(u + 2)
            j, n = u % NW, plan[u][2]
            return u, WH[j][:, 0:n], WL[j][:, 0:n], [hi_tok[u], lo_tok[u]]

        main = [0]

        def mbank():
            b = main[0] % 4
            main[0] += 1
            return b

        def prod_t(b, wh, wl, cols, kcs, ah, al, rows, waits, last=None, first=True, m=P):
            tok = None
            n = len(kcs)
            for i, (k, r) in enumerate(zip(kcs, rows)):
                w = list(waits[i]) if waits else []
                if i == 0 and first:
                    w += bfree[b]
                a, c = wh[:, k, cols], wl[:, k, cols]
                st = first and i == 0
                en = i == n - 1
                mm(bank[b][0:m, :], a, ah[:, r, :], st, False, *w)
                mm(bank[b][0:m, :], a, al[:, r, :], False, False)
                tok = mm(bank[b][0:m, :], c, ah[:, r, :], False, en, count=en)
            return tok

        split(0)
        split(1)

        sqr = [[], []]

        def square_small(src, c, n, b, col, start, *w):
            k = c % 2
            t = act(sq[k][:, :], src, ACT.Square, *w, *sqr[k])
            tok = None
            for q in range(NT):
                tok = mm(bank[b][:, col + q:col + q + 1], sq[k][:, q * P:(q + 1) * P], ones[:, 0:1],
                         start and q == 0, c == n - 1, t, t_c, *(bfree[b] if start and q == 0 else []),
                         count=q == NT - 1, share=True)
            sqr[k] = [tok]
            return tok

        def rpow(out, src, tmp, scale, *w):
            t1 = ts(tmp, src, scale, ALU.mult, *w, s2=EPS, op1=ALU.add)
            n = out.shape[1]
            return t1, G(lambda e: e.tensor_tensor(out, tmp, cst[:, C_HALF:C_HALF + n], ALU.pow), t1, t_c)

        spread_free = [[], []]

        def spread(r, b, w, dst=None):
            t = tt(dg[:, :, :], ident[:, None, :].to_broadcast([P, 4, P]), r[:, :, None].to_broadcast([P, 4, P]),
                   ALU.mult, *w, *spread_free[0], t_c)
            t2 = mm(bank[b][:, :], ones, dg[:, :, :].rearrange("p q n -> p (q n)"), True, True, t, *bfree[b], count=True)
            spread_free[0] = [t2]
            if dst is None:
                return t2
            t3 = act(dst, bank[b][:, :], ACT.Copy, t2, *spread_free[1])
            bfree[b] = [t3]
            return t3

        a_free = [[] for _ in range(8)]

        def prep(c, gcol, w):
            g = par[:, gcol + c:gcol + c + 1]
            t1 = ts(AH[:, c, :], X[:, c, :], g, ALU.mult, *w, *a_free[c], t_p)
            t2 = stt(AL[:, c, :], X[:, c, :], g, AH[:, c, :].bitcast(F), ALU.mult, ALU.subtract, t1)
            return [t1, t2]

        SB_ = 7

        acc = dg[:, :, :].rearrange("p q n -> p (q n)")
        acc_t = [None]

        def add_square(src, first, *w):
            if first:
                acc_t[0] = act(acc, src, ACT.Square, *w, *spread_free[0])
                return acc_t[0]
            k = sqn[0] % 2
            sqn[0] += 1
            t = act(sq[k][:, :], src, ACT.Square, *w, *sqr[k])
            acc_t[0] = tt(acc, acc, sq[k][:, :], ALU.add, t, acc_t[0])
            sqr[k] = [acc_t[0]]
            return t

        sqn = [0]

        rb_free = [[]]

        def norm_r():
            b = SB_
            for q in range(NT):
                t = mm(bank[b][:, q:q + 1], dg[:, q, :], ones[:, 0:1], True, True, acc_t[0], t_c,
                       *(bfree[b] if q == 0 else []), count=q == NT - 1, share=True)
            t1, t2 = rpow(r4[:, :], bank[b][:, 0:4], m4[:, :], 1.0 / D, t)
            bfree[b] = [t1]
            t_r[0] = t2

        def norm_spread():
            spread_free[1] = rb_free[0]
            t_r[1] = spread(r4, SB_, [t_r[0]], rb[:, :])

        t_r = [None, None]
        pend, stage = [], [2]

        def tile_done(fn):
            pend.append(fn)
            if stage[0] == 0:
                norm_r()
            elif stage[0] == 1:
                norm_spread()
            stage[0] += 1
            if stage[0] >= 2:
                for f in pend:
                    f()
                pend.clear()

        ph1 = ExitStack()
        ctx.enter_context(ph1)
        cqH = sb("cqH", [P, 3, S], R, ph1)
        cqL = sb("cqL", [P, 3, S], R, ph1)
        rq3 = sb("rq3", [P, 8], F, ph1)
        mq3 = sb("mq3", [P, 8], F, ph1)
        kr = sb("kr", [P, 4, 32], F, ph1)
        gla = ExitStack()
        ctx.enter_context(gla)
        msk = sb("msk", [P, 7, P], I32, gla)
        gw2 = sb("gw2", [16, 256], F, gla)
        s_m, s_g = newsem(), newsem()
        t_m = pr.dma("sync", msk[:, :, :], MSK, s_m, 16)
        t_g = pr.dma("sync", gw2[:, :], GW2, s_g, 16)
        gq = sb("gq", [P, 2, S], F, gla)
        gk = sb("gk", [P, 2, S], F, gla)
        gb = sb("gb", [P, 2, S], F, gla)
        gsil = sb("gsil", [P, 4, S], F, gla)
        gv = sb("gv", [P, 4, 512], F, gla)
        dd = sb("dd", [P, 2, S], F, gla)
        glow = dd[0:16, 0, :]

        xk = [None] * 8
        for c in range(8):
            add_square(X[:, c, :], c == 0, t_x)
            xk[c] = prep(c, PC_ATT, [t_x])

        u, wh, wl, wt = take("small", 0)
        whv, wlv = wh.rearrange("p (k n) -> p k n", k=8), wl.rearrange("p (k n) -> p k n", k=8)
        b0 = mbank()
        tg0 = prod_t(b0, whv, wlv, slice(0, 16), range(8), AH, AL, range(8), [wt + xk[i] for i in range(8)], m=16)
        b1 = mbank()
        for q in range(NT):
            for k in range(8):
                o = bank[b1][:, 32 * q:32 * q + 32]
                l = AH[:, k, q * P:(q + 1) * P]
                mm(o, l, whv[:, k, 16:48], q == 0 and k == 0, False, *bfree[b1], share=True)
                mm(o, l, wlv[:, k, 16:48], False, False, share=True)
                tkr = mm(o, AL[:, k, q * P:(q + 1) * P], whv[:, k, 16:48], False, k == 7, count=k == 7, share=True)
        pe_done[u] = tkr
        norm_r()
        norm_spread()
        t_r4, t_rb = t_r
        tgl = tt(glow, bank[b0][0:16, :], rb[0:16, :], ALU.mult, tg0, t_rb)
        bfree[b0] = [tgl]
        for q in range(NT):
            tkr = ts(kr[:, q, :], bank[b1][:, 32 * q:32 * q + 32], r4[:, q:q + 1], ALU.mult, tkr, t_r4)
        bfree[b1] = [tkr]
        t_kr = tkr

        ctmp = t2s
        cfree = [[], []]
        t_cq = [None] * 3
        tsq = [None] * 3
        for i in range(3):
            if i != 1:
                u, wh, wl, wt = take("cq" if i == 0 else "ckv", 0)
                nn = 256 if i == 0 else 128
                whv, wlv = wh.rearrange("p (k n) -> p k n", k=8), wl.rearrange("p (k n) -> p k n", k=8)
            b = mbank()
            col = (i % 2) * P
            t = prod_t(b, whv, wlv, slice(col, col + P), range(8), AH, AL, range(8), [wt] * 8)
            if i != 0:
                pe_done[u] = t
            k = i % 2
            t1 = tt(ctmp[k][:, :], bank[b][:, :], rb[:, :], ALU.mult, t, t_rb, *cfree[k])
            bfree[b] = [t1]
            tsq[i] = square_small(ctmp[k][:, :], i if i < 2 else 0, 2 if i < 2 else 1, SB_ - 1, 0 if i < 2 else 4, i == 0, t1)
            g = par[:, PC_QN + i:PC_QN + i + 1]
            t2 = ts(cqH[:, i, :], ctmp[k][:, :], g, ALU.mult, t1, t_p)
            t3 = stt(cqL[:, i, :], ctmp[k][:, :], g, cqH[:, i, :].bitcast(F), ALU.mult, ALU.subtract, t2)
            cfree[k] = [t3, tsq[i]]
            t_cq[i] = [t2, t3]
        t1 = ts(mq3[:, 0:4], bank[SB_ - 1][:, 0:4], 1.0 / 256, ALU.mult, tsq[2], s2=EPS, op1=ALU.add)
        t2 = ts(mq3[:, 4:8], bank[SB_ - 1][:, 4:8], 1.0 / 128, ALU.mult, tsq[2], s2=EPS, op1=ALU.add)
        bfree[SB_ - 1] = [t1, t2]
        t_rq3 = G(lambda e: e.tensor_tensor(rq3[:, :], mq3[:, :], cst[:, C_HALF:C_HALF + 8], ALU.pow), t1, t2, t_c)

        t_gq, t_gk = [None, None], [None, None]
        for name, dst, scale, toks in (("gq", gq, GK ** -0.5, t_gq), ("gk", gk, 1.0, t_gk)):
            u, wh, wl, wt = take(name, 0)
            whv, wlv = wh.rearrange("p (k n) -> p k n", k=8), wl.rearrange("p (k n) -> p k n", k=8)
            for i in range(2):
                b = mbank()
                t = prod_t(b, whv, wlv, slice(i * P, i * P + P), range(8), AH, AL, range(8), [wt] * 8)
                toks[i] = stt(dst[:, i, :], bank[b][:, :], scale, rb[:, :], ALU.mult, ALU.mult, t, t_rb)
                bfree[b] = [toks[i]]
            pe_done[u] = t
        t_b = [None, None]
        for j in range(2):
            b = 5
            t = mm(bank[b][:, :], gw2[:, j * P:(j + 1) * P], glow, True, True, tgl, t_g, *bfree[b], count=True)
            t1 = ts(ctmp[0][:, :], bank[b][:, :], par[:, PC_GB + j:PC_GB + j + 1], ALU.add, t, t_p, *cfree[0])
            bfree[b] = [t1]
            t2 = act(ctmp[1][:, :], ctmp[0][:, :], ACT.Abs, t1, *cfree[1])
            t3 = act(ctmp[1][:, :], ctmp[1][:, :], ACT.Exp, t2, scale=-1.0)
            t4 = act(ctmp[1][:, :], ctmp[1][:, :], ACT.Ln, t3, bias=1.0)
            t5 = stt(ctmp[0][:, :], ctmp[0][:, :], 0.0, ctmp[1][:, :], ALU.min, ALU.subtract, t4, t1)
            cfree[1] = [t5]
            oj = gb[:, j, :]
            t_b[j] = V(lambda e, oj=oj: e.tensor_tensor_scan(oj, cst[:, C_SCAN:C_SCAN + S], ctmp[0][:, :], 0.0,
                                                           ALU.mult, ALU.add), t5, t_c)
            cfree[0] = [t_b[j]]

        bs = [mbank() for _ in range(NT)]
        for hlf in range(2):
            u, wh, wl, wt = take("gv", hlf)
            whv, wlv = wh.rearrange("p (k n) -> p k n", k=4), wl.rearrange("p (k n) -> p k n", k=4)
            for q in range(NT):
                for k in range(4):
                    kk = 4 * hlf + k
                    o = bank[bs[q]][:, :]
                    st = hlf == 0 and k == 0
                    en = k == 3
                    ah, al = AH[:, kk, q * P:(q + 1) * P], AL[:, kk, q * P:(q + 1) * P]
                    mm(o, ah, whv[:, k, :], st, False, *wt, *(bfree[bs[q]] if st else []))
                    mm(o, ah, wlv[:, k, :], False, False)
                    t = mm(o, al, whv[:, k, :], False, en and hlf == 1, count=en)
                if hlf == 1:
                    t_gv = ts(gv[:, q, :], bank[bs[q]][:, :], r4[:, q:q + 1], ALU.mult, t, t_r4)
                    bfree[bs[q]] = [t_gv]
            pe_done[u] = t

        t_sil = [None] * 4
        for i in range(2):
            u, wh, wl, wt = take("gr", i)
            whv, wlv = wh.rearrange("p (k n) -> p k n", k=8), wl.rearrange("p (k n) -> p k n", k=8)
            for c in range(2):
                b = mbank()
                h = 2 * i + c
                t = prod_t(b, whv, wlv, slice(c * P, c * P + P), range(8), AH, AL, range(8), [wt] * 8)
                t1 = tt(gsil[:, h, :], bank[b][:, :], rb[:, :], ALU.mult, t, t_rb)
                bfree[b] = [t1]
                t_sil[h] = act(gsil[:, h, :], gsil[:, h, :], ACT.Silu, t1)
            pe_done[u] = t
        
        qt_ = sb("qt_", [P, 2, S], F, gla)
        kt_ = sb("kt_", [P, 2, S], F, gla)
        AT = sb("AT", [P, GH, S], F, gla)
        kd = sb("kd", [P, 4, 256], F, gla)
        ST = sb("ST", [P, 2, 7, P], F, gla)
        el = sb("el", [P, 2, 8], F, gla)
        t_at0 = G(lambda e: e.memset(AT[:, :, :], 0.0))
        f_qk = [[t_x], [t_x]]
        t_at = [t_at0] * GH
        sb4 = [0]
        for lv in range(7):
            for j in range(2):
                if lv == 0:
                    qs, ks, tq = gq, gk, [t_gq[j], t_gk[j]]
                else:
                    B = LEVELS[lv - 1]
                    bv = gb[:, j, :].rearrange("p (n w) -> p n w", w=2 * B)
                    dv = dd[:, j, :].rearrange("p (n w) -> p n w", w=2 * B)
                    n = S // (2 * B)
                    ref = bv[:, :, B - 1:B].to_broadcast([P, n, B])
                    t1 = tt(dv[:, :, B:2 * B], bv[:, :, B:2 * B], ref, ALU.subtract, t_b[j], *f_qk[j])
                    t2 = tt(dv[:, :, 0:B], ref, bv[:, :, 0:B], ALU.subtract, t_b[j])
                    t3 = act(dd[:, j, :], dd[:, j, :], ACT.Exp, t1, t2, scale=1.0 / 16)
                    t4 = tt(qt_[:, j, :], gq[:, j, :], dd[:, j, :], ALU.mult, t3, *f_qk[j])
                    t5 = tt(kt_[:, j, :], gk[:, j, :], dd[:, j, :], ALU.mult, t3, *f_qk[j])
                    qs, ks, tq = qt_, kt_, [t4, t5]
                for hh in range(2):
                    h = 2 * j + hh
                    b = 4 + sb4[0] % 3
                    sb4[0] += 1
                    rows = slice(64 * hh, 64 * hh + 64)
                    for q in range(NT):
                        cs = slice(q * P, (q + 1) * P)
                        t = mm(bank[b][:, cs], ks[rows, j, cs], qs[rows, j, cs], True, True, *tq,
                               *(bfree[b] if q == 0 else []), count=q == NT - 1, share=True)
                    m = msk[:, lv, None, :].to_broadcast([P, 4, P])
                    o = AT[:, h, :].rearrange("p (q n) -> p q n", q=4)
                    d = bank[b][:, :].rearrange("p (q n) -> p q n", q=4)
                    t_at[h] = V(lambda e, o=o, m=m, d=d: e.copy_predicated(o, m, d), t, t_at[h], t_m)
                    bfree[b] = [t_at[h]]
                if lv > 0:
                    f_qk[j] = [t, t5]
        t_kd, t_qe, t_el = [None] * 2, [None] * 2, [None] * 2
        for j in range(2):
            bv = gb[:, j, :].rearrange("p (n w) -> p n w", w=64)
            dv = dd[:, j, :].rearrange("p (n w) -> p n w", w=64)
            last = bv[:, :, 63:64]
            t_el[j] = act(el[:, j, :], last.rearrange("p n o -> p (n o)"), ACT.Exp, t_b[j], scale=1.0 / 16)
            t1 = tt(dv, last.to_broadcast([P, 8, 64]), bv, ALU.subtract, t_b[j], *f_qk[j])
            t2 = act(dd[:, j, :], dd[:, j, :], ACT.Exp, t1, scale=1.0 / 16)
            t3 = tt(kt_[:, j, :], gk[:, j, :], dd[:, j, :], ALU.mult, t2, *f_qk[j])
            t4 = act(dd[:, j, :], gb[:, j, :], ACT.Exp, t3, scale=1.0 / 16)
            t_qe[j] = tt(qt_[:, j, :], gq[:, j, :], dd[:, j, :], ALU.mult, t4, *f_qk[j])
            b = 4 + j
            for q in range(NT):
                t = tr(bank[b][:, q * P:(q + 1) * P], kt_[:, j, q * P:(q + 1) * P], t3, t_c,
                       *(bfree[b] if q == 0 else []), count=q == NT - 1)
            t_kd[j] = act(kd[:, :, j * P:(j + 1) * P], bank[b][:, :].rearrange("p (q n) -> p q n", q=4), ACT.Copy, t)
            bfree[b] = [t_kd[j]]
        t_st = [None, None]
        for j in range(2):
            tu = {}
            for c in [0, 2, 4, 6, 1, 3, 5]:
                b = 4 + 2 * j + c % 2
                r0 = 64 * (c % 2)
                for hh in range(2):
                    o = bank[b][64 * hh:64 * hh + 64, (c // 2) * P:(c // 2 + 1) * P]
                    h = 2 * j + hh
                    tu[c] = mm(o, kd[r0:r0 + 64, c // 2, j * P + 64 * hh:j * P + 64 * hh + 64],
                               gv[r0:r0 + 64, c // 2, h * GV:(h + 1) * GV], True, True, t_kd[j], t_gv,
                               *(bfree[b] if c < 2 else []), count=True, share=True)
            for c in range(7):
                b = 4 + 2 * j + c % 2
                o = bank[b][:, (c // 2) * P:(c // 2 + 1) * P]
                w = tu[6] if c % 2 == 0 else tu[5]
                if c == 0:
                    t_st[j] = V(lambda e, j=j, o=o: e.tensor_copy(ST[:, j, 0, :], o), w)
                else:
                    t_st[j] = stt(ST[:, j, c, :], ST[:, j, c - 1, :], el[:, j, c:c + 1], o, ALU.mult, ALU.add,
                                  w, t_st[j], t_el[j])
                bfree[b] = [t_st[j]]
        ogs = AT
        t_og, tgs = [None] * 4, None
        SG = 7
        rg = sb("rg", [P, 16], F, gla)
        mg = sb("mg", [P, 16], F, gla)
        for h in range(GH):
            j, hh = h // 2, h % 2
            b = mbank()
            for q in range(NT):
                cs = slice(q * P, (q + 1) * P)
                mm(bank[b][:, cs], gv[:, q, h * GV:(h + 1) * GV], AT[:, h, cs], q == 0, True, t_at[h], t_gv,
                   *(bfree[b] if q == 0 else []), share=True)
            for c in range(1, 8):
                rows = slice(64 * hh, 64 * hh + 64)
                cs = slice(c * 64, c * 64 + 64)
                t = mm(bank[b][:, cs], ST[rows, j, c - 1, :], qt_[rows, j, cs], False, True, t_st[j], t_qe[j],
                       count=c == 7, share=True)
            t_og[h] = act(ogs[:, h, :], bank[b][:, :], ACT.Copy, t)
            bfree[b] = [t_og[h]]
            k = h % 2
            t2 = act(sq[k][:, :], ogs[:, h, :], ACT.Square, t_og[h], *sqr[k])
            for q in range(NT):
                tgs = mm(bank[SG][:, 4 * h + q:4 * h + q + 1], sq[k][:, q * P:(q + 1) * P], ones[:, 0:1], True, True,
                         t2, *(bfree[SG] if h == 0 else []), count=q == NT - 1, share=True)
            sqr[k] = [tgs]
        t1 = ts(mg[:, :], bank[SG][:, 0:16], 1.0 / GV, ALU.mult, tgs, s2=EPS, op1=ALU.add)
        bfree[SG] = [t1]
        t_rg = G(lambda e: e.tensor_tensor(rg[:, :], mg[:, :], cst[:, C_HALF:C_HALF + 16], ALU.pow), t1, t_c)
        o_tok = [None] * 8
        for h in range(GH):
            b = 4 + h % 2
            t = spread(rg[:, 4 * h:4 * h + 4], b, [t_rg])
            t1 = stt(ogs[:, h, :], ogs[:, h, :], par[:, PC_GN:PC_GN + 1], bank[b][:, :], ALU.mult, ALU.mult, t, t_og[h])
            bfree[b] = [t1]
            t2 = tt(ogs[:, h, :], ogs[:, h, :], gsil[:, h, :], ALU.mult, t1, t_sil[h])
            t3 = act(AH[:, h, :], ogs[:, h, :], ACT.Copy, t2, *a_free[h])
            t4 = tt(AL[:, h, :], ogs[:, h, :], AH[:, h, :].bitcast(F), ALU.subtract, t3)
            o_tok[h] = [t3, t4]
        fence = [o_tok[h][i] for h in range(4) for i in range(2)] + [tgs, t_kd[1], t, t_rg]
        gla.close()

        mla = ExitStack()
        ctx.enter_context(mla)
        qm = sb("qm", [P, 4, MH, MQ], F, mla)
        km = sb("km", [P, 4, MH, MQ], F, mla)
        vm = sb("vm", [P, 4, 512], F, mla)
        tmp = sb("tmp", [P, 3072], F, mla)
        trig = sb("trig", [P, 8, 4, 16], F, mla)
        posi = sb("posi", [P, 4], I32, mla)
        posf = sb("posf", [P, 4], F, mla)
        s_r, s_pos = newsem(), newsem()
        t_row = pr.dma("gpsimd", row[:, :], ROW.to_broadcast([P, ROWS]), s_r, 16, fence)
        t_pos = pr.dma("gpsimd", posi[:, :], POS, s_pos, 16, fence)

        u, wh, wl, wt = take("uq", 0)
        whv, wlv = wh.rearrange("p (k n) -> p k n", k=2), wl.rearrange("p (k n) -> p k n", k=2)
        t_qm = [None] * 4
        for q in range(NT):
            for n in range(2):
                b = mbank()
                for k in range(2):
                    ah, al = cqH[:, k, q * P:(q + 1) * P], cqL[:, k, q * P:(q + 1) * P]
                    cs = slice(384 * n, 384 * n + 384)
                    o = bank[b][:, 0:384]
                    mm(o, ah, whv[:, k, cs], k == 0, False, *wt, *t_cq[0], *t_cq[1], *(bfree[b] if k == 0 else []))
                    mm(o, ah, wlv[:, k, cs], False, False)
                    t = mm(o, al, whv[:, k, cs], False, k == 1, count=k == 1)
                t_qm[q] = ts(qm[:, q, 4 * n:4 * n + 4, :], bank[b][:, 0:384].rearrange("p (h d) -> p h d", h=4),
                             rq3[:, q:q + 1], ALU.mult, t, t_rq3, *fence)
                bfree[b] = [t_qm[q]]
        pe_done[u] = t
        u, wh, wl, wt = take("ukv", 0)
        t_km, t_vm = [None] * 4, [None] * 4
        for q in range(NT):
            for n in range(2):
                b = mbank()
                ah, al = cqH[:, 2, q * P:(q + 1) * P], cqL[:, 2, q * P:(q + 1) * P]
                cs = slice(512 * n, 512 * n + 512)
                mm(bank[b][:, :], ah, wh[:, cs], True, False, *wt, *t_cq[2], *bfree[b])
                mm(bank[b][:, :], ah, wl[:, cs], False, False)
                t = mm(bank[b][:, :], al, wh[:, cs], False, True, count=True)
                if n == 0:
                    t_km[q] = ts(km[:, q, :, 0:MN], bank[b][:, :].rearrange("p (h d) -> p h d", h=8),
                                 rq3[:, 4 + q:5 + q], ALU.mult, t, t_rq3)
                    bfree[b] = [t_km[q]]
                else:
                    t_vm[q] = act(vm[:, q, :], bank[b][:, :], ACT.Copy, t, t_rq3, *fence, scale=rq3[:, 4 + q:5 + q])
                    bfree[b] = [t_vm[q]]
        pe_done[u] = t
        for q in range(NT):
            t_krb = V(lambda e, q=q: e.tensor_copy(km[:, q, :, MN:MQ], kr[:, q, None, :].to_broadcast([P, 8, 32])),
                      t_kr, *fence)
        cw = cody_waite()
        t1 = V(lambda e: e.tensor_copy(posf[:, :], posi[:, :]), t_pos)
        ang, nn_, r0_, r1_, co, si, sc = (trig[:, i, :, :].rearrange("p q f -> p (q f)") for i in range(7))
        t2 = tt(trig[:, 0, :, :], posf[:, :, None].to_broadcast([P, 4, 16]),
                cst[:, None, C_IF:C_IF + 16].to_broadcast([P, 4, 16]), ALU.mult, t1, t_c)
        M = 12582912.0
        t3 = ts(nn_, ang, 1.0 / TWO_PI, ALU.mult, t2, s2=M, op1=ALU.add)
        t3 = ts(nn_, nn_, M, ALU.subtract, t3)
        t = t3
        src = ang
        for i, c in enumerate(cw):
            dst = (r0_, r1_)[i % 2]
            t = stt(dst, nn_, -c, src, ALU.mult, ALU.add, t)
            src = dst
        PI_ = 3.1415925
        t = ts(r0_, src, PI_, ALU.min, t, s2=-PI_, op1=ALU.max)
        t_sin = act(si, r0_, ACT.Sin, t)
        t = ts(r1_, r0_, math.pi / 2, ALU.add, t)
        t = ts(sc, r1_, math.pi, ALU.is_gt, t, s2=TWO_PI, op1=ALU.mult)
        t = tt(r1_, r1_, sc, ALU.subtract, t)
        t = ts(r1_, r1_, PI_, ALU.min, t, s2=-PI_, op1=ALU.max)
        t_cos = act(co, r1_, ACT.Sin, t)
        rn = sb("rn", [P, 2, 32], F, mla)
        mn = sb("mn", [P, 2, 32], F, mla)
        t_m = [None, None]
        tf = []
        for i, (z, tz) in enumerate(((qm, t_qm), (km, t_km + [t_krb]))):
            zf = z[:, :, :, :].rearrange("p q h d -> p (q h d)")
            t = act(tmp[:, :], zf, ACT.Square, *tz, *tf, *fence)
            t = V(lambda e, i=i: e.tensor_reduce(mn[:, i, :], tmp[:, :].rearrange("p (a d) -> p a d", d=MQ), AX.X, ALU.add), t)
            t1 = ts(mn[:, i, :], mn[:, i, :], 1.0 / MQ, ALU.mult, t, s2=EPS, op1=ALU.add)
            t = G(lambda e, i=i: e.tensor_tensor(rn[:, i, :], mn[:, i, :], cst[:, C_HALF:C_HALF + 32], ALU.pow), t1, t_c)
            z3 = z[:, :, :, :].rearrange("p q h d -> p (q h) d")
            t = tt(z3, z3, rn[:, i, :, None].to_broadcast([P, 32, MQ]), ALU.mult, t)
            t = tt(z3, z3, row[:, None, MQ * i:MQ * i + MQ].to_broadcast([P, 32, MQ]), ALU.mult, t, t_row)
            x1, x2 = z[:, :, :, MN:MN + 16], z[:, :, :, MN + 16:MQ]
            tv = tmp[:, 0:2048].rearrange("p (i q h f) -> p i q h f", i=4, q=4, h=8)
            cb = trig[:, 4, :, None, :].to_broadcast([P, 4, 8, 16])
            sb_ = trig[:, 5, :, None, :].to_broadcast([P, 4, 8, 16])
            ta = tt(tv[:, 0], x1, cb, ALU.mult, t, t_cos, t1)
            tb = tt(tv[:, 1], x2, sb_, ALU.mult, t, t_sin)
            tc = tt(tv[:, 2], x2, cb, ALU.mult, t)
            td = tt(tv[:, 3], x1, sb_, ALU.mult, t)
            te = tt(x1, tv[:, 0], tv[:, 1], ALU.subtract, ta, tb, td)
            t_m[i] = tt(x2, tv[:, 2], tv[:, 3], ALU.add, tc, td, te)
            tf = [t_m[i]]


        def attention(nh, kdim, qT, kT, head_rows, fetch, v, t_v, scale, bias, hq, od, at, pb=None):
            pb = pb or [sb(f"pb{nh}_{i}", [P, 512], F, at) for i in range(3)]
            ptb = t2s
            st = sb(f"st{nh}", [P, 3, 4], F, at)
            steps = [(h, q) for h in range(nh) for q in range(NT)]
            s_t, p_t, pt_t = {}, {}, {}
            pfree, ptfree, stf = [[], [], []], [[], []], [[], [], []]
            out_t = []

            def scores(i):
                h, q = steps[i]
                tqk = fetch(h, q)
                b = i % 3
                n = (q + 1) * P
                rows = head_rows(h)
                t = mm(bank[b][:, 0:n], qT(h)[rows, q * P:(q + 1) * P], kT(h)[rows, 0:n], True, True,
                       *tqk, *bfree[b], count=bias is not None)
                if bias is None:
                    t = mm(bank[b][:, n - P:n], cst[0:1, C_MA:C_MA + P], cst[0:1, C_MB:C_MB + P], False, True,
                           count=True, share=True)
                hq(h, q, t)
                k = i % 3
                if bias is None:
                    t1 = V(lambda e: e.reduce_max(st[:, k, 0:1], bank[b][:, 0:n], AX.X), t, *stf[k])
                    t2 = ts(st[:, k, 1:2], st[:, k, 0:1], -scale, ALU.mult, t1)
                    t3 = act(pb[k][:, 0:n], bank[b][:, 0:n], ACT.Exp, t2, *pfree[k], bias=st[:, k, 1:2], scale=scale,
                             accum_out=st[:, k, 2:3])
                    bfree[b] = [t3]
                else:
                    gbuf, tg, gdone = bias(h)
                    t1 = V(lambda e: e.tensor_tensor_reduce(out=pb[k][:, 0:n], in0=bank[b][:, 0:n], in1=gbuf[:, 512 - n:512],
                                                            scale=scale, scalar=-3.0e38, op0=ALU.add, op1=ALU.max,
                                                            accum_out=st[:, k, 0:1]), t, *tg, *pfree[k], *stf[k])
                    bfree[b] = [t1]
                    gdone(t1)
                    t2 = ts(st[:, k, 1:2], st[:, k, 0:1], -1.0, ALU.mult, t1)
                    t3 = act(pb[k][:, 0:n], pb[k][:, 0:n], ACT.Exp, t2, bias=st[:, k, 1:2], accum_out=st[:, k, 2:3])
                p_t[i] = t3

            def turn(i):
                h, q = steps[i]
                k = i % 3
                b = 3 + i % 2
                for c in range(q + 1):
                    t = tr(bank[b][:, c * P:(c + 1) * P], pb[k][:, c * P:(c + 1) * P], p_t[i],
                           *(bfree[b] if c == 0 else []), count=c == q)
                pfree[k] = [t]
                n = (q + 1) * P
                t1 = V(lambda e: e.tensor_copy(ptb[i % 2][:, 0:n], bank[b][:, 0:n]), t, *ptfree[i % 2])
                bfree[b] = [t1]
                pt_t[i] = t1

            def values(i):
                h, q = steps[i]
                b = 5 + i % 2
                for c in range(q + 1):
                    t = mm(bank[b][:, 0:64], ptb[i % 2][:, c * P:(c + 1) * P], v[:, c, h * 64:(h + 1) * 64], c == 0, c == q,
                           pt_t[i], *t_v, *(bfree[b] if c == 0 else []), count=c == q)
                ptfree[i % 2] = [t]
                k = i % 3
                t1 = V(lambda e: e.reciprocal(st[:, k, 3:4], st[:, k, 2:3]), p_t[i])
                t2 = ts(od[h // 2][:, q, (h % 2) * 64:(h % 2) * 64 + 64], bank[b][:, 0:64], st[:, k, 3:4], ALU.mult, t, t1)
                bfree[b] = [t2]
                stf[k] = [t2]
                out_t.append(t2)

            n = len(steps)
            for i in range(n + 2):
                if i < n:
                    if i >= 3:
                        pass
                    scores(i)
                if 0 <= i - 1 < n:
                    turn(i - 1)
                if 0 <= i - 2 < n:
                    values(i - 2)
            return out_t[-1]

        qT = [sb(f"qT{i}", [P, S], F, mla) for i in range(2)]
        kT = [sb(f"kT{i}", [P, S], F, mla) for i in range(2)]
        qk_t = {}
        qk_free = [[], []]

        def fetch1(h, q):
            if h not in qk_t:
                k = h % 2
                toks = []
                for z, dst, tz in ((qm, qT, t_m[0]), (km, kT, t_m[1])):
                    for c in range(NT):
                        t = tr(bank[7][0:MQ, c * P:(c + 1) * P], z[:, c, h, :], tz, t_c,
                               *(bfree[7] if c == 0 else []), count=c == 3)
                    dd_ = dst[k]
                    t1 = act(dd_[0:MQ, :], bank[7][0:MQ, :], ACT.Copy, t, *qk_free[k])
                    bfree[7] = [t1]
                    toks.append(t1)
                qk_t[h] = toks
            return qk_t[h]

        def hq1(h, q, t):
            qk_free[h % 2] = [t]

        od1 = [tmp[:, i * 512:(i + 1) * 512].rearrange("p (q d) -> p q d", q=4) for i in range(4)]
        t_o = attention(MH, MQ, lambda h: qT[h % 2], lambda h: kT[h % 2], lambda h: slice(0, MQ), fetch1, vm, t_vm,
                        MQ ** -0.5, None, hq1, od1, mla)
        for i in range(4):
            b = mbank()
            for q in range(NT):
                t = tr(bank[b][:, q * P:(q + 1) * P], od1[i][:, q, :], t_o,
                       *(bfree[b] if q == 0 else []), count=q == 3)
            t1 = act(AH[:, 4 + i, :], bank[b][:, :], ACT.Copy, t, *a_free[4 + i])
            t2 = tt(AL[:, 4 + i, :], bank[b][:, :], AH[:, 4 + i, :].bitcast(F), ALU.subtract, t1)
            bfree[b] = [t2]
            o_tok[4 + i] = [t1, t2]
        fence = [t_o, t2, t]
        mla.close()
        ph1.close()

        def project_residual(name, act_tok, gcol):
            for i in range(4):
                u, wh, wl, wt = take(name, i)
                whv, wlv = wh.rearrange("p (k n) -> p k n", k=8), wl.rearrange("p (k n) -> p k n", k=8)
                for c in range(2):
                    m = 2 * i + c
                    b = mbank()
                    t = prod_t(b, whv, wlv, slice(c * P, c * P + P), range(8), AH, AL, range(8),
                               [wt + act_tok[k] for k in range(8)])
                    x_t[m] = tt(X[:, m, :], X[:, m, :], bank[b][:, :], ALU.add, t, *x_t_w(m))
                    bfree[b] = [x_t[m]]
                    x_read[m] = [add_square(X[:, m, :], m == 0, x_t[m])]
                pe_done[u] = t
            return prep_all(gcol, t)

        def prep_all(gcol, a_done):
            toks = [None] * 8
            for c in range(8):
                g = par[:, gcol + c:gcol + c + 1]
                t1 = act(AH[:, c, :], X[:, c, :], ACT.Copy, x_t[c], a_done, t_p, scale=g)
                t2 = stt(AL[:, c, :], X[:, c, :], g, AH[:, c, :].bitcast(F), ALU.mult, ALU.subtract, t1)
                x_read[c] = x_read[c] + [t1, t2]
                toks[c] = [t1, t2]
            return toks

        x_t = [None] * 8
        x_read = [[] for _ in range(8)]

        def x_t_w(m):
            return [x_t[m], *x_read[m]]

        a_free = [[] for _ in range(8)]
        xk = project_residual("wout", o_tok, PC_MLP)
        stage[0] = 0

        hid = ExitStack()
        ctx.enter_context(hid)
        NH = 10
        HH = [sb(f"HH{i}", [P, S], R, hid) for i in range(NH)]
        HL = [sb(f"HL{i}", [P, S], R, hid) for i in range(NH)]
        hfree = [list(fence) for _ in range(NH)]
        t1s = [sb(f"t1s{i}", [P, S + 2], F, hid) for i in range(2)]
        t1f, t2f = [list(fence), list(fence)], [list(fence), list(fence)]
        h_t = {}

        def up(i):
            u, wh, wl, wt = take("up", i)
            whv, wlv = wh.rearrange("p (k n) -> p k n", k=8), wl.rearrange("p (k n) -> p k n", k=8)

            def rest(m, b, t):
                k, s = m % 2, m % NH
                t1 = stt(t1s[k][:, 0:S], bank[b][:, :], 0.0, rb[:, :], ALU.max, ALU.mult, t, t_r[1], *t1f[k])
                bfree[b] = [t1]
                rb_free[0] = [t1]
                t2 = act(t2s[k][:, :], t1s[k][:, 0:S], ACT.Square, t1, *t2f[k])
                t1f[k] = [t2]
                t3 = act(HH[s][:, :], t2s[k][:, :], ACT.Copy, t2, *hfree[s])
                t4 = tt(HL[s][:, :], t2s[k][:, :], HH[s][:, :].bitcast(F), ALU.subtract, t3)
                t2f[k] = [t4]
                h_t[m] = [t3, t4]

            for c in range(2):
                m = 2 * i + c
                b = mbank()
                t = prod_t(b, whv, wlv, slice(c * P, c * P + P), range(8), AH, AL, range(8),
                           [wt + xk[k] for k in range(8)])
                tile_done(lambda m=m, b=b, t=t: rest(m, b, t))
            pe_done[u] = t
            return t

        def down(name, g, base, kc, gcol=None, a_done=None, final=False):
            toks = [None] * 8
            for i in range(4):
                u, wh, wl, wt = take(name, 4 * g + i)
                whv, wlv = wh.rearrange("p (k n) -> p k n", k=kc), wl.rearrange("p (k n) -> p k n", k=kc)
                for c in range(2):
                    m = 2 * i + c
                    b = mbank()
                    for k in range(kc):
                        s = (base + k) % NH
                        a = whv[:, k, c * P:(c + 1) * P]
                        mm(bank[b][:, :], a, HH[s][:, :], k == 0, False, *wt, *h_t[base + k],
                           *(bfree[b] if k == 0 else []))
                        mm(bank[b][:, :], a, HL[s][:, :], False, False)
                        t = mm(bank[b][:, :], wlv[:, k, c * P:(c + 1) * P], HH[s][:, :], False, k == kc - 1,
                               count=k == kc - 1)
                    x_t[m] = tt(X[:, m, :], X[:, m, :], bank[b][:, :], ALU.add, t, *x_t_w(m))
                    bfree[b] = [x_t[m]]
                    if final:
                        store(m)
                    if gcol is not None:
                        t1 = add_square(X[:, m, :], m == 0, x_t[m])
                        a_free[m] = [a_done]
                        toks[m] = prep(m, gcol, [x_t[m]])
                        x_read[m] = [t1, toks[m][1]]
                pe_done[u] = t
            for k in range(kc):
                hfree[(base + k) % NH] = [t]
            return t, toks

        up_last = None
        for g in range(5):
            if g < 4:
                up_last = up(4 * g)
            if g > 0:
                _, xk_ = down("down", g - 1, 8 * (g - 1), 8, PC_PLE if g == 4 else None, up_last)
            if g < 4:
                for i in range(1, 4):
                    up_last = up(4 * g + i)
        xk = xk_

        s_o = newsem()

        def store(m):
            pr.dma("sync", OUT[:, m, :], X[:, m, :], s_o, 16 * 8, [x_t[m]])

        ple = ExitStack()
        ctx.enter_context(ple)
        pe_x = sb("pe_x", [P, 2, S], F, ple)
        pH = sb("pH", [P, 2, S], R, ple)
        pL = sb("pL", [P, 2, S], R, ple)
        pj = sb("pj", [P, 8, S], F, ple)
        s_pe = newsem()
        t_pe = pr.dma("gpsimd", pe_x[:, :, :], PT, s_pe, 16, fence)
        t1 = act(pH[:, :, :], pe_x[:, :, :], ACT.Copy, t_pe, *fence)
        t2 = tt(pL[:, :, :], pe_x[:, :, :], pH[:, :, :].bitcast(F), ALU.subtract, t1, *fence)
        u, wh, wl, wt = take("proj", 0)
        whv, wlv = wh.rearrange("p (k n) -> p k n", k=2), wl.rearrange("p (k n) -> p k n", k=2)
        t_pj = [None] * 8
        for m in range(8):
            b = mbank()
            t = prod_t(b, whv, wlv, slice(m * P, m * P + P), range(2), pH, pL, range(2), [wt + [t1, t2]] * 2)
            if m == 3:
                norm_r()
            if m == 5:
                norm_spread()
            t_pj[m] = act(pj[:, m, :], bank[b][:, :], ACT.Copy, t, *fence)
            bfree[b] = [t_pj[m]]
        pe_done[u] = t
        xh = [None] * 8
        for i in range(4):
            u, wh, wl, wt = take("pg", i)
            whv, wlv = wh.rearrange("p (k n) -> p k n", k=8), wl.rearrange("p (k n) -> p k n", k=8)
            for c in range(2):
                m = 2 * i + c
                k = m % 2
                b = mbank()
                t = prod_t(b, whv, wlv, slice(c * P, c * P + P), range(8), AH, AL, range(8),
                           [wt + xk[j] for j in range(8)])
                t1 = tt(t2s[k][:, :], bank[b][:, :], rb[:, :], ALU.mult, t, t_r[1], *t2f[k])
                bfree[b] = [t1]
                t2 = act(t2s[k][:, :], t2s[k][:, :], ACT.Sigmoid, t1, t_p, bias=par[:, PC_BPLE + m:PC_BPLE + m + 1])
                t3 = tt(t2s[k][:, :], t2s[k][:, :], pj[:, m, :], ALU.mult, t2, t_pj[m])
                x_t[m] = tt(X[:, m, :], X[:, m, :], t2s[k][:, :], ALU.add, t3, *x_t_w(m))
                t2f[k] = [x_t[m]]
                tq = add_square(X[:, m, :], m == 0, x_t[m])
                g = par[:, PC_MIX + m:PC_MIX + m + 1]
                ta = ts(HH[m][:, :], X[:, m, :], g, ALU.mult, x_t[m], t_p, *hfree[m])
                tb = stt(HL[m][:, :], X[:, m, :], g, HH[m][:, :].bitcast(F), ALU.mult, ALU.subtract, ta)
                xh[m] = [ta, tb]
                x_read[m] = [tq, tb]
            pe_done[u] = t
        rb_free[0] = [t1]
        a_done = t
        fence = [t, x_t[7]]
        ple.close()

        pool = ExitStack()
        ctx.enter_context(pool)
        hp = [sb(f"hp{i}", [P, S + 16], F, pool) for i in range(3)]
        sa = [sb(f"sa{i}", [P, S + 16], F, pool) for i in range(3)]
        sb2 = [sb(f"sb2{i}", [P, S + 16], F, pool) for i in range(3)]
        bps = sb("bps", [P, 8], F, pool)
        tz = None
        for z in (*hp, *sa, *sb2):
            tz = G(lambda e, z=z: e.memset(z[:, 0:16], 0.0), *fence)
        hpf = [[tz]] * 3
        t_bps = tt(bps[:, :], par[:, PC_PB:PC_PB + 8], par[:, PC_PS:PC_PS + 8], ALU.mult, t_p, *fence)
        u, wh, wl, wt = take("pool", 0)
        whv, wlv = wh.rearrange("p (k n) -> p k n", k=8), wl.rearrange("p (k n) -> p k n", k=8)
        ORDER = [6, 7, 4, 5, 0, 1, 2, 3]
        pt, pbk = {}, {}

        def pool_in(m):
            g = m // 2
            b = pbk[m] = mbank()
            for k in range(2):
                a = whv[:, 2 * g + k, (m % 2) * P:(m % 2) * P + P]
                h = 2 * g + k
                mm(bank[b][:, :], a, HH[h][:, :], k == 0, False, *wt, *xh[h], *(bfree[b] if k == 0 else []))
                mm(bank[b][:, :], a, HL[h][:, :], False, False)
                pt[m] = mm(bank[b][:, :], wlv[:, 2 * g + k, (m % 2) * P:(m % 2) * P + P], HH[h][:, :], False, k == 1, count=k == 1)

        def window(m, k, eng):
            w, b = WINDOWS[m // 2], pbk[m]
            t0 = tt(hp[k][:, 16:], bank[b][:, :], rb[:, :], ALU.mult, pt[m], t_r[1], *hpf[k])
            bfree[b] = [t0]
            rb_free[0] = [t0]
            src, t, step = hp[k], t0, 1
            for dst in (sa[k], sb2[k], sa[k], sb2[k]):
                if step >= w:
                    break
                t = pr(eng, lambda e, d=dst, s=src, st=step: e.tensor_tensor(d[:, 16:], s[:, 16:], s[:, 16 - st:16 - st + S],
                                                                          ALU.add), [t])
                src = dst
                step *= 2
            return src, t

        def finish(m, k, src, t):
            w = WINDOWS[m // 2]
            cnt = cst[:, C_CNT + 16 * (m // 2):C_CNT + 16 * (m // 2) + 16]
            ta = tt(src[:, 16:32], src[:, 16:32], cnt, ALU.mult, t)
            ta = tt(src[:, 16:32], src[:, 16:32], hp[k][:, 16:32], ALU.subtract, ta)
            tb = stt(src[:, 32:], src[:, 32:], 1.0 / w, hp[k][:, 32:], ALU.mult, ALU.subtract, t)
            j = m % 2
            t1 = act(t2s[j][:, :], src[:, 16:], ACT.Identity, ta, tb, t_bps, *t2f[j], bias=bps[:, m:m + 1],
                     scale=par[:, PC_PS + m:PC_PS + m + 1])
            hpf[k] = [t1]
            x_t[m] = tt(X[:, m, :], X[:, m, :], t2s[j][:, :], ALU.add, t1, *x_t_w(m))
            t2f[j] = [x_t[m]]
            tq = add_square(X[:, m, :], m == ORDER[2], x_t[m])
            g = par[:, PC_FFN + m:PC_FFN + m + 1]
            t3 = act(AH[:, m, :], X[:, m, :], ACT.Copy, x_t[m], a_done, t_p, scale=g)
            t4 = stt(AL[:, m, :], X[:, m, :], g, AH[:, m, :].bitcast(F), ALU.mult, ALU.subtract, t3)
            xk[m] = [t3, t4]
            x_read[m] = [tq, t3, t4]

        xk = [None] * 8
        for i, m in enumerate(ORDER[:4]):
            pool_in(m)
            if i == 2:
                norm_r()
        norm_spread()
        late = [(m, k, *window(m, k, "gpsimd")) for k, m in enumerate(ORDER[:2])]
        nxt = 4
        for m in ORDER[2:]:
            if nxt < 8:
                pool_in(ORDER[nxt])
                nxt += 1
            finish(m, 2, *window(m, 2, "vector"))
        for a in late:
            finish(*a)
        pe_done[u] = pt[ORDER[7]]
        fence = [pt[ORDER[7]], x_t[7], xk[7][1], xk[7][0]]
        pool.close()
        stage[0] = 0

        cvs = [sb(f"cvs{i}", [P, S], F, hid) for i in range(2)]
        cvf = [[], []]
        tz1 = None
        for z in t1s:
            tz1 = G(lambda e, z=z: e.memset(z[:, 0:2], 0.0), *t1f[0], *t1f[1])
        t1f = [[tz1], [tz1]]

        def ffn(l, fence):
            for s in range(NH):
                hfree[s] = hfree[s] + list(fence)
            gp = {}
            pairs = [[4 * g + i for i in range((b - a) // 2)] for g, (a, b) in enumerate(GROUPS2)]

            def pair(j):
                def rest(name, m, c, b, t):
                    k, s = c, m % NH
                    if name == "gate":
                        a = t1s[k]
                        cw_ = [par[:, PC_CW + 66 * l + 22 * i + m:PC_CW + 66 * l + 22 * i + m + 1] for i in range(3)]
                        cb_ = par[:, PC_CB + 22 * l + m:PC_CB + 22 * l + m + 1]
                        t1 = tt(a[:, 2:], bank[b][:, :], rb[:, :], ALU.mult, t, t_r[1], *t1f[k])
                        bfree[b] = [t1]
                        t2 = ts(t2s[k][:, :], a[:, 0:S], cw_[0], ALU.mult, t1, *t2f[k])
                        t3 = stt(t2s[k][:, :], a[:, 1:S + 1], cw_[1], t2s[k][:, :], ALU.mult, ALU.add, t2)
                        t4 = stt(t2s[k][:, :], a[:, 2:S + 2], cw_[2], t2s[k][:, :], ALU.mult, ALU.add, t3)
                        t1f[k] = [t4]
                        gp[m] = act(t2s[k][:, :], t2s[k][:, :], ACT.Silu, t4, bias=cb_)
                    else:
                        t1 = tt(cvs[k][:, :], bank[b][:, :], rb[:, :], ALU.mult, t, t_r[1], *cvf[k])
                        bfree[b] = [t1]
                        rb_free[0] = [t1]
                        t2 = tt(cvs[k][:, :], cvs[k][:, :], t2s[k][:, :], ALU.mult, t1, gp[m])
                        t2f[k] = [t2]
                        t3 = act(HH[s][:, :], cvs[k][:, :], ACT.Copy, t2, *hfree[s])
                        t4 = tt(HL[s][:, :], cvs[k][:, :], HH[s][:, :].bitcast(F), ALU.subtract, t3)
                        cvf[k] = [t4]
                        h_t[m] = [t3, t4]

                for name in ("gate", "val"):
                    u, wh, wl, wt = take(f"{name}{l}", j)
                    whv, wlv = wh.rearrange("p (k n) -> p k n", k=8), wl.rearrange("p (k n) -> p k n", k=8)
                    for c in range(2):
                        b = mbank()
                        t = prod_t(b, whv, wlv, slice(c * P, c * P + P), range(8), AH, AL, range(8),
                                   [wt + xk[k] for k in range(8)])
                        m = 2 * j + c
                        tile_done(lambda a=(name, m, c, b, t): rest(*a))
                    pe_done[u] = t
                return t

            for g in range(4):
                if g < 3:
                    last = pair(pairs[g][0])
                if g > 0:
                    a, b = GROUPS2[g - 1]
                    t, toks = down(f"fo{l}", g - 1, a, b - a, PC_MIX + 8 if g == 3 and l == 0 else None, last,
                                   g == 3 and l == 1)
                if g < 3:
                    for j in pairs[g][1:]:
                        last = pair(j)
            return toks, t

        xk, t_dn = ffn(0, fence)
        norm_r()
        t_r4 = t_r[0]
        fence = [t_dn, x_t[7]]
        hid.close()

        at2 = ExitStack()
        ctx.enter_context(at2)
        v2 = sb("v2", [P, 4, D], F, at2)
        qTa = sb("qTa", [P, 8, S], F, at2)
        kTa = sb("kTa", [P, 8, S], F, at2)
        qT2 = [qTa[:, i, :] for i in range(8)]
        kT2 = [kTa[:, i, :] for i in range(8)]
        NQ = 4
        qn = [sb(f"qn{i}", [P, 512], F, at2) for i in range(NQ)]
        qs_ = sb("qs_", [P, 512], F, at2)
        rn2 = sb("rn2", [P, NQ, 8], F, at2)
        mn2 = sb("mn2", [P, NQ, 8], F, at2)
        NG = 2
        Gb = [sb(f"Gb{i}", [P, 512], F, at2) for i in range(NG)]
        rel = sb("rel", [16, 513], F, at2)
        ev = sb("ev", [16, 640], F, at2)
        EV = nc.dram_tensor("ev_scratch", (16, P, 640), F, kind="Internal")
        s_rel, s_ev, s_gb = newsem(), newsem(), [newsem() for _ in range(NG)]
        t_rel = pr.dma("gpsimd", rel[:, :], REL, s_rel, 16, fence)
        t1 = ts(ev[:, 0:255], rel[:, 0:1].to_broadcast([16, 255]), 8.0, ALU.mult, t_rel, *fence)
        t2 = ts(ev[:, 255:640], rel[:, 0:385], 8.0, ALU.mult, t_rel)
        t_ev = pr.dma("gpsimd", EV.ap(), ev[:, None, :].to_broadcast([16, P, 640]), s_ev, 16, [t1, t2])
        tms = None
        for i in range(NG):
            tms = G(lambda e, i=i: e.memset(Gb[i][0:64, 448:512], -1e30), *fence)
        qnf = [list(fence) for _ in range(NQ)]
        rnf = [[] for _ in range(NQ)]
        later = []

        def turn_z(blk, q, kx, t7):
            z = qn[kx]
            bb = 4 + kx
            for i in range(4):
                t = tr(bank[bb][:, i * P:(i + 1) * P], z[:, i * P:(i + 1) * P], t7, *(bfree[bb] if i == 0 else []),
                       count=i == 3)
            qnf[kx] = [t]
            d = (qTa if blk < 2 else kTa)[:, 4 * (blk % 2):4 * (blk % 2) + 4, q * P:(q + 1) * P]
            qk2[(blk, q)] = act(d, bank[bb][:, :].rearrange("p (i n) -> p i n", i=4), ACT.Copy, t, *fence)
            bfree[bb] = [qk2[(blk, q)]]

        qk2 = {}
        tqs = list(fence)
        t_v2 = []
        cnt_b, step = 0, 0
        for blk in range(6):
            bs = [mbank() for _ in range(NT)]
            for hlf in range(2):
                u, wh, wl, wt = take("qkv", 2 * blk + hlf)
                whv, wlv = wh.rearrange("p (k n) -> p k n", k=4), wl.rearrange("p (k n) -> p k n", k=4)
                for q in range(NT):
                    for k in range(4):
                        kk = 4 * hlf + k
                        o = bank[bs[q]][:, :]
                        st = hlf == 0 and k == 0
                        ah, al = AH[:, kk, q * P:(q + 1) * P], AL[:, kk, q * P:(q + 1) * P]
                        mm(o, ah, whv[:, k, :], st, False, *wt, *xk[kk], *(bfree[bs[q]] if st else []))
                        mm(o, ah, wlv[:, k, :], False, False)
                        t = mm(o, al, whv[:, k, :], False, k == 3 and hlf == 1, count=k == 3)
                    step += 1
                    while later and later[0][0] <= step - 3:
                        turn_z(*later.pop(0)[1])
                    if hlf == 0:
                        continue
                    if blk >= 4:
                        tv = act(v2[:, q, (blk - 4) * 512:(blk - 3) * 512], bank[bs[q]][:, :], ACT.Copy, t, t_r4, *fence,
                                 scale=r4[:, q:q + 1])
                        bfree[bs[q]] = [tv]
                        t_v2.append(tv)
                        continue
                    kx = cnt_b % NQ
                    z = qn[kx]
                    cnt_b += 1
                    t1 = ts(z[:, :], bank[bs[q]][:, :], r4[:, q:q + 1], ALU.mult, t, t_r4, *qnf[kx])
                    bfree[bs[q]] = [t1]
                    t2 = act(qs_[:, :], z[:, :], ACT.Square, t1, *tqs)
                    t3 = V(lambda e, kx=kx: e.tensor_reduce(mn2[:, kx, :], qs_[:, :].rearrange("p (h d) -> p h d", d=64),
                                                            AX.X, ALU.add), t2, *rnf[kx])
                    tqs = [t3]
                    t4 = ts(mn2[:, kx, :], mn2[:, kx, :], 1.0 / 64, ALU.mult, t3, s2=EPS, op1=ALU.add)
                    t5 = G(lambda e, kx=kx: e.tensor_tensor(rn2[:, kx, :], mn2[:, kx, :], cst[:, C_HALF:C_HALF + 8], ALU.pow),
                           t4, t_c)
                    z3 = z[:, :].rearrange("p (h d) -> p h d", d=64)
                    t6 = tt(z3, z3, rn2[:, kx, :, None].to_broadcast([P, 8, 64]), ALU.mult, t5)
                    rnf[kx] = [t6]
                    g0 = 2 * MQ + (0 if blk < 2 else HD2)
                    t7 = tt(z3, z3, row[:, None, g0:g0 + HD2].to_broadcast([P, 8, 64]), ALU.mult, t6, t_row)
                    later.append((step, (blk, q, kx, t7)))
                pe_done[u] = t
        a_done = t
        fence2 = [t]
        tqk_all = [qk2[k] for k in qk2]
        gb_t, gb_free = {}, [[tms], [tms]]

        def loadG(h):
            i = h % NG
            w = [t_ev, *gb_free[i]]
            src = EV.ap()

            def toe(r0, rows, cols):
                return bass.AP(EV, (h * P + r0) * 640 + 127 - r0, [[639, rows], [1, cols]])
            pr.dma("gpsimd", Gb[i][0:64, 0:448], toe(0, 64, 448), s_gb[i], 0, w)
            gb_t[h] = [pr.dma("gpsimd", Gb[i][64:128, :], toe(64, 64, 512), s_gb[i], 32 * (h // NG + 1), w)]

        def bias2(h):
            def done(t):
                gb_free[h % NG] = [t]
            return Gb[h % NG], gb_t[h], done

        loaded = set()

        def fetch2(h, q):
            if q == 0:
                for x in (h, h + 1):
                    if x < H2 and x not in loaded and (x < NG or x - NG < h):
                        loaded.add(x)
                        loadG(x)
            return tqk_all

        oex = sb("oex", [P, 512], F, at2)
        od2 = [z.rearrange("p (q d) -> p q d", q=4) for z in [oex] + qT2[0:7]]
        t_o = attention(H2, HD2, lambda h: qT2[h // 2], lambda h: kT2[h // 2], lambda h: slice(64 * (h % 2), 64 * (h % 2) + 64),
                        fetch2, v2, t_v2, 0.125, bias2, lambda h, q, t: None, od2, at2, qn)
        for i in range(8):
            b = mbank()
            for q in range(NT):
                t = tr(bank[b][:, q * P:(q + 1) * P], od2[i][:, q, :], t_o,
                       *(bfree[b] if q == 0 else []), count=q == 3)
            t1 = act(AH[:, i, :], bank[b][:, :], ACT.Copy, t, a_done)
            t2 = tt(AL[:, i, :], bank[b][:, :], AH[:, i, :].bitcast(F), ALU.subtract, t1, a_done)
            bfree[b] = [t2]
            o_tok[i] = [t1, t2]
        fence = [t, t1, t2, t_o, gb_t[15][0], gb_t[14][0]]
        at2.close()
        xk = project_residual("wo", o_tok, PC_FFN + 8)
        stage[0] = 0

        hid = ExitStack()
        ctx.enter_context(hid)
        HH = [sb(f"HI{i}", [P, S], R, hid) for i in range(NH)]
        HL = [sb(f"HM{i}", [P, S], R, hid) for i in range(NH)]
        cvs = [sb(f"cvt{i}", [P, S], F, hid) for i in range(2)]
        t1s = [sb(f"t1t{i}", [P, S + 2], F, hid) for i in range(2)]
        for z in t1s:
            tz1 = G(lambda e, z=z: e.memset(z[:, 0:2], 0.0), *fence)
        t1f = [[tz1], [tz1]]
        cvf = [list(fence), list(fence)]
        hfree = [[] for _ in range(NH)]
        t2f = [list(fence), list(fence)]
        ffn(1, fence)

        assert cur[0] == len(plan)

        block = ctx.enter_context(nc.Block())

        @block.sync
        def _(e):
            pr.play("sync", e)
            e.wait_ge(s_o, 16 * 8)

        @block.tensor
        def _(e):
            pr.play("tensor", e)

        @block.vector
        def _(e):
            pr.play("vector", e)

        @block.scalar
        def _(e):
            pr.play("scalar", e)

        @block.gpsimd
        def _(e):
            pr.play("gpsimd", e)


def constants():
    c = np.zeros((P, NCC), np.float32)
    c[:, C_ID:C_ID + P] = np.eye(P)
    c[:, C_ONE:C_ONE + P] = 1.0
    c[:, C_HALF:C_HALF + P] = -0.5
    c[:, C_SCAN:C_SCAN + S] = (np.arange(S) % 64 != 0)
    c[0, C_MA:C_MA + 64] = -1e30
    c[0, C_MB + 64:C_MB + P] = 1.0
    c[:, C_IF:C_IF + 16] = np.float32(10000.0) ** (-np.arange(0, 32, 2, dtype=np.float32) / np.float32(32))
    for g, w in enumerate(WINDOWS):
        c[:, C_CNT + 16 * g:C_CNT + 16 * g + 16] = 1.0 / np.minimum(np.arange(16) + 1, w)
    s, t = np.meshgrid(np.arange(P), np.arange(P), indexing="ij")
    m = np.zeros((P, 7, P), np.int32)
    m[:, 0, :] = s == t
    for i, b in enumerate(LEVELS):
        m[:, i + 1, :] = (s // (2 * b) == t // (2 * b)) & (s % (2 * b) < b) & (t % (2 * b) >= b)
    return c, m


def kernel(**x):
    import concourse.bacc as bacc
    from concourse.bass_utils import run_bass_kernel_spmd as run

    x = {k: np.asarray(v) for k, v in x.items()}
    f4 = np.float32

    def cols(w, a, b):
        k = w.shape[0] // P
        return w[:, a:b].reshape(k, P, b - a).transpose(1, 0, 2).reshape(P, -1)

    w_in = x["w_in"][0]
    ukv = x["mla_w_ukv"][0].reshape(128, MH, 128)
    units = {
        "small": lambda i: cols(np.concatenate([w_in[:, 1024:1040], w_in[:, 1936:1968]], 1), 0, 48),
        "cq": lambda i: cols(w_in, 1552, 1808),
        "ckv": lambda i: cols(w_in, 1808, 1936),
        "gq": lambda i: cols(w_in, 0, 256),
        "gk": lambda i: cols(w_in, 256, 512),
        "gv": lambda i: cols(w_in[512 * i:512 * i + 512], 512, 1024),
        "gr": lambda i: cols(w_in, 1040 + 256 * i, 1296 + 256 * i),
        "uq": lambda i: cols(x["mla_w_uq"][0], 0, 768),
        "ukv": lambda i: np.concatenate([ukv[:, :, 0:64].reshape(128, 512), ukv[:, :, 64:].reshape(128, 512)], 1),
        "wout": lambda i: cols(x["w_out"][0], 256 * i, 256 * i + 256),
        "up": lambda i: cols(x["w_mlp_up"][0], 256 * i, 256 * i + 256),
        "down": lambda i: cols(x["w_mlp_down"][0][1024 * (i // 4):1024 * (i // 4) + 1024], 256 * (i % 4), 256 * (i % 4) + 256),
        "proj": lambda i: cols(x["w_ple_proj"][0], 0, 1024),
        "pg": lambda i: cols(x["w_ple_gate"][0], 256 * i, 256 * i + 256),
        "pool": lambda i: cols(x["pool_w_2"][0].reshape(1024, 256), 0, 256),
        "qkv": lambda i: cols(x["attn_wqkv_2"][0][512 * (i % 2):512 * (i % 2) + 512], 512 * (i // 2), 512 * (i // 2) + 512),
        "wo": lambda i: cols(x["attn_wo_2"][0], 256 * i, 256 * i + 256),
    }
    for l in range(2):
        units[f"gate{l}"] = lambda i, l=l: cols(x["ffn_w_gate_2"][l], 256 * i, 256 * i + 256)
        units[f"val{l}"] = lambda i, l=l: cols(x["ffn_w_val_2"][l], 256 * i, 256 * i + 256)
        units[f"fo{l}"] = lambda i, l=l: cols(x["ffn_w_out_2"][l][P * GROUPS2[i // 4][0]:P * GROUPS2[i // 4][1]],
                                              256 * (i % 4), 256 * (i % 4) + 256)
    plan = unit_plan()
    W = np.zeros((len(plan), P, UE), f4)
    for u, (name, i, n) in enumerate(plan):
        W[u, :, 0:n] = units[name](i)
    vecs = [x["attn_norm"], x["mlp_norm"], x["ple_norm"], x["b_ple_gate"], x["mix_norm_2"], x["ffn_norm_2"],
            x["pool_b_2"], x["pool_scale_2"], x["ffn_conv_w_2"], x["ffn_conv_b_2"], x["gla_gate_b"],
            x["gla_out_norm"], x["mla_q_norm"], x["mla_kv_norm"]]
    PV = np.ascontiguousarray(np.concatenate([v.reshape(-1, P) for v in vecs], 0).T)
    ROW = np.concatenate([x["qk_norm_q"][0], x["qk_norm_k"][0], x["attn_q_norm_2"][0], x["attn_k_norm_2"][0]])[None]
    CST, MSK = constants()
    arrays = {
        "W": W,
        "XT": np.ascontiguousarray(x["x"][0].T.reshape(8, P, S).transpose(1, 0, 2)),
        "PT": np.ascontiguousarray(x["p"][0, 0].T.reshape(2, P, S).transpose(1, 0, 2)),
        "PV": PV,
        "ROW": np.ascontiguousarray(ROW),
        "GW2": np.ascontiguousarray(x["gla_gate_w2"][0]),
        "POS": np.ascontiguousarray(x["positions"][0].reshape(4, P).T),
        "REL": np.ascontiguousarray(x["attn_rel_bias_2"][0][:, ::-1]),
        "CST": CST,
        "MSK": MSK,
    }
    nc = bacc.Bacc("TRN2", target_bir_lowering=False, num_devices=1)
    aps = [nc.dram_tensor(f"in_{k}", a.shape, mybir.dt.from_np(a.dtype), kind="ExternalInput").ap() for k, a in arrays.items()]
    out = nc.dram_tensor("out_0", (P, 8, S), F, kind="ExternalOutput").ap()
    build(nc, *aps, out)
    r = run(nc, [{f"in_{k}": a for k, a in arrays.items()}], core_ids=[0])
    o = r.results[0]["out_0"]
    return np.ascontiguousarray(o.transpose(1, 0, 2).reshape(D, S).T)[None]
```

```python
import math
from contextlib import ExitStack

import numpy as np
import concourse.bass as bass
from concourse import mybir

F = mybir.dt.float32
R = mybir.dt.float32r
I32 = mybir.dt.int32
ALU = mybir.AluOpType
ACT = mybir.ActivationFunctionType
AX = mybir.AxisListType

P = 128
S = 512
D = 1024
NT = 4
EPS = 1e-6
UE = 2048

GH, GK, GV = 4, 64, 128
MH, MN, MR, MV, MQ = 8, 64, 32, 64, 96
H2, HD2 = 16, 64
FF2 = 2816
GROUPS2 = [(0, 8), (8, 16), (16, 22)]
LEVELS = [32, 16, 8, 4, 2, 1]
WINDOWS = (2, 4, 8, 16)

PC_ATT, PC_MLP, PC_PLE, PC_BPLE, PC_MIX, PC_FFN = 0, 8, 16, 24, 32, 48
PC_PB, PC_PS, PC_CW, PC_CB, PC_GB, PC_GN, PC_QN, PC_KVN = 64, 72, 80, 212, 256, 258, 259, 261
NPC = 262
C_ID, C_ONE, C_HALF, C_SCAN, C_MA, C_MB, C_IF, C_CNT = 0, 128, 256, 384, 896, 1024, 1152, 1168
NCC = 1168 + 64
ROWS = 2 * MQ + 2 * HD2

TWO_PI = 2.0 * math.pi


def cody_waite():
    parts, rest = [], TWO_PI
    for bits in (8, 8, 8):
        e = math.floor(math.log2(abs(rest)))
        q = 2.0 ** (e - bits + 1)
        parts.append(math.floor(rest / q) * q)
        rest -= parts[-1]
    return parts + [float(np.float32(rest))]


def unit_plan():
    plan = [("small", 0, 8 * 64), ("cq", 0, 2048), ("ckv", 0, 1024), ("gq", 0, 2048), ("uq", 0, 1536),
            ("ukv", 0, 1024), ("gk", 0, 2048), ("gr", 0, 2048), ("gr", 1, 2048), ("gv", 0, 2048), ("gv", 1, 2048)]
    plan += [("wout", i, 2048) for i in range(4)]
    for g in range(4):
        plan += [("up", 4 * g + i, 2048) for i in range(4)]
    order = plan[:-16]
    ups, k = plan[-16:], 0
    for g in range(5):
        if g < 4:
            order += ups[4 * g:4 * g + 1]
        if g > 0:
            order += [("down", 4 * (g - 1) + i, 2048) for i in range(4)]
        if g < 4:
            order += ups[4 * g + 1:4 * g + 4]
    order += [("proj", 0, 2048)] + [("pg", i, 2048) for i in range(4)] + [("pool", 0, 2048)]

    def ffn(l):
        out = []
        pairs = [[4 * g + i for i in range((b - a) // 2)] for g, (a, b) in enumerate(GROUPS2)]
        for g in range(4):
            if g < 3:
                out += [(f"gate{l}", pairs[g][0], 2048), (f"val{l}", pairs[g][0], 2048)]
            if g > 0:
                kc = GROUPS2[g - 1][1] - GROUPS2[g - 1][0]
                out += [(f"fo{l}", 4 * (g - 1) + i, kc * 256) for i in range(4)]
            if g < 3:
                for j in pairs[g][1:]:
                    out += [(f"gate{l}", j, 2048), (f"val{l}", j, 2048)]
        return out

    order += ffn(0)
    order += [("qkv", i, 2048) for i in range(12)]
    order += [("wo", i, 2048) for i in range(4)]
    order += ffn(1)
    return order


class Prog:

    def __init__(self, sems):
        self.q = {k: [] for k in ("tensor", "vector", "scalar", "gpsimd", "sync")}
        self.n = {k: 0 for k in self.q}
        self.sems = sems

    def __call__(self, eng, fn, waits=(), count=True):
        if count:
            self.n[eng] += 1
        self.q[eng].append((fn, [w for w in waits if w is not None], self.sems[eng] if count else None, 1))
        return (eng, self.n[eng]) if count else None

    def dma(self, eng, out, in_, sem, total, waits=()):
        self.q[eng].append((lambda e: e.dma_start(out, in_), [w for w in waits if w is not None], sem, 16))
        return (sem, total)

    def play(self, eng, e):
        seen = {}
        for fn, waits, sem, by in self.q[eng]:
            for w, n in waits:
                s = self.sems[w] if isinstance(w, str) else w
                if seen.get(id(s), 0) < n:
                    e.wait_ge(s, n)
                    seen[id(s)] = n
            ins = fn(e)
            if sem is not None:
                ins.then_inc(sem, by)


def build(nc, W, XT, PT, PV, ROW, GW2, POS, REL, CST, MSK, OUT):
    plan = unit_plan()
    ctx = ExitStack()
    with ctx:
        sems = {k: ctx.enter_context(nc.semaphore(f"s_{k}")) for k in ("tensor", "vector", "scalar", "gpsimd", "sync")}
        pr = Prog(sems)
        nsem = [0]

        def newsem():
            nsem[0] += 1
            return ctx.enter_context(nc.semaphore(f"s_x{nsem[0]}"))

        def sb(name, shape, dt=F, at=None):
            return (at or ctx).enter_context(nc.sbuf_tensor(name, shape, dt))

        def over(name, shape, at):
            return nc.alloc_sbuf_tensor_at(name, shape, F, offset=at)

        bank = [ctx.enter_context(nc.psum_tensor(f"bank{i}", [P, 512], F)) for i in range(8)]
        bfree = [[] for _ in range(8)]

        cst = sb("cst", [P, NCC])
        par = sb("par", [P, NPC])
        X = sb("X", [P, 8, S])
        AH = sb("AH", [P, 8, S], R)
        AH_at = nc.sbuf_base - 8 * S * 4
        AL = sb("AL", [P, 8, S], R)
        AL_at = nc.sbuf_base - 8 * S * 4
        NR, NW = 2, 3
        RAW = [sb(f"RAW{i}", [P, UE]) for i in range(NR)]
        WH = [sb(f"WH{i}", [P, UE], R) for i in range(NW)]
        W_at = nc.sbuf_base - NW * UE * 4
        WL = [sb(f"WL{i}", [P, UE], R) for i in range(NW)]
        rb = sb("rb", [P, S])
        sq = [sb(f"sq{i}", [P, S]) for i in range(2)]
        dg = sb("dg", [P, 4, P])
        t2s = [sb(f"t2s{i}", [P, S]) for i in range(2)]
        row = sb("row", [P, ROWS])
        r4 = sb("r4", [P, 4])
        m4 = sb("m4", [P, 4])
        ident = cst[:, C_ID:C_ID + P]
        ones = cst[:, C_ONE:C_ONE + P]

        def V(fn, *w):
            return pr("vector", fn, w)

        def A(fn, *w):
            return pr("scalar", fn, w)

        def G(fn, *w):
            return pr("gpsimd", fn, w)

        def T(fn, *w, count=False):
            return pr("tensor", fn, w, count)

        def tt(out, a, b, op, *w):
            return V(lambda e: e.tensor_tensor(out, a, b, op), *w)

        def ts(out, a, s1, op0, *w, s2=None, op1=None):
            if op1 is None:
                return V(lambda e: e.tensor_scalar(out, a, s1, None, op0), *w)
            return V(lambda e: e.tensor_scalar(out, a, s1, s2, op0, op1), *w)

        def stt(out, a, s, b, op0, op1, *w):
            return V(lambda e: e.scalar_tensor_tensor(out, a, s, b, op0, op1), *w)

        def act(out, a, f, *w, **k):
            return A(lambda e: e.activation(out, a, f, **k), *w)

        def mm(out, l, r, start, stop, *w, count=False, share=False):
            return T(lambda e: e.matmul(out, l, r, start=start, stop=stop, skip_group_check=share), *w, count=count)

        def tr(out, a, *w, count=False):
            k = a.shape[0]
            return T(lambda e: e.transpose(out, a, ident[0:k, 0:k]), *w, count=count)

        s_c, s_p, s_xl = newsem(), newsem(), newsem()
        t_p = pr.dma("scalar", par[:, :], PV, s_p, 16)
        s_xl = [s_xl] + [newsem() for _ in range(3)]
        t_xc = [None] * 4

        s_w = [newsem() for _ in range(NR)]
        raw_free = {}
        pe_done = {}
        hi_tok, lo_tok = {}, {}
        w_tok = {}

        def load(u):
            w = raw_free.get(u - NR, [])
            n = plan[u][2]
            w_tok[u] = pr.dma("sync", RAW[u % NR][:, 0:n], W[u, :, 0:n], s_w[u % NR], 16 * (u // NR + 1), w)

        def split(u, *extra):
            if u >= len(plan):
                return
            n, i, j = plan[u][2], u % NR, u % NW
            free = pe_done.get(u - NW)
            hi_tok[u] = act(WH[j][:, 0:n], RAW[i][:, 0:n], ACT.Copy, w_tok[u], free, *extra)
            lo_tok[u] = tt(WL[j][:, 0:n], RAW[i][:, 0:n], WH[j][:, 0:n].bitcast(F), ALU.subtract, hi_tok[u], free)
            raw_free[u] = [hi_tok[u], lo_tok[u]]
            if u + NR < len(plan):
                load(u + NR)

        def load_x(i):
            t_xc[i] = pr.dma("sync", X[:, 2 * i:2 * i + 2, :], XT[:, 2 * i:2 * i + 2, :], s_xl[i], 16)

        load_x(0)
        load(0)
        load_x(1)
        load_x(2)
        load_x(3)
        load(1)
        t_c = pr.dma("scalar", cst[:, :], CST, s_c, 16)
        cur = [0]
        pend, stage, held = [], [3], []

        def take(name, idx, ahead=True):
            u = cur[0]
            assert plan[u][:2] == (name, idx), (u, plan[u], name, idx)
            cur[0] += 1
            if ahead and stage[0] < 3:
                held.append(u + 2)
            elif ahead:
                split(u + 2)
            j, n = u % NW, plan[u][2]
            return u, WH[j][:, 0:n], WL[j][:, 0:n], [hi_tok[u], lo_tok[u]]

        main, ring = [0], [4]

        def mbank():
            b = main[0] % ring[0]
            main[0] += 1
            return b

        def prod_t(b, wh, wl, cols, kcs, ah, al, rows, waits, last=None, first=True, m=P):
            tok = None
            n = len(kcs)
            for i, (k, r) in enumerate(zip(kcs, rows)):
                w = list(waits[i]) if waits else []
                if i == 0 and first:
                    w += bfree[b]
                a, c = wh[:, k, cols], wl[:, k, cols]
                st = first and i == 0
                en = i == n - 1
                mm(bank[b][0:m, :], a, ah[:, r, :], st, False, *w)
                mm(bank[b][0:m, :], a, al[:, r, :], False, False)
                tok = mm(bank[b][0:m, :], c, ah[:, r, :], False, en, count=en)
            return tok

        def group(tiles, ks, waits):
            toks = [None] * len(tiles)
            for n, k in enumerate(ks):
                for i, (b, wh, wl, cols, m) in enumerate(tiles):
                    o, a, c = bank[b][0:m, :], wh[:, k, cols], wl[:, k, cols]
                    st, en = opened.get(b) is None, opened.get(b) == 7
                    mm(o, a, AH[:, k, :], st, False, *waits[k], *(bfree[b] if st else []))
                    mm(o, a, AL[:, k, :], False, False)
                    toks[i] = mm(o, c, AH[:, k, :], False, en, count=en or i == len(tiles) - 1)
                    chunk_done[k] = toks[i]
                    opened[b] = None if en else opened.get(b, 0) + 1 if opened.get(b) is not None else 1
            return toks

        opened, chunk_done = {}, {}

        split(0)

        sqr = [[], []]

        def square_small(src, c, n, b, col, start, *w):
            k = c % 2
            t = act(sq[k][:, :], src, ACT.Square, *w, *sqr[k])
            tok = None
            for q in range(NT):
                tok = mm(bank[b][:, col + q:col + q + 1], sq[k][:, q * P:(q + 1) * P], ones[:, 0:1],
                         start and q == 0, c == n - 1, t, t_c, *(bfree[b] if start and q == 0 else []),
                         count=q == NT - 1, share=True)
            sqr[k] = [tok]
            return tok

        def rpow(out, src, tmp, scale, *w):
            t1 = ts(tmp, src, scale, ALU.mult, *w, s2=EPS, op1=ALU.add)
            n = out.shape[1]
            return t1, G(lambda e: e.tensor_tensor(out, tmp, cst[:, C_HALF:C_HALF + n], ALU.pow), t1, t_c)

        spread_free = [[], []]

        def spread(r, b, w, dst=None):
            t = tt(dg[:, :, :], ident[:, None, :].to_broadcast([P, 4, P]), r[:, :, None].to_broadcast([P, 4, P]),
                   ALU.mult, *w, *spread_free[0], t_c)
            t2 = mm(bank[b][:, :], ones, dg[:, :, :].rearrange("p q n -> p (q n)"), True, True, t, *bfree[b], count=True)
            spread_free[0] = [t2]
            if dst is None:
                return t2
            t3 = act(dst, bank[b][:, :], ACT.Copy, t2, *spread_free[1])
            bfree[b] = [t3]
            return t3

        a_free = [[] for _ in range(8)]

        def prep(c, gcol, w):
            g = par[:, gcol + c:gcol + c + 1]
            t1 = ts(AH[:, c, :], X[:, c, :], g, ALU.mult, *w, *a_free[c], t_p)
            t2 = stt(AL[:, c, :], X[:, c, :], g, AH[:, c, :].bitcast(F), ALU.mult, ALU.subtract, t1)
            return [t1, t2]

        SB_ = 7

        acc = dg[:, :, :].rearrange("p q n -> p (q n)")
        acc_t = [None]

        def add_square(src, first, *w, eng="vector"):
            if first:
                acc_t[0] = act(acc, src, ACT.Square, *w, *spread_free[0])
                return acc_t[0]
            k = sqn[0] % 2
            sqn[0] += 1
            t = act(sq[k][:, :], src, ACT.Square, *w, *sqr[k])
            acc_t[0] = pr(eng, lambda e: e.tensor_tensor(acc, acc, sq[k][:, :], ALU.add), [t, acc_t[0]])
            sqr[k] = [acc_t[0]]
            return t

        sqn = [0]

        rb_free = [[]]

        def norm_r():
            b = SB_
            for q in range(NT):
                t = mm(bank[b][:, q:q + 1], dg[:, q, :], ones[:, 0:1], True, True, acc_t[0], t_c,
                       *(bfree[b] if q == 0 else []), count=q == NT - 1, share=True)
            t1, t2 = rpow(r4[:, :], bank[b][:, 0:4], m4[:, :], 1.0 / D, t)
            bfree[b] = [t1]
            t_r[0] = t2

        def norm_spread():
            spread_free[1] = rb_free[0]
            t_r[1] = spread(r4, SB_, [t_r[0]], rb[:, :])

        t_r = [None, None]
        def tile_done(fn):
            pend.append(fn)
            if stage[0] == 0:
                norm_r()
            elif stage[0] == 2:
                norm_spread()
            stage[0] += 1
            if stage[0] >= 3:
                for u in held:
                    split(u)
                held.clear()
                for f in pend:
                    f()
                pend.clear()

        ph1 = ExitStack()
        ctx.enter_context(ph1)
        gq = sb("gq", [P, 2, S], F, ph1)
        gk = sb("gk", [P, 2, S], F, ph1)
        gsil = sb("gsil", [P, 4, S], F, ph1)
        gv = sb("gv", [P, 4, 512], F, ph1)
        gw2 = sb("gw2", [16, 256], F, ph1)
        s_m, s_g = newsem(), newsem()
        t_g = pr.dma("sync", gw2[:, :], GW2, s_g, 16)
        low = sb("low", [64, S], F, ph1)
        el = sb("el", [P, 2, 8], F, ph1)
        rg = sb("rg", [P, 16], F, ph1)
        mg = sb("mg", [P, 16], F, ph1)
        glow = low[0:16, :]
        mla = ExitStack()
        ctx.enter_context(mla)
        qm = sb("qm", [P, 4, MH, MQ], F, mla)
        qm_at = nc.sbuf_base - 4 * MH * MQ * 4
        km = sb("km", [P, 4, MH, MQ], F, mla)
        msk = sb("msk", [P, 7, P], I32, mla)
        t_msk = pr.dma("gpsimd", msk[:, :, :], MSK, s_m, 16)
        vm = sb("vm", [P, 4, 512], F, mla)
        cqb = sb("cqb", [P, 6, S], R, mla)
        cqH, cqL = cqb[:, 0:3, :], cqb[:, 3:6, :]
        tmp = over("tmp", [P, 6 * S], nc.sbuf_base - 6 * S * 4)
        posi = sb("posi", [P, 4], I32, mla)
        posf = sb("posf", [P, 4], F, mla)
        rq3 = sb("rq3", [P, 8], F, mla)
        mq3 = sb("mq3", [P, 8], F, mla)
        s_r, s_pos = newsem(), newsem()
        t_row = pr.dma("gpsimd", row[:, :], ROW.to_broadcast([P, ROWS]), s_r, 16)
        t_pos = pr.dma("gpsimd", posi[:, :], POS, s_pos, 16)

        xk = [None] * 8
        for c in range(8):
            add_square(X[:, c, :], c == 0, t_xc[c // 2], eng="gpsimd")
            xk[c] = prep(c, PC_ATT, [t_xc[c // 2]])
        split(1)

        u0, wh, wl, wt0 = take("small", 0)
        w8 = (wh.rearrange("p (k n) -> p k n", k=8), wl.rearrange("p (k n) -> p k n", k=8))
        b0 = mbank()
        tg0 = group([(b0, *w8, slice(0, 64), 64)], range(8), [wt0 + xk[k] for k in range(8)])[0]
        pe_done[u0] = tg0
        norm_r()
        u1, wh, wl, wt1 = take("cq", 0)
        w8 = (wh.rearrange("p (k n) -> p k n", k=8), wl.rearrange("p (k n) -> p k n", k=8))
        cq_banks = [mbank(), mbank()]
        tg = group([(cq_banks[0], *w8, slice(0, P), P)], range(8), [wt1] * 8)
        norm_spread()
        tg += group([(cq_banks[1], *w8, slice(P, 2 * P), P)], range(8), [wt1] * 8)
        pe_done[u1] = tg[1]
        t_r4, t_rb = t_r
        tgl = tt(low[:, :], bank[b0][0:64, :], rb[0:64, :], ALU.mult, tg0, t_rb)
        bfree[b0] = [tgl]

        ctmp = t2s
        cfree = [[], []]
        t_cq = [None] * 3
        tsq = [None] * 3
        u, wh, wl, wt = take("ckv", 0)
        whv, wlv = wh.rearrange("p (k n) -> p k n", k=8), wl.rearrange("p (k n) -> p k n", k=8)
        b = mbank()
        pe_done[u] = prod_t(b, whv, wlv, slice(0, P), range(8), AH, AL, range(8), [wt] * 8)
        for i, (b, t) in enumerate([(cq_banks[0], tg[0]), (cq_banks[1], tg[1]), (b, pe_done[u])]):
            k = i % 2
            t1 = tt(ctmp[k][:, :], bank[b][:, :], rb[:, :], ALU.mult, t, t_rb, *cfree[k])
            bfree[b] = [t1]
            tsq[i] = square_small(ctmp[k][:, :], i if i < 2 else 0, 2 if i < 2 else 1, SB_ - 1, 0 if i < 2 else 4, i == 0, t1)
            g = par[:, PC_QN + i:PC_QN + i + 1]
            t2 = ts(cqH[:, i, :], ctmp[k][:, :], g, ALU.mult, t1, t_p)
            t3 = stt(cqL[:, i, :], ctmp[k][:, :], g, cqH[:, i, :].bitcast(F), ALU.mult, ALU.subtract, t2)
            cfree[k] = [t3, tsq[i]]
            t_cq[i] = [t2, t3]
        t1 = ts(mq3[:, 0:4], bank[SB_ - 1][:, 0:4], 1.0 / 256, ALU.mult, tsq[2], s2=EPS, op1=ALU.add)
        t2 = ts(mq3[:, 4:8], bank[SB_ - 1][:, 4:8], 1.0 / 128, ALU.mult, tsq[2], s2=EPS, op1=ALU.add)
        bfree[SB_ - 1] = [t1, t2]
        t_rq3 = G(lambda e: e.tensor_tensor(rq3[:, :], mq3[:, :], cst[:, C_HALF:C_HALF + 8], ALU.pow), t1, t2, t_c)

        t_gq, t_gk = [None, None], [None, None]

        def keys(name, dst, scale, toks):
            u, wh, wl, wt = take(name, 0)
            whv, wlv = wh.rearrange("p (k n) -> p k n", k=8), wl.rearrange("p (k n) -> p k n", k=8)
            for i in range(2):
                b = mbank()
                t = prod_t(b, whv, wlv, slice(i * P, i * P + P), range(8), AH, AL, range(8), [wt] * 8)
                toks[i] = stt(dst[:, i, :], bank[b][:, :], scale, rb[:, :], ALU.mult, ALU.mult, t, t_rb)
                bfree[b] = [toks[i]]
                if name == "gk":
                    fill(2)
            pe_done[u] = t
        keys("gq", gq, GK ** -0.5, t_gq)

        o_tok = [None] * 8
        pieces = []
        t_qm, t_km, t_vm, t_krb = [None] * 4, [None] * 4, [None] * 4, [None]

        def angles():
            cw = cody_waite()
            trig = dg[:, :, :].rearrange("p q n -> p (q n)").rearrange("p (i q f) -> p i q f", i=8, q=4)
            t1 = V(lambda e: e.tensor_copy(posf[:, :], posi[:, :]), t_pos)
            ang, nn_, r0_, r1_, co, si, sc = (trig[:, i, :, :].rearrange("p q f -> p (q f)") for i in range(7))
            t2 = tt(trig[:, 0, :, :], posf[:, :, None].to_broadcast([P, 4, 16]),
                    cst[:, None, C_IF:C_IF + 16].to_broadcast([P, 4, 16]), ALU.mult, t1, t_c, *spread_free[0])
            M = 12582912.0
            t3 = ts(nn_, ang, 1.0 / TWO_PI, ALU.mult, t2, s2=M, op1=ALU.add)
            t3 = ts(nn_, nn_, M, ALU.subtract, t3)
            t = t3
            src = ang
            for i, c in enumerate(cw):
                dst = (r0_, r1_)[i % 2]
                t = stt(dst, nn_, -c, src, ALU.mult, ALU.add, t)
                src = dst
            PI_ = 3.1415925
            t = ts(r0_, src, PI_, ALU.min, t, s2=-PI_, op1=ALU.max)
            t_sin = act(si, r0_, ACT.Sin, t)
            t = ts(r1_, r0_, math.pi / 2, ALU.add, t)
            t = ts(sc, r1_, math.pi, ALU.is_gt, t, s2=TWO_PI, op1=ALU.mult)
            t = tt(r1_, r1_, sc, ALU.subtract, t)
            t = ts(r1_, r1_, PI_, ALU.min, t, s2=-PI_, op1=ALU.max)
            t_cos = act(co, r1_, ACT.Sin, t)
            return t_sin, t_cos

        trig = dg[:, :, :].rearrange("p q n -> p (q n)").rearrange("p (i q f) -> p i q f", i=8, q=4)
        rn = sb("rn", [P, 2, 32], F, mla)
        mn = sb("mn", [P, 2, 32], F, mla)
        t_ang, t_m, t_rn, t_z, tmp_t = [], [None, None], {}, {}, [None]

        gvf, gvf_t = gv[:, :, :].rearrange("p q n -> p (q n)"), [None, None]

        def squares(i, q, z, tz):
            k = q % 2
            o = gvf[:, 768 * k:768 * k + 768]
            t = act(o, z[:, q, :, :].rearrange("p h d -> p (h d)"), ACT.Square, *tz, gvf_t[k])
            c = slice(8 * q, 8 * q + 8)
            t = V(lambda e: e.tensor_reduce(mn[:, i, c], o.rearrange("p (a d) -> p a d", d=MQ), AX.X, ALU.add), t)
            gvf_t[k] = t
            t1 = ts(mn[:, i, c], mn[:, i, c], 1.0 / MQ, ALU.mult, t, s2=EPS, op1=ALU.add)
            t_rn[i, q] = G(lambda e: e.tensor_tensor(rn[:, i, c], mn[:, i, c], cst[:, C_HALF:C_HALF + 8], ALU.pow), t1, t_c)

        def gains(i, q, z):
            c = slice(8 * q, 8 * q + 8)
            t = tt(z[:, q], z[:, q], rn[:, i, c][:, :, None].to_broadcast([P, 8, MQ]), ALU.mult, t_rn[i, q])
            t_z[i] = G(lambda e: e.tensor_tensor(z[:, q], z[:, q], row[:, None, MQ * i:MQ * i + MQ].to_broadcast([P, 8, MQ]),
                                                 ALU.mult), t, t_row)

        tv = tmp[:, 0:2048].rearrange("p (i q h f) -> p i q h f", i=4, q=4, h=8)

        def rope1(i, z):
            x1, x2 = z[:, :, :, MN:MN + 16], z[:, :, :, MN + 16:MQ]
            cb = trig[:, 4, :, None, :].to_broadcast([P, 4, 8, 16])
            sb_ = trig[:, 5, :, None, :].to_broadcast([P, 4, 8, 16])
            t_z[i, 0] = [tt(tv[:, 0], x1, cb, ALU.mult, t_z[i], *t_ang, *tmp_t[0]), tt(tv[:, 1], x2, sb_, ALU.mult, t_z[i]),
                         tt(tv[:, 2], x2, cb, ALU.mult, t_z[i]), tt(tv[:, 3], x1, sb_, ALU.mult, t_z[i])]

        def rope2(i, z):
            x1, x2 = z[:, :, :, MN:MN + 16], z[:, :, :, MN + 16:MQ]
            te = tt(x1, tv[:, 0], tv[:, 1], ALU.subtract, *t_z[i, 0])
            t_m[i] = tt(x2, tv[:, 2], tv[:, 3], ALU.add, *t_z[i, 0], te)
            tmp_t[0] = [t_m[i]]

        for i, z in enumerate((qm, km)):
            for q in range(NT):
                pieces.append(lambda i=i, q=q, z=z: squares(i, q, z, [t_km[q], *t_krb] if i else [t_qm[q]]))
                if q > 0:
                    pieces.append(lambda i=i, q=q, z=z: gains(i, q - 1, z))
            pieces.append(lambda i=i, z=z: gains(i, 3, z))
            if i == 0:
                pieces.append(lambda: t_ang.extend(angles()))
            pieces.append(lambda i=i, z=z: rope1(i, z))
            pieces.append(lambda i=i, z=z: rope2(i, z))

        def fill(n):
            for _ in range(n):
                if pieces:
                    pieces.pop(0)()

        u, wh, wl, wt = take("uq", 0)
        whv, wlv = wh.rearrange("p (k n) -> p k n", k=2), wl.rearrange("p (k n) -> p k n", k=2)
        for q in range(NT):
            for n in range(2):
                b = mbank()
                for k in range(2):
                    ah, al = cqH[:, k, q * P:(q + 1) * P], cqL[:, k, q * P:(q + 1) * P]
                    cs = slice(384 * n, 384 * n + 384)
                    o = bank[b][:, 0:384]
                    mm(o, ah, whv[:, k, cs], k == 0, False, *wt, *t_cq[0], *t_cq[1], *(bfree[b] if k == 0 else []))
                    mm(o, ah, wlv[:, k, cs], False, False)
                    t = mm(o, al, whv[:, k, cs], False, k == 1, count=k == 1)
                t_qm[q] = ts(qm[:, q, 4 * n:4 * n + 4, :], bank[b][:, 0:384].rearrange("p (h d) -> p h d", h=4),
                             rq3[:, q:q + 1], ALU.mult, t, t_rq3)
                bfree[b] = [t_qm[q]]
        pe_done[u] = t
        u, wh, wl, wt = take("ukv", 0)
        for q in range(NT):
            for n in range(2):
                b = mbank()
                ah, al = cqH[:, 2, q * P:(q + 1) * P], cqL[:, 2, q * P:(q + 1) * P]
                cs = slice(512 * n, 512 * n + 512)
                mm(bank[b][:, :], ah, wh[:, cs], True, False, *wt, *t_cq[2], *bfree[b])
                mm(bank[b][:, :], ah, wl[:, cs], False, False)
                t = mm(bank[b][:, :], al, wh[:, cs], False, True, count=True)
                if n == 0:
                    t_km[q] = ts(km[:, q, :, 0:MN], bank[b][:, :].rearrange("p (h d) -> p h d", h=8),
                                 rq3[:, 4 + q:5 + q], ALU.mult, t, t_rq3)
                    bfree[b] = [t_km[q]]
                    fill(1)
                else:
                    t_vm[q] = act(vm[:, q, :], bank[b][:, :], ACT.Copy, t, t_rq3, scale=rq3[:, 4 + q:5 + q])
                    bfree[b] = [t_vm[q]]
                    fill(1)
        pe_done[u] = t
        b = 4
        for q in range(NT):
            t = T(lambda e, q=q: e.transpose(bank[4][:, 32 * q:32 * q + 32], low[32:64, q * P:(q + 1) * P],
                                             ident[32:64, 32:64]), tgl, t_c, *(bfree[4] if q == 0 else []), count=q == 3)
        t_krb[0] = act(km[:, :, :, MN:MQ],
                    bank[4][:, 0:128].rearrange("p (q o d) -> p q o d", q=4, o=1).to_broadcast([P, 4, 8, 32]), ACT.Copy, t)
        bfree[4] = [t_krb[0]]
        tmp_t[0] = [t]
        gate_t, gx_t = [None, None], []
        for j in range(2):
            gx, ge, b = (ctmp[0], sq[0])[j], (ctmp[1], sq[1])[j], 5 + j
            t = mm(bank[b][:, :], gw2[:, j * P:(j + 1) * P], glow, True, True, tgl, t_g, *bfree[b], count=True)
            t1 = ts(gx[:, :], bank[b][:, :], par[:, PC_GB + j:PC_GB + j + 1], ALU.add, t, t_p, *(cfree[0], sqr[0])[j])
            bfree[b] = [t1]
            gx_t.append((gx, ge, t1, act(ge[:, :], gx[:, :], ACT.Abs, t1, *(cfree[1], sqr[1])[j])))
        gx_t = [(gx, ge, t1, act(ge[:, :], ge[:, :], ACT.Exp, t2, scale=-1.0)) for gx, ge, t1, t2 in gx_t]
        gx_t = [(gx, ge, t1, act(ge[:, :], ge[:, :], ACT.Ln, t2, bias=1.0)) for gx, ge, t1, t2 in gx_t]
        for j, (gx, ge, t1, t2) in enumerate(gx_t):
            gate_t[j] = stt(gx[:, :], gx[:, :], 0.0, ge[:, :], ALU.min, ALU.subtract, t2, t1)
        sqr[1] = [gate_t[1]]
        keys("gk", gk, 1.0, t_gk)
        t_sil = [None] * 4
        for i in range(2):
            u, wh, wl, wt = take("gr", i)
            whv, wlv = wh.rearrange("p (k n) -> p k n", k=8), wl.rearrange("p (k n) -> p k n", k=8)
            for c in range(2):
                b = mbank()
                h = 2 * i + c
                t = prod_t(b, whv, wlv, slice(c * P, c * P + P), range(8), AH, AL, range(8), [wt] * 8)
                t1 = tt(gsil[:, h, :], bank[b][:, :], rb[:, :], ALU.mult, t, t_rb)
                bfree[b] = [t1]
                t_sil[h] = act(gsil[:, h, :], gsil[:, h, :], ACT.Silu, t1)
                fill(2)
            pe_done[u] = t
        
        bs = [mbank() for _ in range(NT)]
        for hlf in range(2):
            u, wh, wl, wt = take("gv", hlf)
            whv, wlv = wh.rearrange("p (k n) -> p k n", k=4), wl.rearrange("p (k n) -> p k n", k=4)
            for q in range(NT):
                for k in range(4):
                    kk = 4 * hlf + k
                    o = bank[bs[q]][:, :]
                    st = hlf == 0 and k == 0
                    en = k == 3
                    ah, al = AH[:, kk, q * P:(q + 1) * P], AL[:, kk, q * P:(q + 1) * P]
                    mm(o, ah, whv[:, k, :], st, False, *wt, *(bfree[bs[q]] if st else []))
                    mm(o, ah, wlv[:, k, :], False, False)
                    t = mm(o, al, whv[:, k, :], False, en and hlf == 1, count=en)
                fill(1)
                if hlf == 1:
                    t_gv = ts(gv[:, q, :], bank[bs[q]][:, :], r4[:, q:q + 1], ALU.mult, t, t_r4)
                    bfree[bs[q]] = [t_gv]
            pe_done[u] = t
        g_done = t
        fill(len(pieces))

        gb = over("gb", [P, 2, S], AL_at)
        t_b = [None, None]
        for j in range(2):
            gx = (ctmp[0], sq[0])[j]
            t_b[j] = V(lambda e, j=j, gx=gx: e.tensor_tensor_scan(gb[:, j, :], cst[:, C_SCAN:C_SCAN + S], gx[:, :], 0.0,
                                                                  ALU.mult, ALU.add), gate_t[j], t_c, g_done)
        sqr[0] = [t_b[1]]

        def attention(nh, fetch, v, t_v, scale, bias, pb, obanks, dst, at, sbanks=4, side=()):
            ptb = t2s + sq
            st = sb(f"st{nh}", [P, 6, 4], F, at)
            units_ = [(p, q) for p in range(nh // 2) for q in range(NT)]
            pfree = [[] for _ in range(6)]
            ptfree = [list(t2f_prev), list(t2f_prev), list(sqr[0]), list(sqr[1])]
            stf = [[] for _ in range(6)]
            dfree = [list(spread_free[0]) for _ in range(4)]
            p_t, d_t, pt_t, out = {}, {}, {}, {}

            def scores(u):
                p, q = units_[u]
                n = (q + 1) * P
                for hh in range(2):
                    h, b, k = 2 * p + hh, (2 * u + hh) % sbanks, 2 * (u % 3) + hh
                    ql, kr_, tqk, used = fetch(h, q)
                    t = mm(bank[b][:, 0:n], ql, kr_[:, 0:n], True, True, *tqk, *bfree[b], count=bias is not None)
                    if bias is None:
                        t = mm(bank[b][:, n - P:n], cst[0:1, C_MA:C_MA + P], cst[0:1, C_MB:C_MB + P], False, True,
                               count=True, share=True)
                    used(t)
                    if bias is None:
                        t1 = V(lambda e, k=k, b=b: e.reduce_max(st[:, k, 0:1], bank[b][:, 0:n], AX.X), t, *stf[k])
                        t2 = ts(st[:, k, 1:2], st[:, k, 0:1], -scale, ALU.mult, t1)
                        t3 = act(pb[k][:, 0:n], bank[b][:, 0:n], ACT.Exp, t2, *pfree[k], bias=st[:, k, 1:2],
                                 scale=scale, accum_out=st[:, k, 2:3])
                        bfree[b] = [t3]
                    else:
                        gbuf, tg, gdone = bias(h)
                        t1 = V(lambda e, k=k, b=b, gbuf=gbuf: e.tensor_tensor_reduce(
                            out=pb[k][:, 0:n], in0=bank[b][:, 0:n], in1=gbuf[:, 512 - n:512], scale=scale,
                            scalar=-3.0e38, op0=ALU.add, op1=ALU.max, accum_out=st[:, k, 0:1]),
                            t, *tg, *pfree[k], *stf[k])
                        bfree[b] = [t1]
                        gdone(t1)
                        t2 = ts(st[:, k, 1:2], st[:, k, 0:1], -1.0, ALU.mult, t1)
                        t3 = act(pb[k][:, 0:n], pb[k][:, 0:n], ACT.Exp, t2, bias=st[:, k, 1:2],
                                 accum_out=st[:, k, 2:3])
                    p_t[u, hh] = t3

            def diag(u):
                for hh in range(2):
                    k, i = 2 * (u % 3) + hh, 2 * (u % 2) + hh
                    t = V(lambda e, k=k: e.reciprocal(st[:, k, 3:4], st[:, k, 2:3]), p_t[u, hh])
                    d_t[u, hh] = ts(dg[:, i, :], ident, st[:, k, 3:4], ALU.mult, t, t_c, *dfree[i])
                    stf[k] = [d_t[u, hh]]

            def turn(u):
                p, q = units_[u]
                n = (q + 1) * P
                for hh in range(2):
                    k, i, b = 2 * (u % 3) + hh, 2 * (u % 2) + hh, 4 + hh
                    for c in range(q + 1):
                        t = mm(bank[b][:, c * P:(c + 1) * P], pb[k][:, c * P:(c + 1) * P], dg[:, i, :], True, True,
                               p_t[u, hh], d_t[u, hh], *(bfree[b] if c == 0 else []), count=c == q, share=True)
                    pfree[k], dfree[i] = [t], [t]
                    pt_t[u, hh] = act(ptb[i][:, 0:n], bank[b][:, 0:n], ACT.Copy, t, *ptfree[i])
                    bfree[b] = [pt_t[u, hh]]

            def values(u):
                p, q = units_[u]
                b = obanks[p % len(obanks)]
                for c in range(q + 1):
                    for hh in range(2):
                        i, h = 2 * (u % 2) + hh, 2 * p + hh
                        t = mm(bank[b][64 * hh:64 * hh + 64, q * P:(q + 1) * P], v[:, c, h * 64:(h + 1) * 64],
                               ptb[i][:, c * P:(c + 1) * P], c == 0, c == q, pt_t[u, hh], *t_v,
                               *(bfree[b] if c == 0 and q == 0 else []), count=c == q, share=True)
                        if c == q:
                            ptfree[i] = [t]
                if q == 3:
                    m, w = dst(p)
                    t1 = act(AH[:, m, :], bank[b][:, :], ACT.Copy, t, *w)
                    t2 = tt(AL[:, m, :], bank[b][:, :], AH[:, m, :].bitcast(F), ALU.subtract, t1, *w)
                    bfree[b] = [t2]
                    out[m] = [t1, t2]
                return t

            n = len(units_)
            for i in range(n + 3):
                if 0 <= i - 2 < len(side):
                    side[i - 2][1]()
                if i < n:
                    scores(i)
                if 0 <= i - 1 < n:
                    diag(i - 1)
                if 0 <= i - 3 < n:
                    t = values(i - 3)
                if 0 <= i - 2 < n:
                    turn(i - 2)
                if 0 <= i - 1 < len(side):
                    side[i - 1][0]()
            spread_free[0] = dfree[0] + dfree[2] + dfree[1] + dfree[3]
            sqr[0], sqr[1] = list(ptfree[2]), list(ptfree[3])
            t2f_prev[:] = ptfree[0] + ptfree[1]
            return out, t

        qT = [over(f"qT{i}", [P, S], AH_at + 4 * S * i) for i in range(2)]
        kT = [over(f"kT{i}", [P, S], AH_at + 4 * S * (2 + i)) for i in range(2)]
        qk_t = {}
        qk_free = [[g_done], [g_done]]

        def fetch1(h, q):
            k = h % 2
            if h not in qk_t:
                for g in (h, h + 1):
                    qk_t[g] = []
                    for z, dd_, tz, b in ((qm, qT[g % 2], t_m[0], 3), (km, kT[g % 2], t_m[1], 7)):
                        for c in range(NT):
                            t = tr(bank[b][0:MQ, c * P:(c + 1) * P], z[:, c, g, :], tz, t_c,
                                   *(bfree[b] if c == 0 else []), count=c == 3)
                        if b == 3:
                            t1 = act(dd_[0:MQ, :], bank[b][0:MQ, :], ACT.Copy, t, *qk_free[g % 2])
                        else:
                            t1 = V(lambda e, d=dd_, b=b: e.tensor_copy(d[0:MQ, :], bank[b][0:MQ, :]), t, *qk_free[g % 2])
                        bfree[b] = [t1]
                        qk_t[g].append(t1)
                qm_read[:] = [t]
            return qT[k][0:MQ, q * P:(q + 1) * P], kT[k][0:MQ, :], qk_t[h], lambda t: qk_free.__setitem__(k, [t])

        slot = (cur[0] - 1) % NW
        AT = over("AT", [P, GH, S], W_at + slot * UE * 4)
        qt_ = over("qt_", [P, 2, S], W_at + (NW + slot) * UE * 4)
        kt_ = over("kt_", [P, 2, S], W_at + (NW + slot) * UE * 4 + 2 * S * 4)
        dd = over("dd", [P, 2, S], AL_at + 2 * S * 4)
        kd = over("kd", [P, 4, 256], qm_at)
        ST = over("ST", [P, 2, 7, P], qm_at + 1024 * 4)
        t_at0 = G(lambda e: e.memset(AT[:, :, :], 0.0), g_done)
        f_qk = [[g_done], [g_done]]
        t_at = [t_at0] * GH

        t_kt0 = G(lambda e: e.memset(kt_[:, :, :], 0.0), g_done)

        def decay(lv, j):
            if lv == 0:
                return
            B = LEVELS[lv - 1]
            bv = gb[:, j, :].rearrange("p (n w) -> p n w", w=2 * B)
            dv = dd[:, j, :].rearrange("p (n w) -> p n w", w=2 * B)
            ref = bv[:, :, B - 1:B].to_broadcast([P, S // (2 * B), B])
            t1 = tt(dv[:, :, B:2 * B], bv[:, :, B:2 * B], ref, ALU.subtract, t_b[j], *f_dd[j])
            t2 = tt(dv[:, :, 0:B], ref, bv[:, :, 0:B], ALU.subtract, t_b[j], *f_dd[j])
            f_dd[j] = []
            t_dd[j] = act(dd[:, j, :], dd[:, j, :], ACT.Exp, t1, t2, scale=1.0 / 16)

        def decayed(lv, j):
            if lv == 0:
                ready[lv, j] = [t_gq[j], t_gk[j]]
                return
            B = LEVELS[lv - 1]
            half = lambda z: z.rearrange("p (n w) -> p n w", w=2 * B)
            dv = half(dd[:, j, :])
            t4 = tt(qt_[:, j, 0:256].rearrange("p (n w) -> p n w", w=B), half(gq[:, j, :])[:, :, B:2 * B],
                    dv[:, :, B:2 * B], ALU.mult, t_dd[j], *f_qk[j])
            t5 = tt(half(kt_[:, j, :])[:, :, 0:B], half(gk[:, j, :])[:, :, 0:B], dv[:, :, 0:B], ALU.mult, t_dd[j],
                    *f_qk[j], t_kt0)
            ready[lv, j] = [t4, t5]

        def level(lv, j):
            ks, qs = (kt_, qt_) if lv else (gk, gq)
            n = 64 if lv else P
            for q in range(NT):
                for hh in range(2):
                    b = (7, 3)[hh]
                    rows = slice(64 * hh, 64 * hh + 64)
                    cs = slice(q * n, (q + 1) * n)
                    t = mm(bank[b][:, cs], ks[rows, j, q * P:(q + 1) * P], qs[rows, j, cs], True, True, *ready[lv, j],
                           *(bfree[b] if q == 0 else []), count=q == NT - 1, share=True)
                    t_lv[hh] = t
            bfree[7] = bfree[3] = None
            if lv > 0:
                f_qk[j] = [t]

        def keep(lv, j):
            for hh in range(2):
                b, h = (7, 3)[hh], 2 * j + hh
                if lv == 0:
                    m = msk[:, 0, None, :].to_broadcast([P, 4, P])
                    o = AT[:, h, :].rearrange("p (q n) -> p q n", q=4)
                    d = bank[b][:, :].rearrange("p (q n) -> p q n", q=4)
                else:
                    B = LEVELS[lv - 1]
                    m = msk[:, lv, :].rearrange("p (n w) -> p n w", w=2 * B)[:, None, :, B:2 * B]
                    m = m.to_broadcast([P, 4, 64 // B, B])
                    o = AT[:, h, :].rearrange("p (q n w) -> p q n w", q=4, w=2 * B)[:, :, :, B:2 * B]
                    d = bank[b][:, 0:256].rearrange("p (q n w) -> p q n w", q=4, w=B)
                t_at[h] = V(lambda e, o=o, m=m, d=d: e.copy_predicated(o, m, d), t_lv[hh], t_at[h], t_msk)
                bfree[b] = [t_at[h]]

        ready, t_lv, t_dd, f_dd = {}, [None, None], [None, None], [[g_done], [g_done]]
        t_k3 = [None] * 2
        t_kd, t_qe, t_el = [None] * 2, [None] * 2, [None] * 2
        def between(j):
            bv = gb[:, j, :].rearrange("p (n w) -> p n w", w=64)
            dv = dd[:, j, :].rearrange("p (n w) -> p n w", w=64)
            last = bv[:, :, 63:64]
            t_el[j] = act(el[:, j, :], last.rearrange("p n o -> p (n o)"), ACT.Exp, t_b[j], scale=1.0 / 16)
            t1 = tt(dv, last.to_broadcast([P, 8, 64]), bv, ALU.subtract, t_b[j], *f_qk[j])
            t2 = act(dd[:, j, :], dd[:, j, :], ACT.Exp, t1, scale=1.0 / 16)
            t3 = tt(kt_[:, j, :], gk[:, j, :], dd[:, j, :], ALU.mult, t2, *f_qk[j])
            t4 = act(dd[:, j, :], gb[:, j, :], ACT.Exp, t3, scale=1.0 / 16)
            t_qe[j] = tt(qt_[:, j, :], gq[:, j, :], dd[:, j, :], ALU.mult, t4, *f_qk[j])
            t_k3[j] = t3

        def turn_keys(j):
            b, t3 = 7, t_k3[j]
            for q in range(NT):
                t = tr(bank[b][:, q * P:(q + 1) * P], kt_[:, j, q * P:(q + 1) * P], t3, t_c,
                       *(bfree[b] if q == 0 else []), count=q == NT - 1)
            t_kd[j] = act(kd[:, :, j * P:(j + 1) * P], bank[b][:, :].rearrange("p (q n) -> p q n", q=4), ACT.Copy, t, *qm_read)
            bfree[b] = [t_kd[j]]

        items = [(lv, j) for lv in range(7) for j in range(2)]

        def item(i):
            if i < len(items):
                level(*items[i])
            if i + 1 < len(items):
                decayed(*items[i + 1])
            if i + 2 < len(items):
                decay(*items[i + 2])

        decayed(*items[0])
        side = [(lambda i=i: item(i), lambda i=i: keep(*items[i])) for i in range(len(items))]
        nothing = lambda: None
        side[-1] = (lambda: (item(13), between(0)), side[-1][1])
        side += [(lambda: (turn_keys(0), between(1)), nothing), (lambda: turn_keys(1), nothing)]
        qm_read = []

        t2f_prev = [t_b[1]]
        pb1 = [tmp[:, i * 512:(i + 1) * 512] for i in range(6)]
        out1, t_o = attention(MH, fetch1, vm, t_vm, MQ ** -0.5, None, pb1, [6], lambda p: (4 + p, [g_done]), mla, 3, side)
        for m in out1:
            o_tok[m] = out1[m]
        fence = [t_o] + [z for m in out1 for z in out1[m]]
        t_st = [None, None]
        for j in range(2):
            tu = {}
            for c in [0, 2, 4, 6, 1, 3, 5]:
                b = 4 + 2 * j + c % 2
                r0 = 64 * (c % 2)
                for hh in range(2):
                    o = bank[b][64 * hh:64 * hh + 64, (c // 2) * P:(c // 2 + 1) * P]
                    h = 2 * j + hh
                    tu[c] = mm(o, kd[r0:r0 + 64, c // 2, j * P + 64 * hh:j * P + 64 * hh + 64],
                               gv[r0:r0 + 64, c // 2, h * GV:(h + 1) * GV], True, True, t_kd[j], t_gv,
                               *(bfree[b] if c < 2 else []), count=True, share=True)
            for c in range(7):
                b = 4 + 2 * j + c % 2
                o = bank[b][:, (c // 2) * P:(c // 2 + 1) * P]
                w = tu[6] if c % 2 == 0 else tu[5]
                if c == 0:
                    t_st[j] = V(lambda e, j=j, o=o: e.tensor_copy(ST[:, j, 0, :], o), w)
                else:
                    t_st[j] = stt(ST[:, j, c, :], ST[:, j, c - 1, :], el[:, j, c:c + 1], o, ALU.mult, ALU.add,
                                  w, t_st[j], t_el[j])
                bfree[b] = [t_st[j]]
        ogs = AT
        t_og, tgs = [None] * 4, None
        SG = 7
        wtiles, wus, wts = [], [], []
        main[0] = 0
        for i in range(2):
            u, wh, wl, wt = take("wout", i, False)
            w8 = (wh.rearrange("p (k n) -> p k n", k=8), wl.rearrange("p (k n) -> p k n", k=8))
            wtiles += [(mbank(), *w8, slice(c * P, c * P + P), P) for c in range(2)]
            wus.append(u)
            wts += wt
        wwait = {k: wts + o_tok[k] for k in range(4, 8)}

        def out_sums(h):
            k = h % 2
            for q in range(NT):
                t = mm(bank[SG][:, 4 * h + q:4 * h + q + 1], sq[k][:, q * P:(q + 1) * P], ones[:, 0:1], True, True,
                       t_sq[h], *(bfree[SG] if h == 0 else []), count=q == NT - 1, share=True)
            sqr[k] = [t]
            return t

        t_sq = {}
        for j in range(2):
            ob = (4, 5) if j == 0 else (6, 4)
            for hh in range(2):
                h, b = 2 * j + hh, ob[hh]
                for q in range(NT):
                    cs = slice(q * P, (q + 1) * P)
                    mm(bank[b][:, cs], gv[:, q, h * GV:(h + 1) * GV], AT[:, h, cs], q == 0, True, t_at[h], t_gv,
                       *(bfree[b] if q == 0 else []), share=True)
            for c in range(1, 8):
                for hh in range(2):
                    b = ob[hh]
                    rows = slice(64 * hh, 64 * hh + 64)
                    cs = slice(c * 64, c * 64 + 64)
                    t = mm(bank[b][:, cs], ST[rows, j, c - 1, :], qt_[rows, j, cs], False, True, t_st[j], t_qe[j],
                           count=c == 7, share=True)
                    if c == 7:
                        h = 2 * j + hh
                        t_og[h] = act(ogs[:, h, :], bank[b][:, :], ACT.Copy, t)
                        bfree[b] = [t_og[h]]
            for hh in range(2):
                h = 2 * j + hh
                if j > 0:
                    out_sums(h - 2)
                t_sq[h] = act(sq[hh][:, :], ogs[:, h, :], ACT.Square, t_og[h], *sqr[hh])
        group(wtiles, [4], wwait)
        out_sums(2)
        tgs = out_sums(3)
        t1 = ts(mg[:, :], bank[SG][:, 0:16], 1.0 / GV, ALU.mult, tgs, s2=EPS, op1=ALU.add)
        bfree[SG] = [t1]
        t_rg = G(lambda e: e.tensor_tensor(rg[:, :], mg[:, :], cst[:, C_HALF:C_HALF + 16], ALU.pow), t1, t_c)
        group(wtiles, [5], wwait)
        t_sp = [spread(rg[:, 0:4], 4, [t_rg])]
        for h in range(GH):
            b = 4 + h % 2
            t = t_sp[h]
            if h < 3:
                t_sp.append(spread(rg[:, 4 * h + 4:4 * h + 8], 4 + (h + 1) % 2, [t_rg]))
            if h < 2:
                group(wtiles, [6 + h], wwait)
            t1 = stt(ogs[:, h, :], ogs[:, h, :], par[:, PC_GN:PC_GN + 1], bank[b][:, :], ALU.mult, ALU.mult, t, t_og[h])
            bfree[b] = [t1]
            t2 = tt(ogs[:, h, :], ogs[:, h, :], gsil[:, h, :], ALU.mult, t1, t_sil[h])
            t3 = act(AH[:, h, :], ogs[:, h, :], ACT.Copy, t2, *fence)
            t4 = tt(AL[:, h, :], ogs[:, h, :], AH[:, h, :].bitcast(F), ALU.subtract, t3)
            o_tok[h] = [t3, t4]
        split(wus[0] + 2, *[z for h in range(GH) for z in o_tok[h]])
        wdone = group(wtiles, range(4), {k: o_tok[k] for k in range(4)})
        for u in wus:
            pe_done[u] = wdone[3]
        split(wus[1] + 2)
        fence = [o_tok[h][i] for h in range(4) for i in range(2)] + [tgs, t_kd[1], t, t_rg]
        mla.close()
        ph1.close()


        def project_residual(name, act_tok, gcol, done=()):
            toks = [None] * 8

            def units_of(i0):
                tiles, us, wts = [], [], []
                for i in (i0, i0 + 1):
                    u, wh, wl, wt = take(name, i, i == i0)
                    w8 = (wh.rearrange("p (k n) -> p k n", k=8), wl.rearrange("p (k n) -> p k n", k=8))
                    tiles += [(mbank(), *w8, slice(c * P, c * P + P), P) for c in range(2)]
                    us.append(u)
                    wts.append(wt)
                return tiles, us, wts

            def add(m, b, t):
                x_t[m] = tt(X[:, m, :], X[:, m, :], bank[b][:, :], ALU.add, t, *x_t_w(m))
                bfree[b] = [x_t[m]]
                x_read[m] = [add_square(X[:, m, :], m == 0, x_t[m], eng="gpsimd")]

            def parts(c, *w):
                g = par[:, gcol + c:gcol + c + 1]
                t1 = act(AH[:, c, :], X[:, c, :], ACT.Copy, x_t[c], t_p, *w, scale=g)
                t2 = stt(AL[:, c, :], X[:, c, :], g, AH[:, c, :].bitcast(F), ALU.mult, ALU.subtract, t1)
                x_read[c] = x_read[c] + [t1, t2]
                toks[c] = [t1, t2]

            if not done:
                tiles, us, wts = units_of(0)
                t = group(tiles[0:2], range(4), {k: wts[0] + act_tok[k] for k in range(4)})
                group(tiles[2:4], range(4), {k: wts[1] for k in range(4)})
                t = group(tiles, range(4, 8), {k: act_tok[k] for k in range(4, 8)})
                for u in us:
                    pe_done[u] = t[3]
                split(us[1] + 2)
                done = [(tiles[i][0], t[i]) for i in range(4)]
            for m in range(4):
                add(m, *done[m])
            tiles, us, wts = units_of(2)
            group(tiles[0:2], range(4), [wts[0]] * 4)
            group(tiles[2:4], range(4), [wts[1]] * 4)
            for c in range(4):
                parts(c, chunk_done[c])
            t = group(tiles, range(4, 8), [[]] * 8)
            for u in us:
                pe_done[u] = t[3]
            for m in range(4, 8):
                add(m, tiles[m - 4][0], t[m - 4])
                if m > 4:
                    parts(m - 1, t[3])
            parts(7, t[3])
            split(us[1] + 2)
            return toks

        x_t = [None] * 8
        x_read = [[] for _ in range(8)]

        def x_t_w(m):
            return [x_t[m], *x_read[m]]

        a_free = [[] for _ in range(8)]
        main[0], ring[0] = 4, 7
        xk = project_residual("wout", o_tok, PC_MLP, [(wtiles[i][0], wdone[i]) for i in range(4)])
        stage[0] = 0

        hid = ExitStack()
        ctx.enter_context(hid)
        NH = 10
        HH = [sb(f"HH{i}", [P, S], R, hid) for i in range(NH)]
        HL = [sb(f"HL{i}", [P, S], R, hid) for i in range(NH)]
        hfree = [list(fence) for _ in range(NH)]
        t1s = [sb(f"t1s{i}", [P, S + 2], F, hid) for i in range(2)]
        t1f, t2f = [list(fence), list(fence)], [list(fence), list(fence)]
        h_t = {}

        def up(i):
            u, wh, wl, wt = take("up", i)
            whv, wlv = wh.rearrange("p (k n) -> p k n", k=8), wl.rearrange("p (k n) -> p k n", k=8)

            def rest(m, b, t):
                k, s = m % 2, m % NH
                t1 = stt(t1s[k][:, 0:S], bank[b][:, :], 0.0, rb[:, :], ALU.max, ALU.mult, t, t_r[1], *t1f[k])
                bfree[b] = [t1]
                rb_free[0] = [t1]
                t2 = act(t2s[k][:, :], t1s[k][:, 0:S], ACT.Square, t1, *t2f[k])
                t1f[k] = [t2]
                t3 = act(HH[s][:, :], t2s[k][:, :], ACT.Copy, t2, *hfree[s])
                t4 = tt(HL[s][:, :], t2s[k][:, :], HH[s][:, :].bitcast(F), ALU.subtract, t3)
                t2f[k] = [t4]
                h_t[m] = [t3, t4]

            tiles = [(mbank(), whv, wlv, slice(c * P, c * P + P), P) for c in range(2)]
            w = [wt + xk[k] for k in range(8)]
            if i == 0:
                group(tiles, range(7), w)
            for c in range(2):
                t = group(tiles[c:c + 1], [7] if i == 0 else range(8), w)[0]
                tile_done(lambda m=2 * i + c, b=tiles[c][0], t=t: rest(m, b, t))
            pe_done[u] = t
            return t

        def down(name, g, base, kc, gcol=None, a_done=None, final=False):
            toks = [None] * 8
            for i in range(4):
                u, wh, wl, wt = take(name, 4 * g + i)
                whv, wlv = wh.rearrange("p (k n) -> p k n", k=kc), wl.rearrange("p (k n) -> p k n", k=kc)
                for c in range(2):
                    m = 2 * i + c
                    b = mbank()
                    for k in range(kc):
                        s = (base + k) % NH
                        a = whv[:, k, c * P:(c + 1) * P]
                        mm(bank[b][:, :], a, HH[s][:, :], k == 0, False, *wt, *h_t[base + k],
                           *(bfree[b] if k == 0 else []))
                        mm(bank[b][:, :], a, HL[s][:, :], False, False)
                        t = mm(bank[b][:, :], wlv[:, k, c * P:(c + 1) * P], HH[s][:, :], False, k == kc - 1,
                               count=k == kc - 1)
                    x_t[m] = tt(X[:, m, :], X[:, m, :], bank[b][:, :], ALU.add, t, *x_t_w(m))
                    bfree[b] = [x_t[m]]
                    if final:
                        store(m)
                    if gcol is not None:
                        t1 = add_square(X[:, m, :], m == 0, x_t[m])
                        a_free[m] = [a_done]
                        toks[m] = prep(m, gcol, [x_t[m]])
                        x_read[m] = [t1, toks[m][1]]
                pe_done[u] = t
            for k in range(kc):
                hfree[(base + k) % NH] = [t]
            return t, toks

        ple = ExitStack()
        ctx.enter_context(ple)
        pe_x = sb("pe_x", [P, 2, S], F, ple)
        pH = sb("pH", [P, 2, S], R, ple)
        pL = sb("pL", [P, 2, S], R, ple)
        pj = sb("pj", [P, 8, S], F, ple)
        s_pe = newsem()
        t_pe = pr.dma("gpsimd", pe_x[:, :, :], PT, s_pe, 16, fence)
        t_pH = act(pH[:, :, :], pe_x[:, :, :], ACT.Copy, t_pe, *fence)
        t_pL = tt(pL[:, :, :], pe_x[:, :, :], pH[:, :, :].bitcast(F), ALU.subtract, t_pH, *fence)
        up_last = None
        for g in range(5):
            if g < 4:
                up_last = up(4 * g)
            if g > 0:
                _, xk_ = down("down", g - 1, 8 * (g - 1), 8, PC_PLE if g == 4 else None, up_last)
            if g < 4:
                for i in range(1, 4):
                    up_last = up(4 * g + i)
        xk = xk_

        s_o = newsem()

        def store(m):
            pr.dma("sync", OUT[:, m, :], X[:, m, :], s_o, 16 * 8, [x_t[m]])

        u, wh, wl, wt = take("proj", 0)
        whv, wlv = wh.rearrange("p (k n) -> p k n", k=2), wl.rearrange("p (k n) -> p k n", k=2)
        t_pj = [None] * 8
        for m in range(8):
            b = mbank()
            t = prod_t(b, whv, wlv, slice(m * P, m * P + P), range(2), pH, pL, range(2), [wt + [t_pH, t_pL]] * 2)
            if m == 3:
                norm_r()
            if m == 5:
                norm_spread()
            t_pj[m] = act(pj[:, m, :], bank[b][:, :], ACT.Copy, t, *fence)
            bfree[b] = [t_pj[m]]
        pe_done[u] = t
        xh, behind = [None] * 8, []

        def add_gated(m, k, t2):
            t3 = tt(t2s[k][:, :], t2s[k][:, :], pj[:, m, :], ALU.mult, t2, t_pj[m])
            x_t[m] = tt(X[:, m, :], X[:, m, :], t2s[k][:, :], ALU.add, t3, *x_t_w(m))
            t2f[k] = [x_t[m]]
            tq = add_square(X[:, m, :], m == 0, x_t[m], eng="gpsimd")
            g = par[:, PC_MIX + m:PC_MIX + m + 1]
            ta = ts(HH[m][:, :], X[:, m, :], g, ALU.mult, x_t[m], t_p, *hfree[m])
            tb = stt(HL[m][:, :], X[:, m, :], g, HH[m][:, :].bitcast(F), ALU.mult, ALU.subtract, ta)
            xh[m] = [ta, tb]
            x_read[m] = [tq, tb]

        for i in range(4):
            u, wh, wl, wt = take("pg", i)
            whv, wlv = wh.rearrange("p (k n) -> p k n", k=8), wl.rearrange("p (k n) -> p k n", k=8)
            for c in range(2):
                m = 2 * i + c
                k = m % 2
                b = mbank()
                t = prod_t(b, whv, wlv, slice(c * P, c * P + P), range(8), AH, AL, range(8),
                           [wt + xk[j] for j in range(8)])
                t1 = tt(t2s[k][:, :], bank[b][:, :], rb[:, :], ALU.mult, t, t_r[1], *t2f[k])
                bfree[b] = [t1]
                t2 = act(t2s[k][:, :], t2s[k][:, :], ACT.Sigmoid, t1, t_p, bias=par[:, PC_BPLE + m:PC_BPLE + m + 1])
                if behind:
                    behind.pop()()
                behind.append(lambda m=m, k=k, t2=t2: add_gated(m, k, t2))
            pe_done[u] = t
        behind.pop()()
        rb_free[0] = [t1]
        a_done = t
        fence = [t, x_t[7], xh[7][1], acc_t[0]]
        ple.close()

        pool = ExitStack()
        ctx.enter_context(pool)
        hp = [sb(f"hp{i}", [P, S + 16], F, pool) for i in range(4)]
        sa = [sb(f"sa{i}", [P, S + 16], F, pool) for i in range(4)]
        sb2 = [sb(f"sb2{i}", [P, S + 16], F, pool) for i in range(4)]
        bps = sb("bps", [P, 8], F, pool)
        tz = None
        for z in (*hp, *sa, *sb2):
            tz = G(lambda e, z=z: e.memset(z[:, 0:16], 0.0), *fence)
        hpf = [[tz]] * 4
        t_bps = tt(bps[:, :], par[:, PC_PB:PC_PB + 8], par[:, PC_PS:PC_PS + 8], ALU.mult, t_p, *fence)
        u, wh, wl, wt = take("pool", 0)
        whv, wlv = wh.rearrange("p (k n) -> p k n", k=8), wl.rearrange("p (k n) -> p k n", k=8)
        ORDER = [6, 7, 4, 5, 0, 1, 2, 3]
        pt, pbk, pbn = {}, {}, [0]

        def pool_in(m):
            g = m // 2
            b = pbk[m] = (4, 5, 6, 0, 1, 2, 3)[pbn[0] % 7]
            pbn[0] += 1
            for k in range(2):
                a = whv[:, 2 * g + k, (m % 2) * P:(m % 2) * P + P]
                h = 2 * g + k
                mm(bank[b][:, :], a, HH[h][:, :], k == 0, False, *wt, *xh[h], *(bfree[b] if k == 0 else []))
                mm(bank[b][:, :], a, HL[h][:, :], False, False)
                pt[m] = mm(bank[b][:, :], wlv[:, 2 * g + k, (m % 2) * P:(m % 2) * P + P], HH[h][:, :], False, k == 1, count=k == 1)

        def window(m, k, eng):
            w, b = WINDOWS[m // 2], pbk[m]
            t0 = tt(hp[k][:, 16:], bank[b][:, :], rb[:, :], ALU.mult, pt[m], t_r[1], *hpf[k])
            bfree[b] = [t0]
            rb_free[0] = [t0]
            src, t, step = hp[k], t0, 1
            for dst in (sa[k], sb2[k], sa[k], sb2[k]):
                if step >= w:
                    break
                t = pr(eng, lambda e, d=dst, s=src, st=step: e.tensor_tensor(d[:, 16:], s[:, 16:], s[:, 16 - st:16 - st + S],
                                                                          ALU.add), [t])
                src = dst
                step *= 2
            return src, t

        def finish(m, k, src, t):
            w = WINDOWS[m // 2]
            cnt = cst[:, C_CNT + 16 * (m // 2):C_CNT + 16 * (m // 2) + 16]
            ta = tt(src[:, 16:32], src[:, 16:32], cnt, ALU.mult, t)
            ta = tt(src[:, 16:32], src[:, 16:32], hp[k][:, 16:32], ALU.subtract, ta)
            tb = stt(src[:, 32:], src[:, 32:], 1.0 / w, hp[k][:, 32:], ALU.mult, ALU.subtract, t)
            j = m % 2
            t1 = act(t2s[j][:, :], src[:, 16:], ACT.Identity, ta, tb, t_bps, *t2f[j], bias=bps[:, m:m + 1],
                     scale=par[:, PC_PS + m:PC_PS + m + 1])
            hpf[k] = [t1]
            return t1

        def add_in(m, t1):
            j = m % 2
            x_t[m] = tt(X[:, m, :], X[:, m, :], t2s[j][:, :], ALU.add, t1, *x_t_w(m))
            t2f[j] = [x_t[m]]
            g = par[:, PC_FFN + m:PC_FFN + m + 1]
            t3 = act(AH[:, m, :], X[:, m, :], ACT.Copy, x_t[m], a_done, t_p, scale=g)
            return t3, add_square(X[:, m, :], m == ORDER[2], x_t[m], eng="gpsimd")

        def low_part(m, t3, tq):
            g = par[:, PC_FFN + m:PC_FFN + m + 1]
            t4 = stt(AL[:, m, :], X[:, m, :], g, AH[:, m, :].bitcast(F), ALU.mult, ALU.subtract, t3)
            xk[m] = [t3, t4]
            x_read[m] = [tq, t3, t4]

        xk = [None] * 8
        for m in ORDER[:4]:
            pool_in(m)
        norm_r()
        for m in ORDER[4:7]:
            pool_in(m)
        norm_spread()
        late = [(m, k, *window(m, k, "gpsimd")) for k, m in enumerate(ORDER[:2])]
        pool_in(ORDER[7])
        jobs = [(m, 2 + i % 2, None) for i, m in enumerate(ORDER[2:])] + late
        last = None
        for i, (m, k, *w) in enumerate(jobs):
            got = window(m, k, "vector") if w[0] is None else w
            if last:
                t34 = add_in(*last)
            t1 = finish(m, k, *got)
            if last:
                low_part(last[0], *t34)
            last = (m, t1)
        low_part(last[0], *add_in(*last))
        pe_done[u] = pt[ORDER[7]]
        fence = [pt[ORDER[7]], x_t[7], x_t[6], *xk[7], *xk[6], acc_t[0]]
        pool.close()

        cvs = [sb(f"cvs{i}", [P, S], F, hid) for i in range(2)]
        cvf = [[], []]
        tz1 = None
        for z in t1s:
            tz1 = G(lambda e, z=z: e.memset(z[:, 0:2], 0.0), *t1f[0], *t1f[1])
        t1f = [[tz1], [tz1]]

        def ffn(l, fence):
            for s in range(NH):
                hfree[s] = hfree[s] + list(fence)
            gp = {}
            pairs = [[4 * g + i for i in range((b - a) // 2)] for g, (a, b) in enumerate(GROUPS2)]

            def pair(j):
                def rest(name, m, c, b, t):
                    k, s = c, m % NH
                    if name == "gate":
                        a = t1s[k]
                        cw_ = [par[:, PC_CW + 66 * l + 22 * i + m:PC_CW + 66 * l + 22 * i + m + 1] for i in range(3)]
                        cb_ = par[:, PC_CB + 22 * l + m:PC_CB + 22 * l + m + 1]
                        t1 = tt(a[:, 2:], bank[b][:, :], rb[:, :], ALU.mult, t, t_r[1], *t1f[k])
                        bfree[b] = [t1]
                        t2 = ts(t2s[k][:, :], a[:, 0:S], cw_[0], ALU.mult, t1, *t2f[k])
                        t3 = stt(t2s[k][:, :], a[:, 1:S + 1], cw_[1], t2s[k][:, :], ALU.mult, ALU.add, t2)
                        t4 = stt(t2s[k][:, :], a[:, 2:S + 2], cw_[2], t2s[k][:, :], ALU.mult, ALU.add, t3)
                        t1f[k] = [t4]
                        gp[m] = act(t2s[k][:, :], t2s[k][:, :], ACT.Silu, t4, bias=cb_)
                    else:
                        t1 = tt(cvs[k][:, :], bank[b][:, :], rb[:, :], ALU.mult, t, t_r[1], *cvf[k])
                        bfree[b] = [t1]
                        rb_free[0] = [t1]
                        t2 = tt(cvs[k][:, :], cvs[k][:, :], t2s[k][:, :], ALU.mult, t1, gp[m])
                        t2f[k] = [t2]
                        t3 = act(HH[s][:, :], cvs[k][:, :], ACT.Copy, t2, *hfree[s])
                        t4 = tt(HL[s][:, :], cvs[k][:, :], HH[s][:, :].bitcast(F), ALU.subtract, t3)
                        cvf[k] = [t4]
                        h_t[m] = [t3, t4]

                if l == 0 and j == 0:
                    tiles, us, wts = [], [], []
                    for name in ("gate", "val"):
                        u, wh, wl, wt = take(f"{name}{l}", j, name == "gate")
                        w8 = (wh.rearrange("p (k n) -> p k n", k=8), wl.rearrange("p (k n) -> p k n", k=8))
                        tiles += [(mbank(), *w8, slice(c * P, c * P + P), P) for c in range(2)]
                        us.append(u)
                        wts += wt
                    t = group(tiles, ORDER[2:] + ORDER[:2], [wts + xk[k] for k in range(8)])
                    for u in us:
                        pe_done[u] = t[3]
                    norm_r()
                    held.append(us[1] + 2)
                    stage[0] = 2
                    for i in range(4):
                        pend.append(lambda a=(("gate", "val")[i // 2], i % 2, i % 2, tiles[i][0], t[i]): rest(*a))
                    return t[3]
                for name in ("gate", "val"):
                    first = j == 0 and name == "gate"
                    u, wh, wl, wt = take(f"{name}{l}", j)
                    whv, wlv = wh.rearrange("p (k n) -> p k n", k=8), wl.rearrange("p (k n) -> p k n", k=8)
                    tiles = [(mbank(), whv, wlv, slice(c * P, c * P + P), P) for c in range(2)]
                    w = [wt + xk[k] for k in range(8)]
                    if first:
                        group(tiles, range(7), w)
                    for c in range(2):
                        b = tiles[c][0]
                        t = group(tiles[c:c + 1], [7] if first else range(8), w)[0]
                        m = 2 * j + c
                        tile_done(lambda a=(name, m, c, b, t): rest(*a))
                    pe_done[u] = t
                return t

            for g in range(4):
                if g < 3:
                    last = pair(pairs[g][0])
                if g > 0:
                    a, b = GROUPS2[g - 1]
                    t, toks = down(f"fo{l}", g - 1, a, b - a, PC_MIX + 8 if g == 3 and l == 0 else None, last,
                                   g == 3 and l == 1)
                if g < 3:
                    for j in pairs[g][1:]:
                        last = pair(j)
            return toks, t

        main[0], ring[0] = 0, 7
        xk, t_dn = ffn(0, fence)
        main[0], ring[0] = 0, 4
        fence = [t_dn, x_t[7], acc_t[0]]
        hid.close()

        at2 = ExitStack()
        ctx.enter_context(at2)
        v2 = sb("v2", [P, 4, D], F, at2)
        qTa = sb("qTa", [P, 8, S], F, at2)
        kTa = sb("kTa", [P, 8, S], F, at2)
        qT2 = [qTa[:, i, :] for i in range(8)]
        kT2 = [kTa[:, i, :] for i in range(8)]
        NQ = 4
        qn = [sb(f"qn{i}", [P, 512], F, at2) for i in range(NQ)]
        qs_ = sb("qs_", [P, 512], F, at2)
        rn2 = sb("rn2", [P, NQ, 8], F, at2)
        mn2 = sb("mn2", [P, NQ, 8], F, at2)
        NG = 4
        Gb = [sb(f"Gb{i}", [P, 512], F, at2) for i in range(NG)]
        rel = v2[0:16, 1, 0:513]
        ev = v2[0:16, 0, 0:640]
        qz = sb("qz", [P, 4, P], F, at2)
        t_qz = G(lambda e: e.memset(qz[:, :, :], 0.0), *fence)
        EV = nc.dram_tensor("ev_scratch", (16, P, 640), F, kind="Internal")
        s_rel, s_ev, s_gb = newsem(), newsem(), [newsem() for _ in range(NG)]
        t_rel = pr.dma("gpsimd", rel, REL, s_rel, 16, fence)
        t1 = ts(ev[:, 0:255], rel[:, 0:1].to_broadcast([16, 255]), 8.0, ALU.mult, t_rel, *fence)
        t2 = ts(ev[:, 255:640], rel[:, 0:385], 8.0, ALU.mult, t_rel)
        t_ev = pr.dma("gpsimd", EV.ap(), ev[:, None, :].to_broadcast([16, P, 640]), s_ev, 16, [t1, t2])
        tms = None
        for i in range(NG):
            tms = G(lambda e, i=i: e.memset(Gb[i][0:64, 448:512], -1e30), *fence)
        qnf = [list(fence) for _ in range(NQ)]
        rnf = [[] for _ in range(NQ)]
        later = []

        scale_later = []

        def scale_z(now):
            while scale_later and scale_later[0][0] <= now - 1:
                s0, (blk, q, kx, t5) = scale_later.pop(0)
                z3 = qn[kx][:, :].rearrange("p (h d) -> p h d", d=64)
                t6 = tt(z3, z3, rn2[:, kx, :, None].to_broadcast([P, 8, 64]), ALU.mult, t5)
                rnf[kx] = [t6]
                g0 = 2 * MQ + (0 if blk < 2 else HD2)
                t7 = tt(z3, z3, row[:, None, g0:g0 + HD2].to_broadcast([P, 8, 64]), ALU.mult, t6, t_row)
                later.append((s0, (blk, q, kx, t7)))

        def advance(now):
            scale_z(now)
            while later and later[0][0] <= now - 3:
                turn_z(*later.pop(0)[1])

        def turn_z(blk, q, kx, t7):
            z = qn[kx]
            bb = 4 + kx
            for i in range(4):
                t = tr(bank[bb][:, i * P:(i + 1) * P], z[:, i * P:(i + 1) * P], t7, *(bfree[bb] if i == 0 else []),
                       count=i == 3)
            qnf[kx] = [t]
            d = (qTa if blk < 2 else kTa)[:, 4 * (blk % 2):4 * (blk % 2) + 4, q * P:(q + 1) * P]
            qk2[(blk, q)] = act(d, bank[bb][:, :].rearrange("p (i n) -> p i n", i=4), ACT.Copy, t, *fence)
            bfree[bb] = [qk2[(blk, q)]]

        qk2 = {}
        tqs = list(fence)
        t_v2 = []
        cnt_b, step = 0, 0
        for blk in range(6):
            bs = [mbank() for _ in range(NT)]
            for hlf in range(2):
                scale_z(step + 1)
                u, wh, wl, wt = take("qkv", 2 * blk + hlf)
                whv, wlv = wh.rearrange("p (k n) -> p k n", k=4), wl.rearrange("p (k n) -> p k n", k=4)
                for q in range(NT):
                    for k in range(4):
                        kk = 4 * hlf + k
                        o = bank[bs[q]][:, :]
                        st = hlf == 0 and k == 0
                        ah, al = AH[:, kk, q * P:(q + 1) * P], AL[:, kk, q * P:(q + 1) * P]
                        mm(o, ah, whv[:, k, :], st, False, *wt, *xk[kk], *(bfree[bs[q]] if st else []))
                        mm(o, ah, wlv[:, k, :], False, False)
                        t = mm(o, al, whv[:, k, :], False, k == 3 and hlf == 1, count=k == 3)
                    step += 1
                    if step == 2:
                        norm_r()
                        t_r4 = t_r[0]
                    if hlf == 0:
                        advance(step)
                        continue
                    if blk >= 4:
                        tv = act(v2[:, q, (blk - 4) * 512:(blk - 3) * 512], bank[bs[q]][:, :], ACT.Copy, t, t_r4, t_ev, *fence,
                                 scale=r4[:, q:q + 1])
                        bfree[bs[q]] = [tv]
                        t_v2.append(tv)
                        advance(step)
                        continue
                    kx = cnt_b % NQ
                    z = qn[kx]
                    cnt_b += 1
                    t1 = act(z[:, :], bank[bs[q]][:, :], ACT.Copy, t, t_r4, *qnf[kx], scale=r4[:, q:q + 1])
                    bfree[bs[q]] = [t1]
                    t2 = act(qs_[:, :], z[:, :], ACT.Square, t1, *tqs)
                    t3 = V(lambda e, kx=kx: e.tensor_reduce(mn2[:, kx, :], qs_[:, :].rearrange("p (h d) -> p h d", d=64),
                                                            AX.X, ALU.add), t2, *rnf[kx])
                    tqs = [t3]
                    t4 = ts(mn2[:, kx, :], mn2[:, kx, :], 1.0 / 64, ALU.mult, t3, s2=EPS, op1=ALU.add)
                    t5 = G(lambda e, kx=kx: e.tensor_tensor(rn2[:, kx, :], mn2[:, kx, :], cst[:, C_HALF:C_HALF + 8], ALU.pow),
                           t4, t_c)
                    scale_later.append((step, (blk, q, kx, t5)))
                    advance(step)
                pe_done[u] = t
        a_done = t
        tqk_all = [qk2[k] for k in qk2]
        gb_t, gb_free = {}, [[tms] for _ in range(NG)]

        def loadG(h):
            i = h % NG
            w = [t_ev, *gb_free[i]]
            src = EV.ap()

            def toe(r0, rows, cols):
                return bass.AP(EV, (h * P + r0) * 640 + 127 - r0, [[639, rows], [1, cols]])
            pr.dma("sync", Gb[i][0:64, 0:448], toe(0, 64, 448), s_gb[i], 0, w)
            gb_t[h] = [pr.dma("sync", Gb[i][64:128, :], toe(64, 64, 512), s_gb[i], 32 * (h // NG + 1), w)]

        def bias2(h):
            def done(t):
                gb_free[h % NG] = [t]
            return Gb[h % NG], gb_t[h], done

        loaded = set()
        qzf = [[t_qz] for _ in range(4)]

        def fetch2(h, q):
            if q == 0 and h % 2 == 0:
                for x in range(h, min(h + 4, H2)):
                    if x not in loaded and (x < NG or x - NG < h):
                        loaded.add(x)
                        loadG(x)
            i = 2 * (q % 2) + h % 2
            rows = slice(64 * (h % 2), 64 * (h % 2) + 64)
            src = qT2[h // 2][rows, q * P:(q + 1) * P]
            t = G(lambda e: e.tensor_copy(qz[rows, i, :], src), *tqk_all, *qzf[i])
            return qz[:, i, :], kT2[h // 2], tqk_all + [t], lambda t: qzf.__setitem__(i, [t])

        pb2 = qn + [qs_] + [sb("pb2", [P, 512], F, at2)]
        t2f_prev = list(fence)
        out2, t_o = attention(H2, fetch2, v2, t_v2, 0.125, bias2, pb2, [6, 7], lambda p: (p, [a_done]), at2)
        for m in out2:
            o_tok[m] = out2[m]
        fence = [t_o, gb_t[15][0], gb_t[14][0]] + [z for m in out2 for z in out2[m]]
        at2.close()
        main[0], ring[0] = 0, 7
        xk = project_residual("wo", o_tok, PC_FFN + 8)
        stage[0] = 0

        hid = ExitStack()
        ctx.enter_context(hid)
        HH = [sb(f"HI{i}", [P, S], R, hid) for i in range(NH)]
        HL = [sb(f"HM{i}", [P, S], R, hid) for i in range(NH)]
        cvs = [sb(f"cvt{i}", [P, S], F, hid) for i in range(2)]
        t1s = [sb(f"t1t{i}", [P, S + 2], F, hid) for i in range(2)]
        for z in t1s:
            tz1 = G(lambda e, z=z: e.memset(z[:, 0:2], 0.0), *fence)
        t1f = [[tz1], [tz1]]
        cvf = [list(fence), list(fence)]
        hfree = [[] for _ in range(NH)]
        t2f = [list(fence), list(fence)]
        ffn(1, fence)

        assert cur[0] == len(plan)

        block = ctx.enter_context(nc.Block())

        @block.sync
        def _(e):
            pr.play("sync", e)
            e.wait_ge(s_o, 16 * 8)

        @block.tensor
        def _(e):
            pr.play("tensor", e)

        @block.vector
        def _(e):
            pr.play("vector", e)

        @block.scalar
        def _(e):
            pr.play("scalar", e)

        @block.gpsimd
        def _(e):
            pr.play("gpsimd", e)


def constants():
    c = np.zeros((P, NCC), np.float32)
    c[:, C_ID:C_ID + P] = np.eye(P)
    c[:, C_ONE:C_ONE + P] = 1.0
    c[:, C_HALF:C_HALF + P] = -0.5
    c[:, C_SCAN:C_SCAN + S] = (np.arange(S) % 64 != 0)
    c[0, C_MA:C_MA + 64] = -1e30
    c[0, C_MB + 64:C_MB + P] = 1.0
    c[:, C_IF:C_IF + 16] = np.float32(10000.0) ** (-np.arange(0, 32, 2, dtype=np.float32) / np.float32(32))
    for g, w in enumerate(WINDOWS):
        c[:, C_CNT + 16 * g:C_CNT + 16 * g + 16] = 1.0 / np.minimum(np.arange(16) + 1, w)
    s, t = np.meshgrid(np.arange(P), np.arange(P), indexing="ij")
    m = np.zeros((P, 7, P), np.int32)
    m[:, 0, :] = s == t
    for i, b in enumerate(LEVELS):
        m[:, i + 1, :] = (s // (2 * b) == t // (2 * b)) & (s % (2 * b) < b) & (t % (2 * b) >= b)
    return c, m


def kernel(**x):
    import concourse.bacc as bacc
    from concourse.bass_utils import run_bass_kernel_spmd as run

    x = {k: np.asarray(v) for k, v in x.items()}
    f4 = np.float32

    def cols(w, a, b):
        k = w.shape[0] // P
        return w[:, a:b].reshape(k, P, b - a).transpose(1, 0, 2).reshape(P, -1)

    w_in = x["w_in"][0]
    ukv = x["mla_w_ukv"][0].reshape(128, MH, 128)
    units = {
        "small": lambda i: cols(np.concatenate([w_in[:, 1024:1040], np.zeros((D, 16), f4), w_in[:, 1936:1968]], 1),
                                0, 64),
        "cq": lambda i: cols(w_in, 1552, 1808),
        "ckv": lambda i: cols(w_in, 1808, 1936),
        "gq": lambda i: cols(w_in, 0, 256),
        "gk": lambda i: cols(w_in, 256, 512),
        "gv": lambda i: cols(w_in[512 * i:512 * i + 512], 512, 1024),
        "gr": lambda i: cols(w_in, 1040 + 256 * i, 1296 + 256 * i),
        "uq": lambda i: cols(x["mla_w_uq"][0], 0, 768),
        "ukv": lambda i: np.concatenate([ukv[:, :, 0:64].reshape(128, 512), ukv[:, :, 64:].reshape(128, 512)], 1),
        "wout": lambda i: cols(x["w_out"][0], 256 * i, 256 * i + 256),
        "up": lambda i: cols(x["w_mlp_up"][0], 256 * i, 256 * i + 256),
        "down": lambda i: cols(x["w_mlp_down"][0][1024 * (i // 4):1024 * (i // 4) + 1024], 256 * (i % 4), 256 * (i % 4) + 256),
        "proj": lambda i: cols(x["w_ple_proj"][0], 0, 1024),
        "pg": lambda i: cols(x["w_ple_gate"][0], 256 * i, 256 * i + 256),
        "pool": lambda i: cols(x["pool_w_2"][0].reshape(1024, 256), 0, 256),
        "qkv": lambda i: cols(x["attn_wqkv_2"][0][512 * (i % 2):512 * (i % 2) + 512], 512 * (i // 2), 512 * (i // 2) + 512),
        "wo": lambda i: cols(x["attn_wo_2"][0], 256 * i, 256 * i + 256),
    }
    for l in range(2):
        units[f"gate{l}"] = lambda i, l=l: cols(x["ffn_w_gate_2"][l], 256 * i, 256 * i + 256)
        units[f"val{l}"] = lambda i, l=l: cols(x["ffn_w_val_2"][l], 256 * i, 256 * i + 256)
        units[f"fo{l}"] = lambda i, l=l: cols(x["ffn_w_out_2"][l][P * GROUPS2[i // 4][0]:P * GROUPS2[i // 4][1]],
                                              256 * (i % 4), 256 * (i % 4) + 256)
    plan = unit_plan()
    W = np.zeros((len(plan), P, UE), f4)
    for u, (name, i, n) in enumerate(plan):
        W[u, :, 0:n] = units[name](i)
    vecs = [x["attn_norm"], x["mlp_norm"], x["ple_norm"], x["b_ple_gate"], x["mix_norm_2"], x["ffn_norm_2"],
            x["pool_b_2"], x["pool_scale_2"], x["ffn_conv_w_2"], x["ffn_conv_b_2"], x["gla_gate_b"],
            x["gla_out_norm"], x["mla_q_norm"], x["mla_kv_norm"]]
    PV = np.ascontiguousarray(np.concatenate([v.reshape(-1, P) for v in vecs], 0).T)
    ROW = np.concatenate([x["qk_norm_q"][0], x["qk_norm_k"][0], x["attn_q_norm_2"][0], x["attn_k_norm_2"][0]])[None]
    CST, MSK = constants()
    arrays = {
        "W": W,
        "XT": np.ascontiguousarray(x["x"][0].T.reshape(8, P, S).transpose(1, 0, 2)),
        "PT": np.ascontiguousarray(x["p"][0, 0].T.reshape(2, P, S).transpose(1, 0, 2)),
        "PV": PV,
        "ROW": np.ascontiguousarray(ROW),
        "GW2": np.ascontiguousarray(x["gla_gate_w2"][0]),
        "POS": np.ascontiguousarray(x["positions"][0].reshape(4, P).T),
        "REL": np.ascontiguousarray(x["attn_rel_bias_2"][0][:, ::-1]),
        "CST": CST,
        "MSK": MSK,
    }
    nc = bacc.Bacc("TRN2", target_bir_lowering=False, num_devices=1)
    aps = [nc.dram_tensor(f"in_{k}", a.shape, mybir.dt.from_np(a.dtype), kind="ExternalInput").ap() for k, a in arrays.items()]
    out = nc.dram_tensor("out_0", (P, 8, S), F, kind="ExternalOutput").ap()
    build(nc, *aps, out)
    r = run(nc, [{f"in_{k}": a for k, a in arrays.items()}], core_ids=[0])
    o = r.results[0]["out_0"]
    return np.ascontiguousarray(o.transpose(1, 0, 2).reshape(D, S).T)[None]
```
